# Optimizing a Trainium2 kernel written in Bass

```python
import jax, jax.numpy as jnp
from jax import lax
import numpy as np

D_MODEL = 1024
BATCH = 1
SEQ = 512
DEPTH = 2

HEAD_DIM = 64
N_HEADS_A = D_MODEL // HEAD_DIM
WIDTH_A = N_HEADS_A * HEAD_DIM
N_Q_HEADS_B = D_MODEL // HEAD_DIM
N_KV_HEADS_B = 4
GROUP_B = N_Q_HEADS_B // N_KV_HEADS_B
WIDTH_B = N_Q_HEADS_B * HEAD_DIM
KV_WIDTH_B = N_KV_HEADS_B * HEAD_DIM
WINDOW = 128
Q_BLOCK = 128
ROT_DIM = HEAD_DIM // 4
ROPE_THETA = 500000.0
EPS = 1e-6
N_A_LAYERS = DEPTH // 2
N_B_LAYERS = DEPTH - N_A_LAYERS


def rmsnorm(x, g):
    xf = x.astype(jnp.float32)
    y = xf * lax.rsqrt(jnp.mean(xf * xf, axis=-1, keepdims=True) + EPS)
    return (y * g.astype(jnp.float32)).astype(x.dtype)

def partial_rope(x, positions):
    x_rot, x_pass = x[..., :ROT_DIM], x[..., ROT_DIM:]
    half = ROT_DIM // 2
    inv_freq = jnp.power(jnp.float32(ROPE_THETA), -jnp.arange(0, ROT_DIM, 2, dtype=jnp.float32) / ROT_DIM)
    ang = positions.astype(jnp.float32)[:, None] * inv_freq[None, :]
    cos = jnp.cos(ang)[None, :, None, :]
    sin = jnp.sin(ang)[None, :, None, :]
    xr = x_rot.astype(jnp.float32)
    x1, x2 = xr[..., :half], xr[..., half:]
    rot = jnp.concatenate([x1 * cos - x2 * sin, x1 * sin + x2 * cos], axis=-1)
    return jnp.concatenate([rot.astype(x.dtype), x_pass], axis=-1)

def fox_attention(q, k, v, log_f):
    b, s, h, d = q.shape
    nb = s // Q_BLOCK
    scale = HEAD_DIM ** -0.5
    c = jnp.cumsum(log_f, axis=1)
    c_k = jnp.transpose(c, (0, 2, 1))
    q_blocks = jnp.moveaxis(q.reshape(b, nb, Q_BLOCK, h, d), 1, 0)
    c_blocks = jnp.moveaxis(c_k.reshape(b, h, nb, Q_BLOCK), 2, 0)
    k_pos = jnp.arange(s)

    def block(args):
        idx, qi, ci = args
        logits = jnp.einsum('bqhd,bkhd->bhqk', qi, k, preferred_element_type=jnp.float32) * scale
        logits = logits + ci[..., :, None] - c_k[..., None, :]
        q_pos = idx * Q_BLOCK + jnp.arange(Q_BLOCK)
        causal = k_pos[None, :] <= q_pos[:, None]
        logits = jnp.where(causal, logits, -jnp.inf)
        p = jax.nn.softmax(logits, axis=-1)
        return jnp.einsum('bhqk,bkhd->bqhd', p.astype(v.dtype), v)

    out = lax.map(block, (jnp.arange(nb), q_blocks, c_blocks))
    return jnp.moveaxis(out, 0, 1).reshape(b, s, h, d)

def swa_sink_attention(q, k, v, sinks):
    b, s, hq, d = q.shape
    hkv = k.shape[2]
    g = hq // hkv
    nb = s // WINDOW
    scale = HEAD_DIM ** -0.5
    qb = q.reshape(b, nb, WINDOW, hkv, g, d)
    pad = ((0, 0), (WINDOW, 0), (0, 0), (0, 0))
    kb = jnp.pad(k, pad).reshape(b, nb + 1, WINDOW, hkv, d)
    vb = jnp.pad(v, pad).reshape(b, nb + 1, WINDOW, hkv, d)
    k_band = jnp.concatenate([kb[:, :-1], kb[:, 1:]], axis=2)
    v_band = jnp.concatenate([vb[:, :-1], vb[:, 1:]], axis=2)
    logits = jnp.einsum('bnqhgd,bnkhd->bnhgqk', qb, k_band, preferred_element_type=jnp.float32) * scale
    diff = (jnp.arange(WINDOW)[:, None] + WINDOW) - jnp.arange(2 * WINDOW)[None, :]
    in_window = (diff >= 0) & (diff < WINDOW)
    k_abs = jnp.arange(nb)[:, None] * WINDOW + jnp.arange(2 * WINDOW)[None, :] - WINDOW
    valid = in_window[None] & (k_abs >= 0)[:, None, :]
    logits = jnp.where(valid[None, :, None, None], logits, -jnp.inf)
    sink = jnp.broadcast_to(sinks.astype(jnp.float32).reshape(1, 1, hkv, g, 1, 1), logits.shape[:-1] + (1,))
    probs = jax.nn.softmax(jnp.concatenate([logits, sink], axis=-1), axis=-1)[..., :-1]
    out = jnp.einsum('bnhgqk,bnkhd->bnqhgd', probs.astype(v.dtype), v_band)
    return out.reshape(b, s, hq, d)

def first_inputs(seed: int = 0) -> dict:
    key = jax.random.key(seed)
    ks = jax.random.split(key, 20)
    f32 = jnp.float32
    in_a = 3 * WIDTH_A + N_HEADS_A + WIDTH_A
    in_b = WIDTH_B + WIDTH_B
    return {
        "x": jax.random.normal(ks[0], (BATCH, SEQ, D_MODEL), f32),
        "positions": jnp.arange(SEQ, dtype=jnp.int32),
        "norm_a_g": 1.0 + 0.02 * jax.random.normal(ks[1], (N_A_LAYERS, D_MODEL), f32),
        "w_in_a": jax.random.normal(ks[2], (N_A_LAYERS, D_MODEL, in_a), f32) * D_MODEL ** -0.5,
        "b_forget": 3.0 + 0.1 * jax.random.normal(ks[3], (N_A_LAYERS, N_HEADS_A), f32),
        "qnorm_a_g": 1.0 + 0.02 * jax.random.normal(ks[4], (N_A_LAYERS, HEAD_DIM), f32),
        "knorm_a_g": 1.0 + 0.02 * jax.random.normal(ks[5], (N_A_LAYERS, HEAD_DIM), f32),
        "w_out_a": jax.random.normal(ks[6], (N_A_LAYERS, WIDTH_A, D_MODEL), f32) * WIDTH_A ** -0.5,
        "kv_norm_g": 1.0 + 0.02 * jax.random.normal(ks[7], (D_MODEL,), f32),
        "w_kv": jax.random.normal(ks[8], (D_MODEL, 2 * KV_WIDTH_B), f32) * D_MODEL ** -0.5,
        "knorm_b_g": 1.0 + 0.02 * jax.random.normal(ks[9], (HEAD_DIM,), f32),
        "norm_b_g": 1.0 + 0.02 * jax.random.normal(ks[10], (N_B_LAYERS, D_MODEL), f32),
        "w_in_b": jax.random.normal(ks[11], (N_B_LAYERS, D_MODEL, in_b), f32) * D_MODEL ** -0.5,
        "qnorm_b_g": 1.0 + 0.02 * jax.random.normal(ks[12], (N_B_LAYERS, HEAD_DIM), f32),
        "sinks": 0.5 * jax.random.normal(ks[13], (N_B_LAYERS, N_Q_HEADS_B), f32),
        "w_out_b": jax.random.normal(ks[14], (N_B_LAYERS, WIDTH_B, D_MODEL), f32) * WIDTH_B ** -0.5,
    }

def first_block(x, positions, norm_a_g, w_in_a, b_forget, qnorm_a_g, knorm_a_g, w_out_a,
              kv_norm_g, w_kv, knorm_b_g, norm_b_g, w_in_b, qnorm_b_g, sinks, w_out_b):
    b, s, _ = x.shape
    h = x
    k_shared = None
    v_shared = None
    for layer in range(DEPTH):
        if layer < N_A_LAYERS:
            i = layer
            u = rmsnorm(h, norm_a_g[i])
            proj = u @ w_in_a[i]
            q, k, v, f_logit, gate = jnp.split(
                proj, [WIDTH_A, 2 * WIDTH_A, 3 * WIDTH_A, 3 * WIDTH_A + N_HEADS_A], axis=-1)
            q = rmsnorm(q.reshape(b, s, N_HEADS_A, HEAD_DIM), qnorm_a_g[i])
            k = rmsnorm(k.reshape(b, s, N_HEADS_A, HEAD_DIM), knorm_a_g[i])
            v = v.reshape(b, s, N_HEADS_A, HEAD_DIM)
            log_f = jax.nn.log_sigmoid((f_logit + b_forget[i]).astype(jnp.float32))
            o = fox_attention(q, k, v, log_f).reshape(b, s, WIDTH_A)
            h = h + (o * jax.nn.silu(gate)) @ w_out_a[i]
        else:
            if layer == N_A_LAYERS:
                u_kv = rmsnorm(h, kv_norm_g)
                k_s, v_s = jnp.split(u_kv @ w_kv, [KV_WIDTH_B], axis=-1)
                k_shared = partial_rope(rmsnorm(k_s.reshape(b, s, N_KV_HEADS_B, HEAD_DIM), knorm_b_g), positions)
                v_shared = v_s.reshape(b, s, N_KV_HEADS_B, HEAD_DIM)
            j = layer - N_A_LAYERS
            u = rmsnorm(h, norm_b_g[j])
            q, gate = jnp.split(u @ w_in_b[j], [WIDTH_B], axis=-1)
            q = partial_rope(rmsnorm(q.reshape(b, s, N_Q_HEADS_B, HEAD_DIM), qnorm_b_g[j]), positions)
            o = swa_sink_attention(q, k_shared, v_shared, sinks[j]).reshape(b, s, WIDTH_B)
            h = h + (o * jax.nn.silu(gate)) @ w_out_b[j]
    return h


DEPTH_2 = 1

D_MIX = D_MODEL
HG_HEADS = 4
HG_DK = 128
HG_DV = 128
HG_WIDTH = HG_HEADS * HG_DV
HG_CHUNK = 64
SA_HEADS = 4
SA_HEAD_DIM = 64
SA_WIDTH = SA_HEADS * SA_HEAD_DIM
IDX_HEADS = 8
IDX_DIM = 32
IDX_TOPK_MAX = 256
IDX_TOPK_DIV = 4
CV_WIDTH = D_MIX - HG_WIDTH - SA_WIDTH
CV_WIDTH_FILTER = 31
D_FF = 4 * D_MODEL
N_MOD = 6
NEG_BIG = -1e30
TINY = 1e-30

IN_SIZES = (
    HG_HEADS * HG_DK,
    HG_HEADS * HG_DK,
    HG_WIDTH,
    HG_WIDTH,
    SA_WIDTH,
    SA_WIDTH,
    SA_WIDTH,
    IDX_HEADS * IDX_DIM,
    IDX_DIM,
    IDX_HEADS,
    2 * CV_WIDTH,
)
D_IN = sum(IN_SIZES)


def rmsnorm_2(x, w):
    xf = x.astype(jnp.float32)
    y = xf * lax.rsqrt(jnp.mean(xf * xf, axis=-1, keepdims=True) + EPS)
    return (y * w.astype(jnp.float32)).astype(x.dtype)

def hgrn2_lower_bounds(lb_logits):
    p = jax.nn.softmax(lb_logits.astype(jnp.float32), axis=0)
    return jnp.cumsum(p, axis=0) - p[0]

def hgrn2_mixer(q_raw, f_raw, i_in, g_raw, lb, onorm_w):
    f32 = jnp.float32
    dt = q_raw.dtype
    bsz, L, _ = q_raw.shape
    lb = lb.astype(f32)
    fr = f_raw.astype(f32)
    q = jax.nn.silu(q_raw.astype(f32)) * (HG_DK ** -0.5)
    f = lb + (1.0 - lb) * jax.nn.sigmoid(fr)
    log_f = jnp.log(jnp.maximum(f, TINY))
    k = (1.0 - lb) * jax.nn.sigmoid(-fr)
    v = i_in.astype(f32)
    n_chunks = L // HG_CHUNK

    def to_chunks(t, d):
        return t.reshape(bsz, n_chunks, HG_CHUNK, HG_HEADS, d).transpose(1, 0, 3, 2, 4)

    causal = jnp.tril(jnp.ones((HG_CHUNK, HG_CHUNK), dtype=bool))

    def step(S, xs):
        qc, kc, gc, vc = xs
        G = jnp.cumsum(gc, axis=-2)
        o_inter = jnp.einsum('bhik,bhkv->bhiv', qc * jnp.exp(G), S)
        diff = G[:, :, :, None, :] - G[:, :, None, :, :]
        decay = jnp.exp(jnp.where(causal[:, :, None], diff, NEG_BIG))
        A = jnp.einsum('bhik,bhijk,bhjk->bhij', qc, decay, kc)
        o_intra = jnp.einsum('bhij,bhjv->bhiv', A, vc)
        G_last = G[:, :, -1:, :]
        S_new = jnp.exp(G_last[:, :, 0, :])[..., None] * S + jnp.einsum(
            'bhjk,bhjv->bhkv', kc * jnp.exp(G_last - G), vc)
        return S_new, o_inter + o_intra

    S0 = jnp.zeros((bsz, HG_HEADS, HG_DK, HG_DV), f32)
    _, o = lax.scan(step, S0, (to_chunks(q, HG_DK), to_chunks(k, HG_DK),
                               to_chunks(log_f, HG_DK), to_chunks(v, HG_DV)))
    o = o.transpose(1, 0, 3, 2, 4).reshape(bsz, L, HG_HEADS, HG_DV)
    o = o * lax.rsqrt(jnp.mean(o * o, axis=-1, keepdims=True) + EPS)
    o = o * onorm_w.astype(f32).reshape(HG_HEADS, HG_DV)
    o = o.reshape(bsz, L, HG_WIDTH) * jax.nn.silu(g_raw.astype(f32))
    return o.astype(dt)

def dsa_mixer(q, k, v, q_idx, k_idx, w_idx):
    f32 = jnp.float32
    dt = q.dtype
    bsz, L, _ = q.shape
    topk = min(IDX_TOPK_MAX, L // IDX_TOPK_DIV)
    n_blk = L // Q_BLOCK
    q = q.reshape(bsz, L, SA_HEADS, SA_HEAD_DIM)
    k = k.reshape(bsz, L, SA_HEADS, SA_HEAD_DIM)
    v = v.reshape(bsz, L, SA_HEADS, SA_HEAD_DIM)
    q_idx = q_idx.reshape(bsz, L, IDX_HEADS, IDX_DIM)
    w_idx = w_idx.astype(f32) * (IDX_HEADS ** -0.5)
    k_idx_f = k_idx.astype(f32)
    key_pos = jnp.arange(L, dtype=jnp.int32)

    def blocks(t):
        return t.reshape(bsz, n_blk, Q_BLOCK, *t.shape[2:]).swapaxes(0, 1)

    def one_block(xs):
        qb, qib, wb, t0 = xs
        qpos = t0 + jnp.arange(Q_BLOCK, dtype=jnp.int32)
        s = jnp.einsum('bqhd,bsd->bqhs', qib.astype(f32), k_idx_f) * (IDX_DIM ** -0.5)
        score = jnp.einsum('bqh,bqhs->bqs', wb, jax.nn.relu(s))
        admissible = key_pos[None, :] <= qpos[:, None]
        score = jnp.where(admissible[None], score, NEG_BIG)
        _, sel = lax.top_k(score, topk)
        valid = sel <= qpos[None, :, None]
        kg = jax.vmap(lambda kk, ii: kk[ii])(k, sel)
        vg = jax.vmap(lambda vv, ii: vv[ii])(v, sel)
        logits = jnp.einsum('bqhd,bqkhd->bqhk', qb.astype(f32), kg.astype(f32)) * (SA_HEAD_DIM ** -0.5)
        logits = jnp.where(valid[:, :, None, :], logits, NEG_BIG)
        p = jax.nn.softmax(logits, axis=-1)
        o = jnp.einsum('bqhk,bqkhd->bqhd', p, vg.astype(f32))
        return o.reshape(bsz, Q_BLOCK, SA_WIDTH).astype(dt)

    t0s = jnp.arange(n_blk, dtype=jnp.int32) * Q_BLOCK
    out = lax.map(one_block, (blocks(q), blocks(q_idx), blocks(w_idx), t0s))
    return out.swapaxes(0, 1).reshape(bsz, L, SA_WIDTH)

def conv_module(u, cv_w, cv_b, ln_w, ln_b):
    f32 = jnp.float32
    dt = u.dtype
    a, b = jnp.split(u, 2, axis=-1)
    h = a * jax.nn.sigmoid(b)
    h = lax.conv_general_dilated(
        h, cv_w[:, None, :], window_strides=(1,),
        padding=[(CV_WIDTH_FILTER - 1, 0)],
        dimension_numbers=('NWC', 'WIO', 'NWC'),
        feature_group_count=CV_WIDTH) + cv_b
    hf = h.astype(f32)
    mu = jnp.mean(hf, axis=-1, keepdims=True)
    var = jnp.mean(jnp.square(hf - mu), axis=-1, keepdims=True)
    hf = (hf - mu) * lax.rsqrt(var + EPS) * ln_w.astype(f32) + ln_b.astype(f32)
    return jax.nn.silu(hf).astype(dt)

def second_inputs(seed: int = 0) -> dict:
    key = jax.random.key(seed)
    ks = jax.random.split(key, 17)
    f32 = jnp.float32
    n = lambda k, shape, s: jax.random.normal(k, shape, f32) * s
    return {
        "x": n(ks[0], (BATCH, SEQ, D_MODEL), 1.0),
        "c": n(ks[1], (BATCH, D_MODEL), 1.0),
        "ada_w": n(ks[2], (DEPTH_2, D_MODEL, N_MOD * D_MODEL), 0.5 * D_MODEL ** -0.5),
        "ada_b": n(ks[3], (DEPTH_2, N_MOD * D_MODEL), 0.02),
        "norm_mix_w": 1.0 + n(ks[4], (DEPTH_2, D_MODEL), 0.05),
        "norm_mlp_w": 1.0 + n(ks[5], (DEPTH_2, D_MODEL), 0.05),
        "w_in": n(ks[6], (DEPTH_2, D_MODEL, D_IN), D_MODEL ** -0.5),
        "hg_lb_logits": n(ks[7], (DEPTH_2, HG_HEADS * HG_DK), 1.0),
        "hg_onorm_w": 1.0 + n(ks[8], (DEPTH_2, HG_WIDTH), 0.05),
        "cv_w": n(ks[9], (DEPTH_2, CV_WIDTH_FILTER, CV_WIDTH), CV_WIDTH_FILTER ** -0.5),
        "cv_b": n(ks[10], (DEPTH_2, CV_WIDTH), 0.02),
        "cv_ln_w": 1.0 + n(ks[11], (DEPTH_2, CV_WIDTH), 0.05),
        "cv_ln_b": n(ks[12], (DEPTH_2, CV_WIDTH), 0.02),
        "w_out": n(ks[13], (DEPTH_2, D_MIX, D_MODEL), D_MIX ** -0.5),
        "mlp_w1": n(ks[14], (DEPTH_2, D_MODEL, D_FF), D_MODEL ** -0.5),
        "mlp_w2": n(ks[15], (DEPTH_2, D_FF, D_MODEL), D_FF ** -0.5),
        "final_norm_w": 1.0 + n(ks[16], (D_MODEL,), 0.05),
    }

def second_block(x, c, ada_w, ada_b, norm_mix_w, norm_mlp_w, w_in, hg_lb_logits, hg_onorm_w,
              cv_w, cv_b, cv_ln_w, cv_ln_b, w_out, mlp_w1, mlp_w2, final_norm_w):
    offsets = np.cumsum(IN_SIZES)[:-1].tolist()
    lower_bounds = hgrn2_lower_bounds(hg_lb_logits)
    c_act = jax.nn.silu(c)
    for l in range(DEPTH_2):
        mod = c_act @ ada_w[l] + ada_b[l]
        sh1, sc1, g1, sh2, sc2, g2 = [m[:, None, :] for m in jnp.split(mod, N_MOD, axis=-1)]

        h = rmsnorm_2(x, norm_mix_w[l]) * (1.0 + sc1) + sh1
        proj = h @ w_in[l]
        (hq, hf, hi, hg, sq, sk, sv, iq, ik, iw, cu) = jnp.split(proj, offsets, axis=-1)
        o_a = hgrn2_mixer(hq, hf, hi, hg, lower_bounds[l], hg_onorm_w[l])
        o_b = dsa_mixer(sq, sk, sv, iq, ik, iw)
        o_c = conv_module(cu, cv_w[l], cv_b[l], cv_ln_w[l], cv_ln_b[l])
        mix = jnp.concatenate([o_a, o_b, o_c], axis=-1) @ w_out[l]
        x = x + g1 * mix

        h = rmsnorm_2(x, norm_mlp_w[l]) * (1.0 + sc2) + sh2
        ff = jnp.square(jax.nn.relu(h @ mlp_w1[l])) @ mlp_w2[l]
        x = x + g2 * ff
    return rmsnorm_2(x, final_norm_w)


def setup_inputs(seed=0):
    out = dict(first_inputs(seed))
    for name, value in second_inputs(seed + 1).items():
        if name != "x":
            out[name + "_2"] = value
    return out


def reference(
    x, positions, norm_a_g, w_in_a, b_forget, qnorm_a_g, knorm_a_g, w_out_a, kv_norm_g, w_kv,
    knorm_b_g, norm_b_g, w_in_b, qnorm_b_g, sinks, w_out_b, c_2, ada_w_2, ada_b_2, norm_mix_w_2,
    norm_mlp_w_2, w_in_2, hg_lb_logits_2, hg_onorm_w_2, cv_w_2, cv_b_2, cv_ln_w_2, cv_ln_b_2,
    w_out_2, mlp_w1_2, mlp_w2_2, final_norm_w_2,
):
    x = first_block(
        x, positions, norm_a_g, w_in_a, b_forget, qnorm_a_g, knorm_a_g, w_out_a, kv_norm_g,
        w_kv, knorm_b_g, norm_b_g, w_in_b, qnorm_b_g, sinks, w_out_b,
    )
    return second_block(
        x, c_2, ada_w_2, ada_b_2, norm_mix_w_2, norm_mlp_w_2, w_in_2, hg_lb_logits_2,
        hg_onorm_w_2, cv_w_2, cv_b_2, cv_ln_w_2, cv_ln_b_2, w_out_2, mlp_w1_2, mlp_w2_2,
        final_norm_w_2,
    )


_drawn_inputs = setup_inputs


def setup_inputs(seed=0):
    import zlib

    import numpy as np

    out = dict(_drawn_inputs(seed))
    spreads = {}
    factors = {'norm_a_g': 7.429,
     'b_forget': 4.405,
     'qnorm_a_g': 8.0,
     'knorm_a_g': 8.0,
     'kv_norm_g': 8.0,
     'knorm_b_g': 8.0,
     'norm_b_g': 8.0,
     'qnorm_b_g': 8.0,
     'sinks': 64.0,
     'norm_mix_w_2': 31.368,
     'hg_onorm_w_2': 64.0,
     'cv_b_2': 200.0,
     'cv_ln_w_2': 200.0,
     'cv_ln_b_2': 200.0,
     'ada_b_2': 7.212,
     'norm_mlp_w_2': 8.0,
     'cv_w_2': 12.502,
     'mlp_w1_2': 7.846,
     'mlp_w2_2': 7.245}
    for name, (base, spread) in spreads.items():
        noise = np.random.default_rng([zlib.crc32(name.encode()), seed]).standard_normal(out[name].shape)
        drawn = base * np.exp(spread * noise) if base else spread * noise
        out[name] = __import__('jax').numpy.asarray(drawn.astype(out[name].dtype))
    for name, factor in factors.items():
        out[name] = (out[name] * factor).astype(out[name].dtype)
    return out
```

```python
import math

import numpy as np

import concourse.bass as bass
from concourse import mybir
from contextlib import ExitStack

D = 1024
SEQ = 512
P = 128
KT = D // P
NQ = SEQ // P
DH = 64
WIDTH_A = 1024
EPS = 1e-6
SLOTS = 4
AHEAD = 3
NEG = -1e30
HUGE = 3e38

VEC_ROWS = [("ada_b_2", 48), ("norm_a_g", 8), ("kv_norm_g", 8), ("norm_b_g", 8), ("norm_mix_w_2", 8),
            ("norm_mlp_w_2", 8), ("final_norm_w_2", 8), ("c_2", 8), ("hg_onorm_w_2", 4), ("cv_b_2", 2),
            ("cv_ln_w_2", 2), ("cv_ln_b_2", 2)]
VEC = {}
_at = 0
for _name, _rows in VEC_ROWS:
    VEC[_name] = _at
    _at += _rows
N_VEC = _at


ROPE = [np.float32(500000.0) ** np.float32(-2.0 * r / 16) for r in range(8)]
TWO_PI = 2 * math.pi
_second = math.floor((TWO_PI - 6.28125) * 2 ** 20) / 2 ** 20
TURN_PARTS = [6.28125, _second, TWO_PI - 6.28125 - _second]
PI_DOWN = 3.1415925


TOPK = 128
SA_SCALE, IDX_SCALE = 64 ** -0.5, 32 ** -0.5
LN_TINY = math.log(1e-30)
I_COLUMNS = [2816, 2944, 3072, 2048, 2176, 2304, 2432, 2560, 2688, 3112, 3240, 3368, 3496]


class Unit:

    def __init__(self, base, j=0, i=0, per=0):
        self.n = i * per + (base + j)
        self.slot = (base + j) % SLOTS
        self.of_slot = i * (per // SLOTS) + (base + j) // SLOTS
        self.of_pair = i * (per // 2) + (base + j) // 2
        self.bank = (base + j) % 2
        self.of_bank = i * (per // 2) + (base + j) // 2


def wait(eng, sem, value):
    if not isinstance(value, int) or value > 0:
        eng.wait_ge(sem, value)


AFTER = {f"c_{x}": (f"a_{x}", 64) for x in ("scores", "logits", "exps", "pT", "pT_out", "probs")}
AFTER.update({f"c_{x}": (f"a_{x}", last) for x, last in (("o", 16), ("gated", 8), ("gated_hi", 8), ("gated_lo", 8))})
AFTER.update({f"h_{x}": (f"b_{x}", 8) for x in ("silu", "softplus", "logsig", "sigmoid", "gated", "gated_hi", "gated_lo",
                                                "raw0", "q")})
AFTER.update({f"hq_{x}": (f"a_{x}", 8) for x in ("softplus", "logsig", "sigmoid")})
AFTER.update({f"cv_{x}": (f"cg_{x}", 2) for x in ("softplus", "logsig", "sigmoid")})
AFTER.update({"h_raw1": ("a_raw1", 8), "h_raw2": ("a_vraw", 8), "h_raw3": ("b_zraw", 8), "h_vturn": ("a_vturn", 8),
              "h_v": ("a_v", 8), "h_root": ("b_root0", 8), "h_sq": ("b_sq0", 8), "h_sum": ("b_sum0", 8),
              "h_products": ("b_scores", 16), "h_aT": ("b_exps", 64), "h_x": ("b_probs", 64), "h_diff": ("b_pT", 32),
              "h_exp": ("b_pT_out", 32), "h_o": ("b_o", 16), "h_k": ("b_normed", 8), "h_state": ("b_negmax", 16),
              "h_meansq": ("b_sum0_taken", 8), "h_g": ("b_turned", 8), "h_klog": ("b_turn_taken", 8)})
for _n, _key in enumerate(("a", "kv", "mix", "mlp", "f")):
    AFTER.update({f"{x}_{_key}": (f"norm_{x}", per * _n) for x, per in (("sq", 8), ("sums", 8), ("meansq", 1), ("root", 1))})
for _n, _key in enumerate(("a", "kv", "b", "mix", "mlp", "f")):
    AFTER.update({f"{x}_{_key}": (f"norm_{x}", 8 * _n) for x in ("h32", "hhi", "lo")})


class Link:

    def __init__(self, eng, sem):
        self.eng, self.sem, self.base, self.here, self.i, self.per = eng, sem, 0, 0, 0, 0

    def __call__(self, *instructions):
        for ins in instructions:
            ins.then_inc(self.sem, 1)
            self.here += 1
        self.eng.wait_ge(self.sem, self.i * self.per + (self.base + self.here))


def repeated(eng, turns, body, link=None, first=0):
    start = link.here if link else 0
    body(first)
    if turns - first > 1:
        if link:
            per = link.here - start
            link.base += link.here - per
            link.here = 0
            link.per = per
            link.base -= per * first
            link.base += 0
            with eng.Fori(first + 1, turns) as i:
                link.i = i
                body(i)
                assert link.here == per or per == 0, (link.here, per)
            link.base += per * (turns - 1) + per
            link.here = 0
            link.i = link.per = 0
        else:
            with eng.Fori(first + 1, turns) as i:
                body(i)


def build(nc, a, out):
    f32, f32r, bf16, i32 = mybir.dt.float32, mybir.dt.float32r, mybir.dt.bfloat16, mybir.dt.int32
    ALU, ACT, AX = mybir.AluOpType, mybir.ActivationFunctionType, mybir.AxisListType
    ctx = ExitStack()
    with ctx:
        def sb(name, shape, dt=f32):
            return ctx.enter_context(nc.sbuf_tensor(name, shape, dt))

        sems = {}

        def sem(name):
            counter, base = AFTER.get(name, (name, 0))
            if counter not in sems:
                sems[counter] = ctx.enter_context(nc.semaphore(counter))
            return sems[counter]

        def since(name):
            return AFTER.get(name, (name, 0))[1]

        def mark(name, count):
            return sem(name), count + since(name)

        xT = sb("xT", [P, KT, SEQ])
        hi1, lo1 = sb("hi1", [P, KT, SEQ], f32r), sb("lo1", [P, KT, SEQ], f32r)
        hi2, lo2 = sb("hi2", [P, KT, SEQ], f32r), sb("lo2", [P, KT, SEQ], f32r)
        w32 = sb("w32", [P, 2, KT, P])
        wH, wL = sb("wH", [P, SLOTS, KT, P], f32r), sb("wL", [P, SLOTS, KT, P], f32r)
        adaw = sb("adaw", [P, 2, KT, P])
        ident = sb("ident", [P, P])
        identb = sb("identb", [P, P], bf16)
        band = sb("band", [P, 2, P], bf16)
        causal = band[:, 1, :]
        ones = sb("ones", [P, P])
        pair1 = sb("pair1", [P, P])
        turnm = sb("turnm", [P, P])
        epsc = sb("epsc", [P, 1])
        vecs = sb("vecs", [N_VEC, P])
        vecT = sb("vecT", [P, N_VEC])
        gains = sb("gains", [P, 4])
        bfg = sb("bfg", [16, 1])
        sinkb = sb("sinkb", [P, 16])
        cs = sb("cs", [P, 2, SEQ])
        cosb, sinb = cs[:, 0, :], cs[:, 1, :]
        scr = sb("scr", [P, 4096])
        xin = scr[:, :].rearrange("p (q d) -> p q d", q=NQ)
        logits = scr[:, 0:1280]
        probs = scr[:, 1280:2560]
        probsT = scr[:, 2560:3840]
        sq = sb("sq", [P, 2, SEQ])
        rms = sb("rms", [P, 2, SEQ])
        rinv = sb("rinv", [P, 2, SEQ])
        tmp = sb("tmp", [P, 2, SEQ])
        qraw, kraw, vraw = sb("qraw", [P, SEQ]), sb("kraw", [P, SEQ]), sb("vraw", [P, SEQ])
        zraw, th = sb("zraw", [P, SEQ]), sb("th", [P, SEQ])
        qn, kn = sb("qn", [P, SEQ]), sb("kn", [P, SEQ])
        vp = sb("vp", [P, NQ, P])
        sg = sb("sg", [P, SEQ])
        og = sb("og", [P, SEQ])
        cbias = sb("cbias", [P, 2, SEQ])
        stat = sb("stat", [P, 2, 8, 4])
        kd = sb("kd", [P, 4, SEQ])
        fz = kd[0:16, :, :]
        vb = sb("vb", [P, 4, NQ, DH])
        kg, vg = kn, vp[:, :, 0:DH]
        c_dram = nc.dram_tensor("c_dram", [16, SEQ], f32).ap()
        row = sb("row", [1, P])
        modT = sb("modT", [P, 48])
        gainm = sb("gainm", [P, 16])
        cact, cth = sb("cact", [P, KT]), sb("cth", [P, KT])
        taps = sb("taps", [62, P])
        tapT = sb("tapT", [P, 62])
        iqT = cs
        ik4 = qraw
        iwp = sb("iwp", [P, NQ, 8])
        best = sb("best", [P, 2, 8])
        flat = adaw[:, :, :, :].rearrange("p a k n -> p (a k n)")
        sel = flat[:, 0:1280]
        restart = flat[:, 1280:1792]
        sqT, skT, svT = cbias, kd[:, 0:2, :], kd[:, 2:4, :]
        svp = vb[:, :, :, :].rearrange("p a b c -> p (a b c)").rearrange("p (q d) -> p q d", q=NQ)
        ca, cb, cth2 = [rms[:, 1, :], rinv[:, 1, :]], tmp, sq
        PAD = 30
        cpad = scr[:, 0:2 * (PAD + SEQ)].rearrange("p (c s) -> p c s", c=2)
        cacc = scr[:, 1152:1152 + 2 * SEQ].rearrange("p (c s) -> p c s", c=2)
        gc, gf = cbias[:, 0, :], cbias[:, 1, :]
        dd, xx = kd[:, 0:2, :], kd[:, 2:4, :]
        qe, ke = cs[:, 0, :], cs[:, 1, :]
        keT = scr[:, 0:384].rearrange("p (c k) -> p c k", c=3)
        aT = scr[:, 512:1024].rearrange("p (c k) -> p c k", c=4)
        state = scr[:, 1024:1408].rearrange("p (c k) -> p c k", c=3)
        fth = og
        dec = sb("dec", [P, 4])
        jx = flat[:, 1792:1920]
        jj, ii, it = jx.bitcast(i32), flat[:, 1920:2048].bitcast(i32), flat[:, 1920:2048]
        level = sb("level", [P, 7, P], mybir.dt.uint8)
        invf = sb("invf", [P, 1])
        posi = vb[:, 0:2, :, :].rearrange("p a b c -> p (a b c)").bitcast(i32)
        tmp2 = scr[:, 0:2 * SEQ].rearrange("p (a s) -> p a s", a=2)

        G = [ctx.enter_context(nc.psum_tensor(f"G{n}", [P, SEQ], f32)) for n in range(2)]
        S = [ctx.enter_context(nc.psum_tensor(f"S{n}", [P, SEQ], f32)) for n in range(2)]
        T = [ctx.enter_context(nc.psum_tensor(f"T{n}", [P, SEQ], f32)) for n in range(2)]
        O = ctx.enter_context(nc.psum_tensor("O", [P, SEQ], f32))
        N = ctx.enter_context(nc.psum_tensor("N", [P, SEQ], f32))

        w_here = [sem(f"w_here{n}") for n in range(2)]
        w_hi, w_lo, gemm_done = sem("w_hi"), sem("w_lo"), sem("gemm_done")

        UA, UOA, UKV, UB, UOB, UI, UH, UOM, UM = 1, 33, 41, 45, 61, 69, 82, 98, 106
        NU = UM + 4 * 16

        def cols(w, c):
            return w[0, :, bass.ds(c, P)].rearrange("(k p) n -> p k n", p=P)

        block = ctx.enter_context(nc.Block())

        A_AT = [0, P, 3 * P, 6 * P]
        AT_AT = [0, 512, 896, 1152]
        B_AT = [0, P, 3 * P, 5 * P]
        B_W = [P, 2 * P, 2 * P, 2 * P]

        @block.sync
        def _(sp):
            sp.dma_start(xin, a["x"][0].rearrange("(q p) d -> p q d", p=P)).then_inc(sem("x_here"), 16)
            for name, rows in VEC_ROWS:
                t = a[name]
                flat = t.rearrange("(r p) -> r p", p=P) if len(t.shape) == 1 else t.rearrange("a (r p) -> (a r) p", p=P)
                sp.dma_start(vecs[VEC[name]:VEC[name] + rows, :], flat).then_inc(sem("vec_here"), 16)
            for n, name in enumerate(["qnorm_a_g", "knorm_a_g", "qnorm_b_g", "knorm_b_g"]):
                t = a[name]
                col = t.rearrange("(p o) -> p o", o=1) if len(t.shape) == 1 else t.rearrange("o p -> p o")
                for half in range(2):
                    sp.dma_start(gains[half * DH:(half + 1) * DH, n:n + 1], col).then_inc(sem("vec_here"), 16)
            sp.dma_start(bfg[:, :], a["b_forget"].rearrange("o p -> p o")).then_inc(sem("vec_here"), 16)
            sp.dma_start(taps[:, :], a["cv_w_2"].rearrange("o t (c p) -> (o t c) p", p=P)).then_inc(sem("vec_here"), 16)
            sp.dma_start(sinkb[:, :], a["sinks"][0:1, :].partition_broadcast(P)).then_inc(sem("vec_here"), 16)
            sp.dma_start(posi[:, :], a["positions"].rearrange("(a s) -> a s", a=1).partition_broadcast(P)
                         ).then_inc(sem("pos_here"), 16)

            def load_unit(u, src):
                wait(sp, w_lo, u.n - 1)
                sp.dma_start(w32[:, u.slot % 2], src).then_inc(w_here[u.slot % 2], 16)

            def load_ada(e, slot):
                wait(sp, sem("ada_done"), e - 1)
                sp.dma_start(adaw[:, slot], cols(a["ada_w_2"], e * P)).then_inc(sem(f"ada_here{slot}"), 16)

            def ada_two(e):
                load_ada(e, 0)
                load_ada(e + 1, 1)

            wa, wb = a["w_in_a"], a["w_in_b"]
            load_unit(Unit(0), cols(wa, 3 * WIDTH_A))

            def pair_a(t):
                for j, c in enumerate([0, WIDTH_A, 2 * WIDTH_A, 3 * WIDTH_A + 16]):
                    load_unit(Unit(UA, j, t, 4), cols(wa, t * P + c))
                    if j in (0, 3) and not (isinstance(t, int) and t == 0):
                        ada_two(4 * t - (4 if j == 0 else 2))
            pair_a(0)
            repeated(sp, 8, pair_a, first=1)
            for n in range(8):
                load_unit(Unit(UOA, n), cols(a["w_out_a"], n * P))
                if n in (0, 3):
                    ada_two(28 if n == 0 else 30)
            wkv = a["w_kv"].rearrange("(o k) n -> o k n", o=1)
            for n in range(4):
                load_unit(Unit(UKV, n), cols(wkv, n * P))

            def group_b(g):
                for p in range(2):
                    for j, c in enumerate([0, D]):
                        load_unit(Unit(UB, 2 * p + j, g, 4), cols(wb, g * (2 * P) + (p * P + c)))
                        if j == 0 and not (isinstance(g, int) and g == 0):
                            ada_two(g * 4 + (28 + 2 * p))
            group_b(0)
            repeated(sp, 4, group_b, first=1)
            for n in range(8):
                load_unit(Unit(UOB, n), cols(a["w_out_b"], n * P))
                if n in (0, 2):
                    ada_two(44 + n)
            wi = a["w_in_2"]
            for n, c in enumerate(I_COLUMNS):
                load_unit(Unit(UI, n), cols(wi, c))

            def head(t):
                for j in range(4):
                    load_unit(Unit(UH, j, t, 4), cols(wi, t * P + 512 * j))
            repeated(sp, 4, head)
            for n in range(8):
                load_unit(Unit(UOM, n), cols(a["w_out_2"], n * P))
            def quarter(c):
                for n in range(8):
                    load_unit(Unit(UM, n, c, 16), cols(a["mlp_w1_2"], c * D + n * P))
                for n in range(8):
                    load_unit(Unit(UM, 8 + n, c, 16), a["mlp_w2_2"][0, bass.ds(c * D, D), n * P:(n + 1) * P]
                              .rearrange("(k p) n -> p k n", p=P))
            repeated(sp, 4, quarter)
            sp.wait_ge(sem("o_stored"), 16 * NQ)

        @block.gpsimd
        def _(pool):
            g = nc.gpsimd
            link = Link(pool, sem("pool_link"))
            g.memset(ones[:, :], 1.0).then_inc(sem("const"), 1)
            g.memset(epsc[:, :], EPS).then_inc(sem("const"), 1)
            link(g.memset(ident[:, :], 0.0), g.memset(band[:, :, :], 0.0),
                 g.memset(pair1[:, :], 0.0), g.memset(turnm[:, :], 0.0), g.memset(row[:, :], 0.0))
            turn3 = turnm[:, :].rearrange("p (h r) -> p h r", h=2)
            link(g.affine_select(out=ident[:, :], in_=ident[:, :], compare_op=ALU.not_equal, fill=1.0, base=0,
                                 pattern=[[-1, P]], channel_multiplier=1),
                 g.affine_select(out=band[:, 1, :], in_=band[:, 1, :], compare_op=ALU.is_ge, fill=NEG, base=0,
                                 pattern=[[-1, P]], channel_multiplier=1),
                 g.affine_select(out=band[:, 0, :], in_=band[:, 0, :], compare_op=ALU.is_gt, fill=NEG, base=0,
                                 pattern=[[1, P]], channel_multiplier=-1),
                 g.affine_select(out=turn3[:, :, 0:8], in_=turn3[:, :, 0:8], compare_op=ALU.not_equal, fill=-1.0,
                                 base=-8, pattern=[[-DH, 2], [-1, 8]], channel_multiplier=1),
                 g.affine_select(out=turn3[:, :, 8:16], in_=turn3[:, :, 8:16], compare_op=ALU.not_equal, fill=1.0,
                                 base=0, pattern=[[-DH, 2], [-1, 8]], channel_multiplier=1))
            link(g.memset(pair1[0:DH, 0:DH], 1.0))
            link(g.memset(pair1[DH:P, DH:P], 1.0))
            freq = row[:, :].rearrange("o (h r) -> o h r", h=2)
            for r in range(16):
                last = g.memset(freq[:, :, r:r + 1], float(ROPE[r % 8]))
            link(last)
            g.tensor_copy(identb[:, :], ident[:, :]).then_inc(sem("const"), 1)

            def split_lo(u):
                pool.wait_ge(w_hi, u.n + 1)
                wait(pool, gemm_done, u.n - (SLOTS - 1))
                g.tensor_tensor(wL[:, u.slot], w32[:, u.slot % 2], wH[:, u.slot].bitcast(f32),
                                ALU.subtract).then_inc(w_lo, 1)

            def split_next(u):
                if u.n + AHEAD < NU:
                    split_lo(Unit(u.n + AHEAD))
            for n in range(AHEAD):
                split_lo(Unit(n))
            split_next(Unit(0))

            def pair(t):
                for j in range(4):
                    split_lo(Unit(UA + AHEAD, j, t, 4))
            repeated(pool, 8, pair)
            for n in range(8):
                split_next(Unit(UOA, n))
            for n in range(4):
                split_next(Unit(UKV, n))

            def group(t):
                for j in range(4):
                    split_lo(Unit(UB + AHEAD, j, t, 4))
            repeated(pool, 4, group)
            for n in range(8):
                split_next(Unit(UOB, n))
            pool.wait_ge(sem("ada_done"), 48)
            link(g.iota(jj, pattern=[[0, P]], base=0, channel_multiplier=1),
                 g.iota(ii, pattern=[[1, P]], base=0, channel_multiplier=0),
                 g.memset(restart, 1.0))
            g.memset(restart.rearrange("p (c k) -> p c k", k=64)[:, :, 0:1], 0.0).then_inc(sem("iotas"), 1)
            for n in range(3):
                split_next(Unit(UI, n))
            pool.wait_ge(sem("xor"), 1)
            g.affine_select(out=jx, in_=jx, compare_op=ALU.is_gt, fill=0.0, base=0, pattern=[[1, P]],
                            channel_multiplier=-1).then_inc(sem("later"), 1)
            for n in range(3, 13):
                split_next(Unit(UI, n))

            def differences(t, steps):
                for step in steps:
                    if step == 0:
                        pool.wait_ge(sem("h_g"), t + 1 + since("h_g"))
                        half = lambda x: x.rearrange("p (c a k) -> p c a k", c=4, a=2)
                        g.tensor_tensor(half(gf)[:, :, 1, :], half(gc)[:, :, 1, :],
                                        half(gc)[:, :, 0, 63:64].broadcast_to((P, 4, 64)), ALU.add)
                        g.tensor_copy(half(gf)[:, :, 0, :], half(gc)[:, :, 0, :]).then_inc(sem("h_diff"), 1)
                        continue
                    wait(pool, sem("h_x"), (t * 9 + (step - 1 if step > 1 else 0)) + since("h_x"))
                    if step == 1:
                        pool.wait_ge(sem("h_diff"), t * 9 + 1 + since("h_diff"))
                        whole = lambda x: x.rearrange("p (c k) -> p c k", c=4)
                        g.tensor_tensor(whole(dd[:, 1, :]), whole(gf)[:, :, P - 1:P].broadcast_to((P, 4, P)), whole(gf),
                                        ALU.subtract).then_inc(sem("h_diff"), 1)
                        continue
                    m = (P // 2) >> (step - 2)
                    half = lambda x: x.rearrange("p (n a m) -> p n a m", a=2, m=m)
                    d, c = half(dd[:, step % 2, :]), half(gc)
                    mid = c[:, :, 0, m - 1:m].broadcast_to((P, SEQ // (2 * m), m))
                    g.tensor_tensor(d[:, :, 0, :], mid, c[:, :, 0, :], ALU.subtract)
                    if m == 64:
                        g.tensor_copy(d[:, :, 1, :], c[:, :, 1, :]).then_inc(sem("h_diff"), 1)
                    else:
                        g.tensor_tensor(d[:, :, 1, :], c[:, :, 1, :], mid, ALU.subtract).then_inc(sem("h_diff"), 1)

            def head(t, work=True):
                for j in range(4):
                    if work and j < 3:
                        differences(t - 1, range(3 * j, 3 * j + 3))
                    split_lo(Unit(UH + AHEAD, j, t, 4))
            head(0, False)
            repeated(pool, 4, head, first=1)
            differences(3, range(9))
            for n in range(8):
                split_next(Unit(UOM, n))
            def quarter(c, n_units=16):
                for n in range(n_units):
                    split_lo(Unit(UM + AHEAD, n, c, 16))
            repeated(pool, 3, quarter)
            quarter(3, 13)

        mm = nc.tensor.matmul
        v, s = nc.vector, nc.scalar

        def rsqrt_scalar(link, which, scale, taken, done):
            link(s.activation(rinv[:, which, :], N[:, :], ACT.Ln, bias=epsc[:, 0:1], scale=scale))
            s.activation(rms[:, which, :], N[:, :], ACT.Identity, bias=epsc[:, 0:1], scale=scale).then_inc(taken, 1)
            link(s.activation(rinv[:, which, :], rinv[:, which, :], ACT.Exp, scale=-0.5))
            s.activation(sq[:, which, :], rinv[:, which, :], ACT.Square).then_inc(done, 1)

        def rsqrt_vector(link, which):
            link(v.scalar_tensor_tensor(out=sq[:, which, :], in0=sq[:, which, :], scalar=-0.5, in1=rms[:, which, :],
                                        op0=ALU.mult, op1=ALU.mult))
            link(v.scalar_tensor_tensor(out=rinv[:, which, :], in0=sq[:, which, :], scalar=1.5, in1=rinv[:, which, :],
                                        op0=ALU.add, op1=ALU.mult))

        NORMS = {"a": (vecT, VEC["norm_a_g"], None, hi1, lo1), "kv": (vecT, VEC["kv_norm_g"], None, hi1, lo1),
                 "b": (vecT, VEC["norm_b_g"], None, hi2, lo2), "mix": (gainm, 0, 0, hi2, lo2),
                 "mlp": (gainm, 8, 24, hi2, lo2), "f": (vecT, VEC["final_norm_w_2"], None, None, None)}

        def norm_squares(act, link, key, x_ready, before=0):
            for k in range(KT):
                act.wait_ge(x_ready, before + k + 1)
                wait(act, sem(f"sums_{key}"), k - 1 + since(f"sums_{key}"))
                s.activation(sq[:, k % 2, :], xT[:, k, :], ACT.Square).then_inc(sem(f"sq_{key}"), 1)
            act.wait_ge(sem(f"sums_{key}"), KT + since(f"sums_{key}"))
            rsqrt_scalar(link, 0, 1.0 / D, sem(f"meansq_{key}"), sem(f"root_{key}"))

        def norm_high(act, key):
            _, _, shift, H, L = NORMS[key]
            for k in range(KT):
                act.wait_ge(sem(f"h32_{key}"), k + 1 + since(f"h32_{key}"))
                bias = 0.0 if shift is None else modT[:, shift + k:shift + k + 1]
                s.activation(H[:, k, :], tmp[:, k % 2, :], ACT.Identity, bias=bias).then_inc(sem(f"hhi_{key}"), 1)

        def norm_tensor(pe, key):
            for k in range(KT):
                pe.wait_ge(sem(f"sq_{key}"), k + 1 + since(f"sq_{key}"))
                mm(N[:, :], ones[:, :], sq[:, k % 2, :], start=(k == 0), stop=(k == KT - 1)
                   ).then_inc(sem(f"sums_{key}"), 1)

        def norm_vector(dve, link, key):
            table, gain, shift, H, L = NORMS[key]
            root = key if key != "b" else "kv"
            if key == root:
                dve.wait_ge(sem(f"root_{key}"), 1 + since(f"root_{key}"))
                rsqrt_vector(link, 0)

            def low(k):
                dve.wait_ge(sem(f"hhi_{key}"), k + 1 + since(f"hhi_{key}"))
                if shift is None:
                    v.tensor_tensor(L[:, k, :], tmp[:, k % 2, :], H[:, k, :].bitcast(f32),
                                    ALU.subtract).then_inc(sem(f"lo_{key}"), 1)
                else:
                    v.scalar_tensor_tensor(out=L[:, k, :], in0=tmp[:, k % 2, :], scalar=modT[:, shift + k:shift + k + 1],
                                           in1=H[:, k, :].bitcast(f32), op0=ALU.add, op1=ALU.subtract
                                           ).then_inc(sem(f"lo_{key}"), 1)
            for k in range(KT):
                dst = xT[:, k, :] if H is None else tmp[:, k % 2, :]
                if H is not None:
                    wait(dve, sem(f"lo_{key}"), k - 1 + since(f"lo_{key}"))
                v.scalar_tensor_tensor(out=dst, in0=xT[:, k, :], scalar=table[:, gain + k:gain + k + 1],
                                       in1=rinv[:, 0, :], op0=ALU.mult, op1=ALU.mult).then_inc(sem(f"h32_{key}"), 1)
                if H is not None and k >= 1:
                    low(k - 1)
            if H is not None:
                low(KT - 1)

        def gemm(pe, u, H, L, free, h_ready=None):
            pe.wait_ge(w_lo, u.n + 1)
            if free is not None:
                wait(pe, *free)
            for k in range(KT):
                if h_ready is not None:
                    pe.wait_ge(h_ready[0], h_ready[1] + k + 1)
                whi, wlo = wH[:, u.slot, k, :], wL[:, u.slot, k, :]
                mm(G[u.bank][:, :], whi, H[:, k, :], start=(k == 0), stop=False)
                mm(G[u.bank][:, :], whi, L[:, k, :], start=False, stop=False)
                last = mm(G[u.bank][:, :], wlo, H[:, k, :], start=False, stop=(k == KT - 1))
            last.then_inc(gemm_done, 1)

        def silu_scalar_1(act, link, ph, n, z, th):
            link(s.activation(th, z, ACT.Abs))
            link(s.activation(th, th, ACT.Exp, scale=-1.0))
            s.activation(th, th, ACT.Ln, bias=1.0).then_inc(sem(f"{ph}_softplus"), 1)

        def silu_vector_1(dve, ph, n, z, th):
            dve.wait_ge(sem(f"{ph}_softplus"), n + 1 + since(f"{ph}_softplus"))
            v.scalar_tensor_tensor(out=th, in0=z, scalar=0.0, in1=th, op0=ALU.min, op1=ALU.subtract
                                   ).then_inc(sem(f"{ph}_logsig"), 1)

        def silu_scalar_2(act, ph, n, th):
            act.wait_ge(sem(f"{ph}_logsig"), n + 1 + since(f"{ph}_logsig"))
            s.activation(th, th, ACT.Exp).then_inc(sem(f"{ph}_sigmoid"), 1)

        def scores(pe, ph, t, h, masked, qn=qn, kn=kn):
            lo, hi = h * DH, (h + 1) * DH
            if h == 0 and masked:
                pe.wait_ge(sem(f"{ph}_qk"), 2 * t + 2)
            for q in range(NQ):
                wait(pe, sem(f"{ph}_logits"), t * 8 + (4 * h + q - 1) + since(f"{ph}_logits"))
                w = (q + 1) * P
                last = mm(S[q % 2][:, 0:w], qn[lo:hi, q * P:(q + 1) * P], kn[lo:hi, 0:w], start=True, stop=not masked)
                if masked:
                    last = mm(S[q % 2][:, q * P:w], identb[:, :], causal, start=False, stop=True)
                last.then_inc(sem(f"{ph}_scores"), 1)

        def take_logits(dve, ph, t, h, bias):
            for q in range(NQ):
                w = (q + 1) * P
                dve.wait_ge(sem(f"{ph}_scores"), t * 8 + (4 * h + q + 1) + since(f"{ph}_scores"))
                if q == 0:
                    wait(dve, sem(f"{ph}_exps"), t * 8 + 4 * h + since(f"{ph}_exps"))
                v.memset(stat[:, h, 0, q:q + 1], 0.0)
                v.tensor_tensor_reduce(out=logits[:, A_AT[q]:A_AT[q] + w], in0=S[q % 2][:, 0:w], in1=bias(h, q),
                                       scale=-1.0, scalar=HUGE, op0=ALU.add, op1=ALU.min,
                                       accum_out=stat[:, h, 1, q:q + 1]).then_inc(sem(f"{ph}_logits"), 1)

        def exps(act, ph, t, h):
            for q in range(NQ):
                act.wait_ge(sem(f"{ph}_logits"), t * 8 + (4 * h + q + 1) + since(f"{ph}_logits"))
                if q == 0:
                    wait(act, sem(f"{ph}_pT"), t * 8 + 4 * h + since(f"{ph}_pT"))
                s.activation(probs[:, A_AT[q]:A_AT[q] + (q + 1) * P], logits[:, A_AT[q]:A_AT[q] + (q + 1) * P],
                             ACT.Exp, bias=stat[:, h, 1, q:q + 1], scale=-1.0,
                             accum_out=stat[:, h, 2, q:q + 1]).then_inc(sem(f"{ph}_exps"), 1)

        def normalise(dve, link, ph, t, h):
            for q in range(NQ):
                w = (q + 1) * P
                dve.wait_ge(sem(f"{ph}_exps"), t * 8 + (4 * h + q + 1) + since(f"{ph}_exps"))
                link(v.reciprocal(stat[:, h, 3, q:q + 1], stat[:, h, 2, q:q + 1]))
                v.tensor_scalar(probs[:, A_AT[q]:A_AT[q] + w], probs[:, A_AT[q]:A_AT[q] + w],
                                stat[:, h, 3, q:q + 1], None, ALU.mult).then_inc(sem(f"{ph}_probs"), 1)

        def turn_probs(pe, ph, t, h):
            for kt in range(NQ):
                wait(pe, sem(f"{ph}_pT_out"), t * 8 + (4 * h + kt - 1) + since(f"{ph}_pT_out"))
                if h == 0 and kt == 0 and ph == "a":
                    pe.wait_ge(sem(f"{ph}_v"), t + 1 + since(f"{ph}_v"))
                for q in range(kt, NQ):
                    pe.wait_ge(sem(f"{ph}_probs"), t * 8 + (4 * h + q + 1) + since(f"{ph}_probs"))
                    last = nc.tensor.transpose(T[kt % 2][:, (q - kt) * P:(q - kt + 1) * P],
                                               probs[:, A_AT[q] + kt * P:A_AT[q] + (kt + 1) * P], ident[:, :])
                last.then_inc(sem(f"{ph}_pT"), 1)

        def take_turned(dve, ph, t, h):
            for kt in range(NQ):
                dve.wait_ge(sem(f"{ph}_pT"), t * 8 + (4 * h + kt + 1) + since(f"{ph}_pT"))
                if kt == 0:
                    wait(dve, sem(f"{ph}_o"), t * 2 + h + since(f"{ph}_o"))
                v.tensor_copy(probsT[:, AT_AT[kt]:AT_AT[kt] + SEQ - kt * P], T[kt % 2][:, 0:SEQ - kt * P]
                              ).then_inc(sem(f"{ph}_pT_out"), 1)

        def mix_values(pe, ph, t, h, v_of, o_taken):
            if h == 0:
                wait(pe, *o_taken)
            for kt in range(NQ):
                pe.wait_ge(sem(f"{ph}_pT_out"), t * 8 + (4 * h + kt + 1) + since(f"{ph}_pT_out"))
                last = mm(O[h * DH:(h + 1) * DH, kt * P:SEQ], v_of(kt, h),
                          probsT[:, AT_AT[kt]:AT_AT[kt] + SEQ - kt * P], start=(kt == 0), stop=(kt == NQ - 1))
            last.then_inc(sem(f"{ph}_o"), 1)

        def raw_scalar(act, ph, n, which, u, dst, used):
            act.wait_ge(gemm_done, u.n + 1)
            if used is not None:
                wait(act, *used)
            s.activation(sq[:, which, :], G[u.bank][:, :], ACT.Square).then_inc(sem(f"{ph}_sq{which}"), 1)
            s.activation(dst[:, :], G[u.bank][:, :], ACT.Copy).then_inc(sem(f"{ph}_raw{which}"), 1)

        def sum_tensor(pe, ph, n, which, n_free):
            pe.wait_ge(sem(f"{ph}_sq{which}"), n + 1)
            if n_free is not None:
                wait(pe, *n_free)
            mm(N[:, :], pair1[:, :], sq[:, which, :], start=True, stop=True).then_inc(sem(f"{ph}_sum{which}"), 1)

        def root_scalar(act, link, ph, n, which):
            act.wait_ge(sem(f"{ph}_sum{which}"), n + 1)
            rsqrt_scalar(link, which, 1.0 / DH, sem(f"{ph}_sum{which}_taken"), sem(f"{ph}_root{which}"))

        def normed_vector(dve, link, ph, n, which, src, dst, gain, used, done):
            dve.wait_ge(sem(f"{ph}_root{which}"), n + 1)
            rsqrt_vector(link, which)
            if used is not None:
                wait(dve, *used)
            v.scalar_tensor_tensor(out=dst, in0=src[:, :], scalar=gains[:, gain:gain + 1], in1=rinv[:, which, :],
                                   op0=ALU.mult, op1=ALU.mult).then_inc(done, 1)

        def gate_vector(dve, ph, t, z, th, o_ready):
            wait(dve, *o_ready)
            dve.wait_ge(sem(f"{ph}_silu"), t + 1 + since(f"{ph}_silu"))
            wait(dve, sem(f"{ph}_gated_lo"), t + since(f"{ph}_gated_lo"))
            v.tensor_tensor(og[:, :], O[:, :], sg[:, :], ALU.mult).then_inc(sem(f"{ph}_gated"), 1)

        def silu_vector_2(dve, ph, n, z, th, used):
            dve.wait_ge(sem(f"{ph}_sigmoid"), n + 1 + since(f"{ph}_sigmoid"))
            wait(dve, *used)
            v.tensor_tensor(sg[:, :], z, th, ALU.mult).then_inc(sem(f"{ph}_silu"), 1)

        def gated_high(act, ph, t, H):
            act.wait_ge(sem(f"{ph}_gated"), t + 1 + since(f"{ph}_gated"))
            s.activation(H[:, bass.ds(t, 1), :], og[:, :].unsqueeze(1), ACT.Copy).then_inc(sem(f"{ph}_gated_hi"), 1)

        def gated_low(dve, ph, t, H, L):
            dve.wait_ge(sem(f"{ph}_gated_hi"), t + 1 + since(f"{ph}_gated_hi"))
            v.tensor_tensor(L[:, bass.ds(t, 1), :], og[:, :].unsqueeze(1), H[:, bass.ds(t, 1), :].bitcast(f32),
                            ALU.subtract).then_inc(sem(f"{ph}_gated_lo"), 1)

        def add_output(dve, ph, unit, gate=None):
            for n in range(KT):
                u = unit(n)
                dve.wait_ge(gemm_done, u.n + 1)
                if gate is None:
                    v.tensor_tensor(xT[:, n, :], G[u.bank][:, :], xT[:, n, :], ALU.add).then_inc(sem(f"x_{ph}"), 1)
                else:
                    v.scalar_tensor_tensor(out=xT[:, n, :], in0=G[u.bank][:, :], scalar=modT[:, gate + n:gate + n + 1],
                                           in1=xT[:, n, :], op0=ALU.mult, op1=ALU.add).then_inc(sem(f"x_{ph}"), 1)

        def ada(pe, e, slot, of_slot):
            pe.wait_ge(sem(f"ada_here{slot}"), of_slot * 16 + 16)
            for k in range(KT):
                last = mm(T[1][:, bass.ds(384 + e, 1)], adaw[:, slot, k, :], cact[:, k:k + 1], start=(k == 0),
                          stop=(k == KT - 1))
            last.then_inc(sem("ada_done"), 1)

        def scores_b(pe, t, h):
            lo, hi = h * DH, (h + 1) * DH
            if h == 0:
                pe.wait_ge(sem("b_q"), t + 1)
            wait(pe, sem("b_exps"), t * 8 + 4 * h)
            for q in range(NQ):
                at = [0, P, 0, 2 * P][q]
                w, k0 = B_W[q], max(q - 1, 0) * P
                mm(S[q // 2][:, at:at + w], qn[lo:hi, q * P:(q + 1) * P], kg[lo:hi, k0:k0 + w], start=True, stop=False)
                last = mm(S[q // 2][:, at:at + w], identb[:, :],
                          causal if q == 0 else band[:, :, :].rearrange("p a k -> p (a k)"), start=False, stop=True)
            last.then_inc(sem("b_scores"), 1)

        def maxima_b(dve, link, t, h, head):
            dve.wait_ge(sem("b_scores"), t * 2 + (h + 1))
            wait(dve, sem("b_sink"), t * 2 + (h - 1))
            v.reduce_max(stat[:, h, 0, 0:1], S[0][:, 0:P], AX.X)
            v.reduce_max(stat[:, h, 0, 1:2], S[0][:, P:3 * P], AX.X)
            link(v.reduce_max(stat[:, h, 0, 2:4], S[1][:, :].rearrange("p (q k) -> p q k", q=2), AX.X))
            link(v.tensor_scalar(stat[:, h, 0, :], stat[:, h, 0, :], sinkb[:, bass.ds(head, 1)], None, ALU.max))
            v.tensor_scalar(stat[:, h, 1, :], stat[:, h, 0, :], -1.0, None, ALU.mult).then_inc(sem("b_negmax"), 1)

        def exps_b(act, t, h, head):
            act.wait_ge(sem("b_negmax"), t * 2 + (h + 1))
            wait(act, sem("b_pT"), t * 4 + 2 * h)
            for q in range(NQ):
                at = [0, P, 0, 2 * P][q]
                s.activation(probs[:, B_AT[q]:B_AT[q] + B_W[q]], S[q // 2][:, at:at + B_W[q]], ACT.Exp,
                             bias=stat[:, h, 1, q:q + 1], accum_out=stat[:, h, 2, q:q + 1]).then_inc(sem("b_exps"), 1)
            s.activation(stat[:, h, 4, :], stat[:, h, 1, :], ACT.Exp, bias=sinkb[:, bass.ds(head, 1)]
                         ).then_inc(sem("b_sink"), 1)

        def normalise_b(dve, link, t, h):
            dve.wait_ge(sem("b_sink"), t * 2 + (h + 1))
            link(v.tensor_tensor(stat[:, h, 5, :], stat[:, h, 2, :], stat[:, h, 4, :], ALU.add))
            link(v.reciprocal(stat[:, h, 3, :], stat[:, h, 5, :]))
            for q in range(NQ):
                v.tensor_scalar(probs[:, B_AT[q]:B_AT[q] + B_W[q]], probs[:, B_AT[q]:B_AT[q] + B_W[q]],
                                stat[:, h, 3, q:q + 1], None, ALU.mult).then_inc(sem("b_probs"), 1)

        B_BLOCKS = [(0, 0), (1, 0), (1, 1), (2, 1), (2, 2), (3, 2), (3, 3)]

        def turn_b(pe, t, h):
            for n, (q, kt) in enumerate(B_BLOCKS):
                if n in (0, 4):
                    wait(pe, sem("b_pT_out"), t * 4 + (2 * h - 2 + n // 4 + 1))
                pe.wait_ge(sem("b_probs"), t * 8 + (4 * h + q + 1))
                src = B_AT[q] + (kt - max(q - 1, 0)) * P
                last = nc.tensor.transpose(T[n // 4][:, (n % 4) * P:(n % 4 + 1) * P], probs[:, src:src + P], ident[:, :])
                if n in (3, 6):
                    last.then_inc(sem("b_pT"), 1)

        def take_turned_b(dve, t, h):
            for n, w in ((0, 4), (1, 3)):
                dve.wait_ge(sem("b_pT"), t * 4 + (2 * h + n + 1))
                if n == 0:
                    wait(dve, sem("b_o"), t * 2 + h)
                v.tensor_copy(probsT[:, n * 512:n * 512 + w * P], T[n][:, 0:w * P]).then_inc(sem("b_pT_out"), 1)

        def mix_b(pe, t, h):
            if h == 0:
                wait(pe, sem("b_gated"), t)
            for n, (q, kt) in enumerate(B_BLOCKS):
                if n in (0, 4):
                    pe.wait_ge(sem("b_pT_out"), t * 4 + (2 * h + n // 4 + 1))
                last = mm(O[h * DH:(h + 1) * DH, q * P:(q + 1) * P], vg[:, kt, :], probsT[:, n * P:(n + 1) * P],
                          start=(q != kt or q == 0), stop=(q == kt))
            last.then_inc(sem("b_o"), 1)

        @block.tensor
        def _(pe):
            pe.wait_ge(sem("const"), 3)
            pe.wait_ge(sem("x_here"), 16)
            for k in range(KT):
                wait(pe, sem("x_copied"), k - 1)
                for q in range(NQ):
                    last = nc.tensor.transpose(T[k % 2][:, q * P:(q + 1) * P], xin[:, q, k * P:(k + 1) * P], ident[:, :])
                last.then_inc(sem("x_turned"), 1)
            pe.wait_ge(sem("vec_here"), 16 * (len(VEC_ROWS) + 11))
            nc.tensor.transpose(O[:, 0:N_VEC], vecs[:, :], ident[0:N_VEC, 0:N_VEC])
            nc.tensor.transpose(O[:, 128:129], row[:, :], ident[0:1, 0:1])
            nc.tensor.transpose(O[:, 192:254], taps[:, :], ident[0:62, 0:62]).then_inc(sem("vec_turned"), 1)
            norm_tensor(pe, "a")
            gemm(pe, Unit(0), hi1, lo1, None, mark("lo_a", 0))
            pe.wait_ge(sem("c_silu"), 1)

            def turn_v(t):
                pe.wait_ge(sem("a_vraw"), t + 1)
                wait(pe, sem("a_pT_out"), t * 8)
                for q in range(NQ):
                    last = nc.tensor.transpose(T[0][:, q * P:(q + 1) * P], vraw[:, q * P:(q + 1) * P], ident[:, :])
                last.then_inc(sem("a_vturn"), 1)

            def v_a(kt, h):
                return vp[:, kt, h * DH:(h + 1) * DH]

            def pair_a(t, attend=True):
                gemm(pe, Unit(UA, 0, t, 4), hi1, lo1, mark("a_vraw", t))
                if attend:
                    scores(pe, "a", t - 1, 0, True)
                gemm(pe, Unit(UA, 1, t, 4), hi1, lo1, mark("a_zraw", t) if attend else mark("f_raw", 1))
                if attend:
                    turn_probs(pe, "a", t - 1, 0)
                    scores(pe, "a", t - 1, 1, True)
                gemm(pe, Unit(UA, 2, t, 4), hi1, lo1, mark("a_raw0", t + 1))
                if attend:
                    mix_values(pe, "a", t - 1, 0, v_a, mark("a_gated", t - 1))
                for j in range(2):
                    ada(pe, 4 * t + j, j, t * 2)
                if attend:
                    turn_probs(pe, "a", t - 1, 1)
                sum_tensor(pe, "a", t, 0, mark("a_sum1_taken", t))
                gemm(pe, Unit(UA, 3, t, 4), hi1, lo1, mark("a_raw1", t + 1))
                sum_tensor(pe, "a", t, 1, mark("a_sum0_taken", t + 1))
                if attend:
                    mix_values(pe, "a", t - 1, 1, v_a, mark("a_gated", t - 1))
                for j in range(2):
                    ada(pe, 4 * t + (j + 2), j, t * 2 + 1)
                turn_v(t)
            pair_a(0, False)
            repeated(pe, 8, pair_a, first=1)
            scores(pe, "a", 7, 0, True)
            turn_probs(pe, "a", 7, 0)
            scores(pe, "a", 7, 1, True)
            mix_values(pe, "a", 7, 0, v_a, mark("a_gated", 7))
            turn_probs(pe, "a", 7, 1)
            mix_values(pe, "a", 7, 1, v_a, mark("a_gated", 7))
            for n in range(8):
                gemm(pe, Unit(UOA, n), hi2, lo2, mark("x_a", n - 1) if n > 1 else [mark("a_vraw", 8), mark("a_zraw", 8)][n],
                     mark("a_gated_lo", 0) if n == 0 else None)

            norm_tensor(pe, "kv")
            for n in range(4):
                gemm(pe, Unit(UKV, n), hi1, lo1, [mark("x_a", 7), mark("x_a", 8), mark("bk_raw0", 1), mark("bk_raw1", 1)][n],
                     mark("lo_kv", 0) if n == 0 else None)
                if n >= 1 and n < 3:
                    sum_tensor(pe, "bk", 0, n - 1, mark("bk_turn_taken", n - 1) if n > 1 else None)
                    wait(pe, sem("bk_normed"), n)
                    mm(N[:, :], turnm[:, :], tmp[:, n - 1, :], start=True, stop=True).then_inc(sem("bk_turned"), 1)
            for n in range(2):
                pe.wait_ge(sem("bv_raw"), n + 1)
                wait(pe, sem("bv_out"), n)
                src = [vraw, zraw][n]
                for q in range(NQ):
                    last = nc.tensor.transpose(T[0][:, q * P:(q + 1) * P], src[:, q * P:(q + 1) * P], ident[:, :])
                last.then_inc(sem("bv_turn"), 1)

            def pair_b(t, attend, first):
                u0, u1 = t["u"]
                gemm(pe, u0, hi2, lo2, mark("b_raw0", t["n"]) if not first else mark("bv_raw", 1),
                     mark("lo_b", 0) if first else None)
                if attend:
                    wait(pe, sem("b_kg"), t["gprev"])
                    scores_b(pe, t["n"] - 1, 0)
                sum_tensor(pe, "b", t["n"], 0, mark("b_turn_taken", t["n"]) if not first else mark("bk_turn_taken", 2))
                if attend:
                    turn_b(pe, t["n"] - 1, 0)
                    scores_b(pe, t["n"] - 1, 1)
                gemm(pe, u1, hi2, lo2, mark("b_zraw", t["n"]) if not first else mark("bv_raw", 2))
                if attend:
                    mix_b(pe, t["n"] - 1, 0)
                    turn_b(pe, t["n"] - 1, 1)
                pe.wait_ge(sem("b_normed"), t["n"] + 1)
                mm(N[:, :], turnm[:, :], qraw[:, :], start=True, stop=True).then_inc(sem("b_turned"), 1)
                if attend:
                    mix_b(pe, t["n"] - 1, 1)
                for j in range(2):
                    ada(pe, 32 + 2 * t["n"] + j, j, t["n"] + 16)

            def group_b(g):
                static = isinstance(g, int)
                pair_b(dict(n=g * 2, u=(Unit(UB, 0, g, 4), Unit(UB, 1, g, 4)), gprev=g), not (static and g == 0), static and g == 0)
                pair_b(dict(n=g * 2 + 1, u=(Unit(UB, 2, g, 4), Unit(UB, 3, g, 4)), gprev=g + 1), True, False)
            group_b(0)
            repeated(pe, 4, group_b, first=1)
            pe.wait_ge(sem("b_kg"), 4)
            scores_b(pe, 7, 0)
            turn_b(pe, 7, 0)
            scores_b(pe, 7, 1)
            mix_b(pe, 7, 0)
            turn_b(pe, 7, 1)
            mix_b(pe, 7, 1)
            for n in range(8):
                gemm(pe, Unit(UOB, n), hi1, lo1, mark("x_b", n - 1) if n > 1 else [mark("b_raw0", 8), mark("b_zraw", 8)][n],
                     mark("b_gated_lo", 0) if n == 0 else None)
            norm_tensor(pe, "mix")
            for n in range(3):
                gemm(pe, Unit(UI, n), hi2, lo2, [mark("x_b", 7), mark("x_b", 8), mark("i_raw", 1)][n],
                     mark("lo_mix", 0) if n == 0 else None)
            gemm(pe, Unit(UI, 3), hi2, lo2, mark("i_raw", 2))
            pe.wait_ge(sem("i_raw"), 3)
            for q in range(NQ):
                last = nc.tensor.transpose(T[0][:, q * P:(q + 1) * P], vraw[:, q * P:(q + 1) * P], ident[:, :])
            last.then_inc(sem("iw_turned"), 1)
            pe.wait_ge(sem("ik_here"), 64)
            for n in range(24):
                q, h = 1 + n // 8, n % 8
                lo = 32 * (h % 4)
                wait(pe, sem("i_relu"), n - 1)
                mm(S[n % 2][:, 0:(q + 1) * P], iqT[lo:lo + 32, h // 4, q * P:(q + 1) * P],
                   ik4[lo:lo + 32, 0:(q + 1) * P], start=True, stop=True, tile_position=(lo, 0)).then_inc(sem("i_scores"), 1)
                if n % 5 == 4 and n // 5 < 5 and UI + 4 + n // 5 < UI + 9:
                    j = 4 + n // 5
                    gemm(pe, Unit(UI, j), hi2, lo2, mark("i_raw", j - 1))
            gemm(pe, Unit(UI, 8), hi2, lo2, mark("i_raw", 7))
            for n in range(2):
                pe.wait_ge(sem("i_raw"), 8 + n)
                wait(pe, sem("sv_out"), n)
                if n == 0:
                    pe.wait_ge(sem("iw_there"), 1)
                for q in range(NQ):
                    last = nc.tensor.transpose(T[0][:, q * P:(q + 1) * P], svT[:, n, q * P:(q + 1) * P], ident[:, :])
                last.then_inc(sem("sv_turned"), 1)
            for n in range(9, 13):
                gemm(pe, Unit(UI, n), hi2, lo2, mark("i_raw", n - 1))
            pe.wait_ge(sem("sv_out"), 2)

            def v_c(t):
                return lambda kt, h: svp[:, kt, (2 * t + h) * DH:(2 * t + h + 1) * DH]
            for t in range(2):
                for h in range(2):
                    scores(pe, "c", t, h, False, sqT[:, t, :], skT[:, t, :])
                    turn_probs(pe, "c", t, h)
                    mix_values(pe, "c", t, h, v_c(t), mark("c_gated", t))

            def products(t, first, last_):
                for p in range(first, last_):
                    wait(pe, sem("h_aT"), t * 8 + (p - 1) + since("h_aT"))
                    if p < 7:
                        pe.wait_ge(sem("h_x"), t * 9 + (p + 3) + since("h_x"))
                    for c in range(NQ):
                        cs_ = slice(c * P, (c + 1) * P)
                        x = xx[:, p % 2, cs_]
                        last = mm(S[p % 2][:, cs_], kn[:, cs_] if p == 7 else x, qn[:, cs_] if p == 7 else x,
                                  start=True, stop=True)
                    last.then_inc(sem("h_products"), 1)

            def states(t):
                pe.wait_ge(sem("h_x"), t * 9 + 2 + since("h_x"))
                for c in range(3):
                    last = nc.tensor.transpose(T[1][:, c * P:(c + 1) * P], ke[:, c * P:(c + 1) * P], ident[:, :])
                last.then_inc(sem("h_keT"), 1)
                pe.wait_ge(sem("h_keT_out"), t + 1)
                pe.wait_ge(sem("h_v"), t + 1 + since("h_v"))
                for c in range(3):
                    last = mm(T[0][:, c * P:(c + 1) * P], keT[:, c, :], vp[:, c, :], start=True, stop=True)
                last.then_inc(sem("h_update"), 1)

            def outputs(t):
                pe.wait_ge(sem("h_state"), t * 3 + 3 + since("h_state"))
                pe.wait_ge(sem("h_aT"), t * 8 + 8 + since("h_aT"))
                wait(pe, sem("h_normed"), t)
                for c in range(NQ):
                    cs_ = slice(c * P, (c + 1) * P)
                    if c:
                        mm(O[:, cs_], state[:, c - 1, :], qe[:, cs_], start=True, stop=False)
                    last = mm(O[:, cs_], vp[:, c, :], aT[:, c, :], start=(c == 0), stop=True)
                last.then_inc(sem("h_o"), 1)
                pe.wait_ge(sem("h_sq"), t + 1 + since("h_sq"))
                wait(pe, sem("h_meansq"), t + since("h_meansq"))
                pe.wait_ge(sem("conv_var"), 1)
                mm(N[:, :], ones[:, :], sq[:, 0, :], start=True, stop=True).then_inc(sem("h_sum"), 1)

            def turn_h(t):
                pe.wait_ge(sem("h_raw2"), t + 1 + since("h_raw2"))
                wait(pe, sem("h_state"), t * 3 + since("h_state"))
                for q in range(NQ):
                    last = nc.tensor.transpose(T[0][:, q * P:(q + 1) * P], vraw[:, q * P:(q + 1) * P], ident[:, :])
                last.then_inc(sem("h_vturn"), 1)

            def head(t, work=True):
                gemm(pe, Unit(UH, 0, t, 4), hi2, lo2, mark("h_raw2", t) if work else mark("i_raw", 12))
                if work:
                    states(t - 1)
                    products(t - 1, 0, 2)
                gemm(pe, Unit(UH, 1, t, 4), hi2, lo2, mark("h_raw3", t) if work else mark("i_raw", 13))
                if work:
                    products(t - 1, 2, 5)
                gemm(pe, Unit(UH, 2, t, 4), hi2, lo2, mark("h_raw0", t + 1))
                if work:
                    products(t - 1, 5, 8)
                gemm(pe, Unit(UH, 3, t, 4), hi2, lo2, mark("h_raw1", t + 1))
                if work:
                    outputs(t - 1)
                turn_h(t)

            def conv_sums():
                for k in range(2):
                    pe.wait_ge(sem("conv"), k + 1)
                    last = mm(N[:, :], ones[:, :], cacc[:, k, :], start=(k == 0), stop=(k == 1))
                last.then_inc(sem("conv_sum"), 1)
                pe.wait_ge(sem("conv_centred"), 2)
                for k in range(2):
                    pe.wait_ge(sem("conv_sq"), k + 1)
                    last = mm(N[:, :], ones[:, :], sq[:, k, :], start=(k == 0), stop=(k == 1))
                last.then_inc(sem("conv_sqsum"), 1)
            head(0, False)
            conv_sums()
            repeated(pe, 4, head, first=1)
            states(3)
            products(3, 0, 8)
            outputs(3)
            for name, count in (("c_gated_lo", 2), ("cv_gated_lo", 2), ("h_gated_lo", 4)):
                wait(pe, sem(name), count + since(name))
            for n in range(8):
                gemm(pe, Unit(UOM, n), hi1, lo1, mark("x_m", n - 1) if n > 1 else [mark("h_raw2", 4), mark("h_raw3", 4)][n])
            norm_tensor(pe, "mlp")

            def quarter(c):
                first = isinstance(c, int) and c == 0
                for n in range(8):
                    free = (mark("x_m", 7 + n) if first else mark("x_f", c * 8 + (n - 1))) if n < 2 else mark("f_relu", c * 8 + (n - 1))
                    gemm(pe, Unit(UM, n, c, 16), hi2, lo2, free, mark("lo_mlp", 0) if first and n == 0 else None)
                pe.wait_ge(sem("f_lo"), c * 8 + 8)
                for n in range(8):
                    free = mark("x_f", c * 8 + (n - 1)) if n > 1 else mark("f_relu", c * 8 + (7 + n))
                    gemm(pe, Unit(UM, 8 + n, c, 16), hi1, lo1, free)
            repeated(pe, 3, quarter)
            quarter(3)
            norm_tensor(pe, "f")
            for q in range(NQ):
                for half in range(2):
                    wait(pe, sem("y_out"), 2 * q + half - 1)
                    for k in range(4 * half, 4 * half + 4):
                        pe.wait_ge(sem("h32_f"), k + 1 + since("h32_f"))
                        last = nc.tensor.transpose(T[half][:, (k % 4) * P:(k % 4 + 1) * P], xT[:, k, q * P:(q + 1) * P], ident[:, :])
                    last.then_inc(sem("y_turned"), 1)

        @block.scalar
        def _(act):
            link = Link(act, sem("act_link"))
            s.preload_act_table_set("natural_log_exp_and_others")

            def split_hi(u):
                act.wait_ge(w_here[u.slot % 2], u.of_pair * 16 + 16)
                wait(act, gemm_done, u.n - (SLOTS - 1))
                s.activation(wH[:, u.slot], w32[:, u.slot % 2], ACT.Copy).then_inc(w_hi, 1)

            def split_next(u):
                if u.n + AHEAD < NU:
                    split_hi(Unit(u.n + AHEAD))

            for n in range(AHEAD):
                split_hi(Unit(n))
            act.wait_ge(sem("const"), 3)
            norm_squares(act, link, "a", sem("x_copied"))
            norm_high(act, "a")
            act.wait_ge(sem("vec_there"), 1)
            cond = vecT[:, VEC["c_2"]:VEC["c_2"] + KT]
            silu_scalar_1(act, link, "c", 0, cond, cth[:, :])
            silu_scalar_2(act, "c", 0, cth[:, :])
            split_next(Unit(0))
            act.wait_ge(gemm_done, 1)
            s.activation(fz[:, 0, :], G[0][0:16, :], ACT.Identity, bias=bfg[:, 0:1]).then_inc(sem("f_raw"), 1)
            act.wait_ge(sem("f_raw"), 1)
            link(s.activation(fz[:, 1, :], fz[:, 0, :], ACT.Abs))
            link(s.activation(fz[:, 2, :], fz[:, 1, :], ACT.Exp, scale=-1.0))
            s.activation(fz[:, 3, :], fz[:, 2, :], ACT.Ln, bias=1.0).then_inc(sem("f_ln"), 1)
            act.wait_ge(sem("c_ready"), 1)
            act.dma_start(c_dram, fz[:, 3, :]).then_inc(sem("c_stored"), 16)
            act.wait_ge(sem("c_stored"), 16)
            act.wait_ge(sem("angles"), 1)
            s.activation(sinb[:, :], sinb[:, :], ACT.Sin).then_inc(sem("sines"), 1)
            s.activation(cosb[:, :], cosb[:, :], ACT.Sin).then_inc(sem("sines"), 1)
            s.preload_act_table_set("natural_log_exp_and_others")

            def load_c(t):
                wait(act, sem("a_logits"), t * 8)
                act.dma_start(cbias[:, :, :], c_dram[bass.ds(t * 2, 2), :].partition_broadcast(P)
                              ).then_inc(sem("c_here"), 16)

            def pair_a(t, attend=True):
                if attend:
                    load_c(t - 1)
                split_hi(Unit(UA + AHEAD, 0, t, 4))
                raw_scalar(act, "a", t, 0, Unit(UA, 0, t, 4), qraw, mark("a_qk", t * 2))
                if attend:
                    exps(act, "a", t - 1, 0)
                split_hi(Unit(UA + AHEAD, 1, t, 4))
                raw_scalar(act, "a", t, 1, Unit(UA, 1, t, 4), kraw, mark("a_qk", t * 2))
                split_hi(Unit(UA + AHEAD, 2, t, 4))
                u = Unit(UA, 2, t, 4)
                if attend:
                    exps(act, "a", t - 1, 1)
                act.wait_ge(gemm_done, u.n + 1)
                wait(act, sem("a_vturn"), t)
                s.activation(vraw[:, :], G[u.bank][:, :], ACT.Copy).then_inc(sem("a_vraw"), 1)
                root_scalar(act, link, "a", t, 0)
                split_hi(Unit(UA + AHEAD, 3, t, 4))
                root_scalar(act, link, "a", t, 1)
                u = Unit(UA, 3, t, 4)
                act.wait_ge(gemm_done, u.n + 1)
                wait(act, sem("a_silu"), t)
                s.activation(zraw[:, :], G[u.bank][:, :], ACT.Copy).then_inc(sem("a_zraw"), 1)
                act.wait_ge(sem("a_zraw"), t + 1)
                silu_scalar_1(act, link, "a", t, zraw[:, :], th[:, :])
                if attend:
                    gated_high(act, "a", t - 1, hi2)
                silu_scalar_2(act, "a", t, th[:, :])
            pair_a(0, False)
            repeated(act, 8, pair_a, link, first=1)
            load_c(7)
            exps(act, "a", 7, 0)
            exps(act, "a", 7, 1)
            gated_high(act, "a", 7, hi2)
            for n in range(8):
                split_next(Unit(UOA, n))

            norm_squares(act, link, "kv", sem("x_a"))
            norm_high(act, "kv")
            split_next(Unit(UKV, 0))
            norm_high(act, "b")
            for n in range(2):
                raw_scalar(act, "bk", 0, n, Unit(UKV, n), [qraw, kraw][n], None)
                split_next(Unit(UKV, n + 1))
                root_scalar(act, link, "bk", 0, n)
            for n in range(2):
                u = Unit(UKV, 2 + n)
                act.wait_ge(gemm_done, u.n + 1)
                s.activation([vraw, zraw][n][:, :], G[u.bank][:, :], ACT.Copy).then_inc(sem("bv_raw"), 1)
                if n == 0:
                    split_next(Unit(UKV, 3))
            for n in range(2):
                act.wait_ge(sem("bk_done"), n + 1)
                src = cbias[:, n, :]
                for half in range(2):
                    for dst in range(2):
                        act.dma_start(kd[dst * DH:(dst + 1) * DH, 2 * n + half, :], src[half * DH:(half + 1) * DH, :]
                                      ).then_inc(sem("kd_here"), 16)
            act.wait_ge(sem("bv_turn"), 2)

            def pair_b(n, u0, u1, ahead, attend):
                split_hi(ahead[0])
                raw_scalar(act, "b", n, 0, u0, qraw, mark("b_q", n))
                if attend:
                    exps_b(act, n - 1, 0, n * 2 - 2)
                root_scalar(act, link, "b", n, 0)
                split_hi(ahead[1])
                if attend:
                    exps_b(act, n - 1, 1, n * 2 - 1)
                act.wait_ge(gemm_done, u1.n + 1)
                wait(act, sem("b_silu"), n)
                s.activation(zraw[:, :], G[u1.bank][:, :], ACT.Copy).then_inc(sem("b_zraw"), 1)
                act.wait_ge(sem("b_zraw"), n + 1)
                silu_scalar_1(act, link, "b", n, zraw[:, :], th[:, :])
                if attend:
                    gated_high(act, "b", n - 1, hi1)
                silu_scalar_2(act, "b", n, th[:, :])

            def group_b(g):
                first = isinstance(g, int) and g == 0
                pair_b(g * 2, Unit(UB, 0, g, 4), Unit(UB, 1, g, 4), (Unit(UB + AHEAD, 0, g, 4), Unit(UB + AHEAD, 1, g, 4)), not first)
                pair_b(g * 2 + 1, Unit(UB, 2, g, 4), Unit(UB, 3, g, 4), (Unit(UB + AHEAD, 2, g, 4), Unit(UB + AHEAD, 3, g, 4)), True)
            group_b(0)
            repeated(act, 4, group_b, link, first=1)
            exps_b(act, 7, 0, 14)
            exps_b(act, 7, 1, 15)
            gated_high(act, "b", 7, hi1)
            for n in range(8):
                split_next(Unit(UOB, n))
            norm_squares(act, link, "mix", sem("x_b"))
            act.wait_ge(sem("mod"), 1)
            norm_high(act, "mix")
            split_next(Unit(UI, 0))

            places = ([(iqT[:, 0, :], 1.0), (iqT[:, 1, :], 1.0), (vraw[:, :], 1.0)] +
                      [(sqT[:, n, :], SA_SCALE) for n in range(2)] + [(skT[:, n, :], 1.0) for n in range(2)] +
                      [(svT[:, n, :], 1.0) for n in range(2)] + [(ca[0], 1.0), (ca[1], 1.0), (cb[:, 0, :], 1.0), (cb[:, 1, :], 1.0)])

            def raw(n):
                u = Unit(UI, n)
                act.wait_ge(gemm_done, u.n + 1)
                if n == 11:
                    act.wait_ge(sem("lo_mix"), KT + since("lo_mix"))
                s.activation(places[n][0], G[u.bank][:, :], ACT.Copy, scale=places[n][1]).then_inc(sem("i_raw"), 1)
                if n < 12:
                    split_next(Unit(UI, n + 1))
            for n in range(3):
                raw(n)
            act.wait_ge(sem("i_raw"), 3)
            for n in range(4):
                act.dma_start(ik4[32 * n:32 * n + 32, :], vraw[0:32, :]).then_inc(sem("ik_here"), 16)
            raw(3)
            for n in range(24):
                q = 1 + n // 8
                act.wait_ge(sem("i_scores"), n + 1)
                wait(act, sem("i_acc"), n - 1)
                s.activation([th, sg][n % 2][:, 0:(q + 1) * P], S[n % 2][:, 0:(q + 1) * P], ACT.Relu,
                             scale=IDX_SCALE).then_inc(sem("i_relu"), 1)
                if n % 5 == 4 and n // 5 < 4:
                    raw(4 + n // 5)
            for n in range(8, 13):
                raw(n)
            for n in range(2):
                act.wait_ge(sem("i_raw"), 13)
                silu_scalar_1(act, link, "cg", n, cb[:, n, :], cth2[:, n, :])
            for n in range(2):
                silu_scalar_2(act, "cg", n, cth2[:, n, :])
            for t in range(2):
                for h in range(2):
                    exps(act, "c", t, h)
                act.wait_ge(sem("c_gated"), t + 1 + since("c_gated"))
                s.activation(hi1[:, 4 + t, :], og[:, :], ACT.Copy).then_inc(sem("c_gated_hi"), 1)

            def decay(t, step):
                act.wait_ge(sem("h_diff"), t * 9 + (step + 1) + since("h_diff"))
                wait(act, sem("h_x"), (t * 9 + (step - 1 if step > 1 else 0)) + since("h_x"))
                s.activation(dd[:, step % 2, :], gf if step == 0 else dd[:, step % 2, :], ACT.Exp).then_inc(sem("h_exp"), 1)
                if step == 0:
                    s.activation(dec[:, :], gf.rearrange("p (c k) -> p c k", c=4)[:, :, P - 1], ACT.Exp).then_inc(sem("h_dec"), 1)

            def head(t, work=True):
                raws = [(qraw, "h_q"), (kraw, "h_k"), (vraw, "h_vturn"), (zraw, "h_silu")]
                steps = [(0, 1), (2, 3, 4), (5, 6, 7), (8,)]
                for j in range(4):
                    if work:
                        for step in steps[j]:
                            decay(t - 1, step)
                    split_hi(Unit(UH + AHEAD, j, t, 4))
                    raw_h(t, j, *raws[j])
                act.wait_ge(sem("h_raw3"), t + 1 + since("h_raw3"))
                silu_scalar_1(act, link, "hq", t, qraw[:, :], th[:, :])
                if work:
                    norm_head(t - 1)
                    gated_h(t - 1)
                silu_scalar_2(act, "hq", t, th[:, :])
                wait(act, sem("h_gated_lo"), t + since("h_gated_lo"))
                link(s.activation(fth[:, :], kraw[:, :], ACT.Abs))
                link(s.activation(fth[:, :], fth[:, :], ACT.Exp, scale=-1.0))
                s.activation(fth[:, :], fth[:, :], ACT.Ln, bias=1.0).then_inc(sem("hf_softplus"), 1)
                act.wait_ge(sem("h_klog"), t + 1 + since("h_klog"))
                s.activation(kn[:, :], fth[:, :], ACT.Exp, scale=-1.0).then_inc(sem("h_k"), 1)
                act.wait_ge(sem("h_q"), t + 1 + since("h_q"))
                silu_scalar_1(act, link, "h", t, zraw[:, :], th[:, :])
                silu_scalar_2(act, "h", t, th[:, :])

            def raw_h(t, j, dst, used):
                u = Unit(UH, j, t, 4)
                act.wait_ge(gemm_done, u.n + 1)
                wait(act, sem(used), t + since(used))
                s.activation(dst[:, :], G[u.bank][:, :], ACT.Copy).then_inc(sem(f"h_raw{j}"), 1)

            def norm_head(t):
                act.wait_ge(sem("h_o"), t + 1 + since("h_o"))
                wait(act, sem("h_normed"), t)
                s.activation(sq[:, 0, :], O[:, :], ACT.Square).then_inc(sem("h_sq"), 1)
                act.wait_ge(sem("h_sum"), t + 1 + since("h_sum"))
                rsqrt_scalar(link, 0, 1.0 / P, sem("h_meansq"), sem("h_root"))

            def gated_h(t):
                act.wait_ge(sem("h_gated"), t + 1 + since("h_gated"))
                s.activation(hi1[:, bass.ds(t, 1), :], og[:, :].unsqueeze(1), ACT.Copy).then_inc(sem("h_gated_hi"), 1)

            def conv_norm():
                for k in range(2):
                    act.wait_ge(sem("conv_centred"), k + 1)
                    s.activation(sq[:, k, :], cacc[:, k, :], ACT.Square).then_inc(sem("conv_sq"), 1)
                act.wait_ge(sem("conv_sqsum"), 1)
                rsqrt_scalar(link, 0, 1.0 / 256, sem("conv_var"), sem("conv_root"))
                for k in range(2):
                    act.wait_ge(sem("conv_z"), k + 1)
                    silu_scalar_1(act, link, "cv", k, cacc[:, k, :], cb[:, k, :])
                    silu_scalar_2(act, "cv", k, cb[:, k, :])
                    act.wait_ge(sem("cv_gated"), k + 1)
                    s.activation(hi1[:, 6 + k, :], cpad[:, k, 0:SEQ], ACT.Copy).then_inc(sem("cv_gated_hi"), 1)
            head(0, False)
            conv_norm()
            repeated(act, 4, head, link, first=1)
            for step in range(9):
                decay(3, step)
            norm_head(3)
            gated_h(3)
            for n in range(8):
                split_next(Unit(UOM, n))
            norm_squares(act, link, "mlp", sem("x_m"))
            norm_high(act, "mlp")

            def quarter(c, ahead=True):
                for n in range(16):
                    if n < 8:
                        u = Unit(UM, n, c, 16)
                        act.wait_ge(gemm_done, u.n + 1)
                        wait(act, sem("f_sq"), c * 8 + (n - 1))
                        s.activation(tmp[:, n % 2, :], G[u.bank][:, :], ACT.Relu).then_inc(sem("f_relu"), 1)
                    if ahead or n < 13:
                        split_hi(Unit(UM + AHEAD, n, c, 16))
                    if 1 <= n < 9:
                        wait(act, sem("f_sq"), c * 8 + n)
                        s.activation(hi1[:, n - 1, :], rms[:, (n - 1) % 2, :], ACT.Copy).then_inc(sem("f_hi"), 1)
            repeated(act, 3, quarter)
            quarter(3, False)
            norm_squares(act, link, "f", sem("x_f"), 24)
            for q in range(NQ):
                for half in range(2):
                    act.wait_ge(sem("y_turned"), 2 * q + half + 1)
                    s.activation(xin[:, q, half * 512:half * 512 + 512], T[half][:, :], ACT.Copy
                                 ).then_inc(sem("y_out"), 1)
                act.wait_ge(sem("y_out"), 2 * q + 2)
                act.dma_start(out[0, q * P:(q + 1) * P, :], xin[:, q, :]).then_inc(sem("o_stored"), 16)

        @block.vector
        def _(dve):
            link = Link(dve, sem("dve_link"))
            cond = vecT[:, VEC["c_2"]:VEC["c_2"] + KT]
            for k in range(KT):
                dve.wait_ge(sem("x_turned"), k + 1)
                v.tensor_copy(xT[:, k, :], T[k % 2][:, :]).then_inc(sem("x_copied"), 1)
            dve.wait_ge(sem("vec_turned"), 1)
            link(v.tensor_copy(vecT[:, :], O[:, 0:N_VEC]), v.tensor_copy(invf[:, :], O[:, 128:129]),
                 v.tensor_copy(tapT[:, :], O[:, 192:254]))
            v.memset(stat[:, 0, 0, 0:1], 0.0).then_inc(sem("vec_there"), 1)
            link(v.tensor_scalar(gains[:, 0:1], gains[:, 0:1], DH ** -0.5, None, ALU.mult),
                 v.tensor_scalar(gains[:, 2:3], gains[:, 2:3], DH ** -0.5, None, ALU.mult))
            norm_vector(dve, link, "a")
            silu_vector_1(dve, "c", 0, cond, cth[:, :])

            dve.wait_ge(sem("pos_here"), 16)
            if True:
                ang, num, t0 = probs[:, 0:SEQ], probsT[:, 0:SEQ], logits[:, 0:SEQ]
                link(v.tensor_copy(t0, posi[:, :]))
                link(v.tensor_scalar(ang, t0, invf[:, 0:1], None, ALU.mult))
                for dst, quarter in ((sinb, 0.0), (cosb, 0.25)):
                    link(v.tensor_scalar(num.bitcast(i32), ang, 1.0 / TWO_PI, quarter, ALU.mult, ALU.add))
                    link(v.tensor_copy(t0, num.bitcast(i32)))
                    for n, part in enumerate(TURN_PARTS):
                        link(v.scalar_tensor_tensor(out=(dst[:, :]), in0=t0, scalar=-part, in1=ang if n == 0 else dst[:, :],
                                                    op0=ALU.mult, op1=ALU.add))
                    link(v.tensor_scalar(dst[:, :], dst[:, :], quarter * TWO_PI, PI_DOWN, ALU.add, ALU.min))
                    link(v.tensor_scalar(dst[:, :], dst[:, :], -PI_DOWN, None, ALU.max))
            v.memset(stat[:, 0, 0, 0:1], 0.0).then_inc(sem("angles"), 1)
            dve.wait_ge(sem("c_sigmoid"), 1)
            v.tensor_tensor(cact[:, :], cond, cth[:, :], ALU.mult).then_inc(sem("c_silu"), 1)
            dve.wait_ge(sem("f_ln"), 1)
            link(v.tensor_scalar(fz[:, 1, :], fz[:, 0, :], 0.0, None, ALU.min))
            link(v.tensor_tensor(fz[:, 2, :], fz[:, 3, :], fz[:, 1, :], ALU.subtract), v.memset(fz[:, 0, :], 1.0))
            v.tensor_tensor_scan(fz[:, 3, :], fz[:, 0, :], fz[:, 2, :], 0.0, ALU.mult, ALU.add
                                 ).then_inc(sem("c_ready"), 1)

            def c_bias(h, q):
                return cbias[:, h, 0:(q + 1) * P]

            def attend_a(t, h):
                if h == 0:
                    dve.wait_ge(sem("c_here"), t * 16 + 16)
                take_logits(dve, "a", t, h, c_bias)
                normalise(dve, link, "a", t, h)
                take_turned(dve, "a", t, h)

            def pair_a(t, attend=True):
                if attend:
                    attend_a(t - 1, 0)
                    attend_a(t - 1, 1)
                normed_vector(dve, link, "a", t, 0, qraw, qn[:, :], 0, mark("a_scores", t * 8), sem("a_qk"))
                normed_vector(dve, link, "a", t, 1, kraw, kn[:, :], 1, mark("a_scores", t * 8), sem("a_qk"))
                if attend:
                    gate_vector(dve, "a", t - 1, None, None, mark("a_o", 2 * t))
                dve.wait_ge(sem("a_vturn"), t + 1)
                v.tensor_copy(vp[:, :, :], T[0][:, :].rearrange("p (q d) -> p q d", q=NQ)).then_inc(sem("a_v"), 1)
                silu_vector_1(dve, "a", t, zraw[:, :], th[:, :])
                if attend:
                    gated_low(dve, "a", t - 1, hi2, lo2)
                silu_vector_2(dve, "a", t, zraw[:, :], th[:, :], mark("a_gated", t))
            pair_a(0, False)
            repeated(dve, 8, pair_a, link, first=1)
            attend_a(7, 0)
            attend_a(7, 1)
            gate_vector(dve, "a", 7, None, None, mark("a_o", 16))
            gated_low(dve, "a", 7, hi2, lo2)
            add_output(dve, "a", lambda n: Unit(UOA, n))

            norm_vector(dve, link, "kv")
            dve.wait_ge(sem("lo_kv"), KT + since("lo_kv"))
            norm_vector(dve, link, "b")
            dve.wait_ge(sem("sines"), 2)
            def rotate(n, which, src, dst, ph, rot_ready, done):
                wait(dve, *rot_ready)
                v.tensor_tensor(tmp2[:, 0, :], N[:, :], sinb[:, :], ALU.mult).then_inc(sem(f"{ph}_turn_taken"), 1)
                link(v.tensor_tensor(tmp2[:, 1, :], src, cosb[:, :], ALU.mult))
                v.tensor_tensor(dst, tmp2[:, 0, :], tmp2[:, 1, :], ALU.add).then_inc(done, 1)

            for n in range(2):
                normed_vector(dve, link, "bk", 0, n, [qraw, kraw][n], tmp[:, n, :], 3, mark("lo_b", KT), sem("bk_normed"))
                rotate(n, 0, tmp[:, n, :], cbias[:, n, :], "bk", mark("bk_turned", n + 1), sem("bk_done"))
            for n in range(2):
                dve.wait_ge(sem("bv_turn"), n + 1)
                v.tensor_copy(vb[:, 2 * n:2 * n + 2, :, :].rearrange("p g q d -> p q g d"),
                              T[0][:, :].rearrange("p (q g d) -> p q g d", q=NQ, g=2)).then_inc(sem("bv_out"), 1)

            def attend_b(t, h, head):
                maxima_b(dve, link, t, h, head)
                normalise_b(dve, link, t, h)
                take_turned_b(dve, t, h)

            def load_group(g, scores_used, o_used):
                wait(dve, sem("b_scores"), scores_used)
                if isinstance(g, int) and g == 0:
                    dve.wait_ge(sem("kd_here"), 16 * 8)
                    dve.wait_ge(sem("bv_out"), 2)
                v.tensor_copy(kg[:, :].unsqueeze(1), kd[:, bass.ds(g, 1), :])
                wait(dve, sem("b_o"), o_used)
                v.tensor_copy(vg.unsqueeze(1), vb[:, bass.ds(g, 1), :, :]).then_inc(sem("b_kg"), 1)

            def pair_b(n, attend, g=None):
                if attend:
                    attend_b(n - 1, 0, n * 2 - 2)
                dve.wait_ge(sem("b_root0"), n + 1)
                rsqrt_vector(link, 0)
                v.scalar_tensor_tensor(out=qraw[:, :], in0=qraw[:, :], scalar=gains[:, 2:3], in1=rinv[:, 0, :],
                                       op0=ALU.mult, op1=ALU.mult).then_inc(sem("b_normed"), 1)
                if attend:
                    attend_b(n - 1, 1, n * 2 - 1)
                wait(dve, sem("b_scores"), n * 2)
                rotate(n, 0, qraw[:, :], qn[:, :], "b", mark("b_turned", n + 1), sem("b_q"))
                silu_vector_1(dve, "b", n, zraw[:, :], th[:, :])
                if attend:
                    gate_vector(dve, "b", n - 1, None, None, mark("b_o", 2 * n))
                    gated_low(dve, "b", n - 1, hi1, lo1)
                silu_vector_2(dve, "b", n, zraw[:, :], th[:, :], mark("b_gated", n))
                if g is not None:
                    load_group(g, n * 2, n * 2)

            def group_b(g):
                first = isinstance(g, int) and g == 0
                pair_b(g * 2, not first, g)
                pair_b(g * 2 + 1, True)
            group_b(0)
            repeated(dve, 4, group_b, link, first=1)
            attend_b(7, 0, 14)
            attend_b(7, 1, 15)
            gate_vector(dve, "b", 7, None, None, mark("b_o", 16))
            gated_low(dve, "b", 7, hi1, lo1)
            add_output(dve, "b", lambda n: Unit(UOB, n))
            dve.wait_ge(sem("ada_done"), 48)
            link(v.tensor_tensor(modT[:, :], T[1][:, 384:432], vecT[:, 0:48], ALU.add))
            link(v.scalar_tensor_tensor(out=gainm[:, 0:8], in0=modT[:, 8:16], scalar=1.0,
                                        in1=vecT[:, VEC["norm_mix_w_2"]:VEC["norm_mix_w_2"] + 8], op0=ALU.add, op1=ALU.mult))
            link(v.scalar_tensor_tensor(out=gainm[:, 8:16], in0=modT[:, 32:40], scalar=1.0,
                                        in1=vecT[:, VEC["norm_mlp_w_2"]:VEC["norm_mlp_w_2"] + 8], op0=ALU.add, op1=ALU.mult))
            v.memset(stat[:, 0, 0, 0:1], 0.0).then_inc(sem("mod"), 1)
            norm_vector(dve, link, "mix")
            dve.wait_ge(sem("iotas"), 1)
            link(v.tensor_tensor(ii, jj, ii, ALU.bitwise_xor))
            v.tensor_copy(jx, ii).then_inc(sem("xor"), 1)
            dve.wait_ge(sem("later"), 1)
            for n in range(7):
                link(v.tensor_scalar(it, jx, float(64 >> n), None, ALU.is_ge))
                link(v.scalar_tensor_tensor(out=level[:, n, :], in0=jx, scalar=float(128 >> n), in1=it, op0=ALU.is_lt,
                                            op1=ALU.mult))
            dve.wait_ge(sem("iw_turned"), 1)
            v.tensor_scalar(iwp[:, :, :], T[0][:, :].rearrange("p (q c) -> p q c", q=NQ)[:, :, 32:40], 8 ** -0.5, None,
                            ALU.mult).then_inc(sem("iw_there"), 1)
            dve.wait_ge(sem("iw_there"), 1)
            v.tensor_copy(sel[:, 0:P], causal)
            for n in range(24):
                q, h = 1 + n // 8, n % 8
                w = (q + 1) * P
                part = sel[:, A_AT[q]:A_AT[q] + w]
                dve.wait_ge(sem("i_relu"), n + 1)
                relu = [th, sg][n % 2][:, 0:w]
                if h == 0:
                    v.tensor_scalar(part, relu, iwp[:, q, h:h + 1], None, ALU.mult).then_inc(sem("i_acc"), 1)
                else:
                    wait(dve, sem("i_acc"), n)
                    v.scalar_tensor_tensor(out=part, in0=relu, scalar=iwp[:, q, h:h + 1], in1=part, op0=ALU.mult,
                                           op1=ALU.add).then_inc(sem("i_acc"), 1)
            for q in range(1, NQ):
                part = sel[:, A_AT[q]:A_AT[q] + (q + 1) * P]
                own = sel[:, A_AT[q] + q * P:A_AT[q] + (q + 1) * P]
                wait(dve, sem("i_acc"), 8 * q)
                link(v.tensor_tensor(own, own, causal, ALU.add))
                for n in range(TOPK // 8):
                    link(v.max(best[:, n % 2, :], part))
                    link(v.match_replace(part, best[:, n % 2, :], part, -HUGE))
                link(v.tensor_scalar(part, part, -HUGE, -NEG, ALU.is_equal, ALU.mult))
                link(v.tensor_scalar(part, part, NEG, None, ALU.add))
                if q == 1:
                    for n in range(2):
                        dve.wait_ge(sem("sv_turned"), n + 1)
                        v.tensor_copy(svp[:, :, n * P:(n + 1) * P], T[0][:, :].rearrange("p (q d) -> p q d", q=NQ)
                                      ).then_inc(sem("sv_out"), 1)
            for n in range(2):
                silu_vector_1(dve, "cg", n, cb[:, n, :], cth2[:, n, :])

            def sel_bias(h, q):
                return sel[:, A_AT[q]:A_AT[q] + (q + 1) * P]
            for t in range(2):
                for h in range(2):
                    take_logits(dve, "c", t, h, sel_bias)
                    normalise(dve, link, "c", t, h)
                    take_turned(dve, "c", t, h)
                dve.wait_ge(sem("c_o"), 2 * t + 2 + since("c_o"))
                if t:
                    wait(dve, sem("c_gated_lo"), t + since("c_gated_lo"))
                v.tensor_copy(og[:, :], O[:, :]).then_inc(sem("c_gated"), 1)
                dve.wait_ge(sem("c_gated_hi"), t + 1 + since("c_gated_hi"))
                v.tensor_tensor(lo1[:, 4 + t, :], og[:, :], hi1[:, 4 + t, :].bitcast(f32), ALU.subtract).then_inc(sem("c_gated_lo"), 1)

            dve.wait_ge(sem("c_gated_lo"), 2 + since("c_gated_lo"))
            dve.wait_ge(sem("cg_sigmoid"), 2)
            link(v.memset(cpad[:, :, 0:PAD], 0.0))
            for k in range(2):
                link(v.tensor_tensor(cpad[:, k, PAD:PAD + SEQ], ca[k], cth2[:, k, :], ALU.mult))
            b0 = VEC["cv_b_2"]
            link(*[v.tensor_scalar(cacc[:, k, :], cpad[:, k, 0:SEQ], tapT[:, k:k + 1], vecT[:, b0 + k:b0 + k + 1],
                                   ALU.mult, ALU.add) for k in range(2)])
            for tap in range(1, 31):
                for k in range(2):
                    ins = v.scalar_tensor_tensor(out=cacc[:, k, :], in0=cpad[:, k, tap:tap + SEQ],
                                                 scalar=tapT[:, 2 * tap + k:2 * tap + k + 1], in1=cacc[:, k, :],
                                                 op0=ALU.mult, op1=ALU.add)
                    if tap < 30:
                        link(ins)
                    else:
                        ins.then_inc(sem("conv"), 1)

            def conv_norm():
                dve.wait_ge(sem("conv_sum"), 1)
                for k in range(2):
                    dve.wait_ge(sem("conv"), k + 1)
                    v.scalar_tensor_tensor(out=cacc[:, k, :], in0=N[:, :], scalar=-1.0 / 256, in1=cacc[:, k, :],
                                           op0=ALU.mult, op1=ALU.add).then_inc(sem("conv_centred"), 1)
                dve.wait_ge(sem("conv_root"), 1)
                rsqrt_vector(link, 0)
                w0, b1 = VEC["cv_ln_w_2"], VEC["cv_ln_b_2"]
                for k in range(2):
                    link(v.scalar_tensor_tensor(out=cacc[:, k, :], in0=cacc[:, k, :], scalar=vecT[:, w0 + k:w0 + k + 1],
                                                in1=rinv[:, 0, :], op0=ALU.mult, op1=ALU.mult))
                    v.tensor_scalar(cacc[:, k, :], cacc[:, k, :], vecT[:, b1 + k:b1 + k + 1], None, ALU.add
                                    ).then_inc(sem("conv_z"), 1)
                for k in range(2):
                    dve.wait_ge(sem("conv_z"), k + 1)
                    silu_vector_1(dve, "cv", k, cacc[:, k, :], cb[:, k, :])
                    dve.wait_ge(sem("cv_sigmoid"), k + 1 + since("cv_sigmoid"))
                    v.tensor_tensor(cpad[:, k, 0:SEQ], cacc[:, k, :], cb[:, k, :], ALU.mult).then_inc(sem("cv_gated"), 1)
                    dve.wait_ge(sem("cv_gated_hi"), k + 1)
                    v.tensor_tensor(lo1[:, 6 + k, :], cpad[:, k, 0:SEQ], hi1[:, 6 + k, :].bitcast(f32), ALU.subtract
                                    ).then_inc(sem("cv_gated_lo"), 1)

            q4 = lambda x: x.rearrange("p (c k) -> p c k", c=4)

            def work_1(t):
                dve.wait_ge(sem("h_k"), t + 1 + since("h_k"))
                dve.wait_ge(sem("h_q"), t + 1 + since("h_q"))
                for step in range(2):
                    dve.wait_ge(sem("h_exp"), t * 9 + (step + 1) + since("h_exp"))
                    wait(dve, sem("h_o"), t + since("h_o"))
                    v.tensor_tensor([qe, ke][step], dd[:, step, :], [qn, kn][step][:, :], ALU.mult).then_inc(sem("h_x"), 1)
                dve.wait_ge(sem("h_keT"), t + 1)
                v.tensor_copy(keT[:, :, :], T[1][:, 0:384].rearrange("p (c k) -> p c k", c=3)).then_inc(sem("h_keT_out"), 1)
                operands(t, 0)
                operands(t, 1)
                dve.wait_ge(sem("h_update"), t + 1)
                dve.wait_ge(sem("h_dec"), t + 1)
                v.tensor_copy(state[:, 0, :], T[0][:, 0:P]).then_inc(sem("h_state"), 1)
                for c in range(1, 3):
                    wait(dve, sem("h_state"), t * 3 + c + since("h_state"))
                    v.scalar_tensor_tensor(out=state[:, c, :], in0=state[:, c - 1, :], scalar=dec[:, c:c + 1],
                                           in1=T[0][:, c * P:(c + 1) * P], op0=ALU.mult, op1=ALU.add).then_inc(sem("h_state"), 1)

            def operands(t, lv):
                m = (P // 2) >> lv
                split = lambda x: x.rearrange("p (n a m) -> p n a m", a=2, m=m)
                e, x = split(dd[:, lv % 2, :]), split(xx[:, lv % 2, :])
                dve.wait_ge(sem("h_exp"), t * 9 + (lv + 3) + since("h_exp"))
                wait(dve, sem("h_products"), (t * 8 + (lv - 1 if lv > 1 else 0)) + since("h_products"))
                v.tensor_tensor(x[:, :, 0, :], e[:, :, 0, :], split(kn[:, :])[:, :, 0, :], ALU.mult)
                v.tensor_tensor(x[:, :, 1, :], e[:, :, 1, :], split(qn[:, :])[:, :, 1, :], ALU.mult).then_inc(sem("h_x"), 1)

            def joined(t, p):
                dve.wait_ge(sem("h_products"), t * 8 + (p + 1) + since("h_products"))
                mask = ident[:, :].bitcast(i32) if p == 7 else level[:, p, :]
                wait(dve, sem("h_aT"), t * 8 + p + since("h_aT"))
                v.memset(stat[:, 0, 0, 0:1], 0.0)
                v.copy_predicated(aT[:, :, :], mask.unsqueeze(1).broadcast_to((P, NQ, P)), q4(S[p % 2][:, :])
                                  ).then_inc(sem("h_aT"), 1)

            def work_2(t):
                for lv in range(2, 7):
                    joined(t, lv - 2)
                    operands(t, lv)
                for p in range(5, 8):
                    joined(t, p)

            def work_3(t):
                dve.wait_ge(sem("h_root"), t + 1 + since("h_root"))
                rsqrt_vector(link, 0)
                v.scalar_tensor_tensor(out=og[:, :], in0=O[:, :], scalar=vecT[:, bass.ds(VEC["hg_onorm_w_2"] + t, 1)],
                                       in1=rinv[:, 0, :], op0=ALU.mult, op1=ALU.mult).then_inc(sem("h_normed"), 1)
                dve.wait_ge(sem("h_normed"), t + 1)
                dve.wait_ge(sem("h_silu"), t + 1 + since("h_silu"))
                v.tensor_tensor(og[:, :], og[:, :], sg[:, :], ALU.mult).then_inc(sem("h_gated"), 1)
                dve.wait_ge(sem("h_gated_hi"), t + 1 + since("h_gated_hi"))
                v.tensor_tensor(lo1[:, bass.ds(t, 1), :], og[:, :].unsqueeze(1), hi1[:, bass.ds(t, 1), :].bitcast(f32),
                                ALU.subtract).then_inc(sem("h_gated_lo"), 1)

            def prepare(t):
                dve.wait_ge(sem("h_vturn"), t + 1 + since("h_vturn"))
                v.tensor_copy(vp[:, :, :], q4(T[0][:, :])).then_inc(sem("h_v"), 1)
                silu_vector_1(dve, "hq", t, qraw[:, :], th[:, :])
                dve.wait_ge(sem("hq_sigmoid"), t + 1 + since("hq_sigmoid"))
                v.scalar_tensor_tensor(out=qn[:, :], in0=qraw[:, :], scalar=P ** -0.5, in1=th[:, :], op0=ALU.mult,
                                       op1=ALU.mult).then_inc(sem("h_q"), 1)
                dve.wait_ge(sem("hf_softplus"), t + 1)
                link(v.scalar_tensor_tensor(out=gf, in0=kraw[:, :], scalar=0.0, in1=fth[:, :], op0=ALU.min,
                                            op1=ALU.subtract))
                v.scalar_tensor_tensor(out=fth[:, :], in0=kraw[:, :], scalar=0.0, in1=fth[:, :], op0=ALU.max,
                                       op1=ALU.add).then_inc(sem("h_klog"), 1)
                link(v.tensor_scalar(gf, gf, LN_TINY, None, ALU.max))
                v.tensor_tensor_scan(gc, restart, gf, 0.0, ALU.mult, ALU.add).then_inc(sem("h_g"), 1)
                silu_vector_1(dve, "h", t, zraw[:, :], th[:, :])
                silu_vector_2(dve, "h", t, zraw[:, :], th[:, :], mark("h_gated", t))

            def head(t, work=True):
                if work:
                    work_1(t - 1)
                    work_2(t - 1)
                    work_3(t - 1)
                prepare(t)
            head(0, False)
            conv_norm()
            dve.wait_ge(sem("cv_gated_lo"), 2)
            link(v.memset(scr[:, 512:1024], 0.0))
            repeated(dve, 4, head, link, first=1)
            work_1(3)
            work_2(3)
            work_3(3)
            add_output(dve, "m", lambda n: Unit(UOM, n), 16)
            norm_vector(dve, link, "mlp")

            def quarter(c):
                for n in range(9):
                    if n < 8:
                        u = Unit(UM, n, c, 16)
                        dve.wait_ge(sem("f_relu"), c * 8 + (n + 1))
                        wait(dve, sem("f_lo"), c * 8 + (n - 1))
                        v.tensor_tensor(rms[:, n % 2, :], tmp[:, n % 2, :], tmp[:, n % 2, :], ALU.mult
                                        ).then_inc(sem("f_sq"), 1)
                    if n:
                        wait(dve, sem("f_hi"), c * 8 + n)
                        v.tensor_tensor(lo1[:, n - 1, :], rms[:, (n - 1) % 2, :], hi1[:, n - 1, :].bitcast(f32),
                                        ALU.subtract).then_inc(sem("f_lo"), 1)
                add_output(dve, "f", lambda n: Unit(UM, 8 + n, c, 16), 40)
            repeated(dve, 4, quarter)
            norm_vector(dve, link, "f")


def kernel(**inputs):
    import numpy as np
    import concourse.bacc as bacc
    from concourse.bass_utils import run_bass_kernel_spmd as run

    nc = bacc.Bacc("TRN2", target_bir_lowering=False, num_devices=1)
    arrays, aps = {}, {}
    for name, value in inputs.items():
        value = np.ascontiguousarray(value)
        arrays[name + "_dram"] = value
        aps[name] = nc.dram_tensor(name + "_dram", value.shape, mybir.dt.from_np(value.dtype), kind="ExternalInput").ap()
    out = nc.dram_tensor("out_dram", (1, SEQ, D), mybir.dt.float32, kind="ExternalOutput").ap()
    build(nc, aps, out)
    r = run(nc, [arrays], core_ids=[0])
    return r.results[0]["out_dram"]
```

```python
import math

import numpy as np

import concourse.bass as bass
from concourse import mybir
from contextlib import ExitStack

D = 1024
SEQ = 512
P = 128
KT = D // P
NQ = SEQ // P
DH = 64
WIDTH_A = 1024
EPS = 1e-6
SLOTS = 4
AHEAD = 3
NEG = -1e30
HUGE = 3e38

VEC_ROWS = [("ada_b_2", 48), ("norm_a_g", 8), ("kv_norm_g", 8), ("norm_b_g", 8), ("norm_mix_w_2", 8),
            ("norm_mlp_w_2", 8), ("final_norm_w_2", 8), ("c_2", 8), ("hg_onorm_w_2", 4), ("cv_b_2", 2),
            ("cv_ln_w_2", 2), ("cv_ln_b_2", 2)]
VEC = {}
_at = 0
for _name, _rows in VEC_ROWS:
    VEC[_name] = _at
    _at += _rows
N_VEC = _at

ROPE = [np.float32(500000.0) ** np.float32(-2.0 * r / 16) for r in range(8)]
TWO_PI = 2 * math.pi
_second = math.floor((TWO_PI - 6.28125) * 2 ** 20) / 2 ** 20
TURN_PARTS = [6.28125, _second, TWO_PI - 6.28125 - _second]
PI_DOWN = 3.1415925

TOPK = 128
SA_SCALE, IDX_SCALE = 64 ** -0.5, 32 ** -0.5
LN_TINY = math.log(1e-30)
I_COLUMNS = [2816, 2944, 3072, 3112, 3240, 3368, 3496, 2048, 2176, 2304, 2432, 2560, 2688]
I_AFTER = {1: range(4, 8), 2: range(8, 13), 3: ()}
CONV_CUTS = [0, 3, 6, 9, 12, 15, 23, 27, 31, 35, 39, 45, 51, 56, 60]


class Unit:

    def __init__(self, base, j=0, i=0, per=0):
        self.n = i * per + (base + j)
        self.slot = (base + j) % SLOTS
        self.of_slot = i * (per // SLOTS) + (base + j) // SLOTS
        self.of_pair = i * (per // 2) + (base + j) // 2
        self.bank = (base + j) % 2
        self.of_bank = i * (per // 2) + (base + j) // 2


def wait(eng, sem, value):
    if not isinstance(value, int) or value > 0:
        eng.wait_ge(sem, value)


AFTER = {f"c_{x}": (f"a_{x}", 64) for x in ("scores", "logits", "exps", "pT", "pT_out", "probs")}
AFTER.update({f"c_{x}": (f"a_{x}", last) for x, last in (("o", 16), ("gated", 8), ("gated_hi", 8), ("gated_lo", 8))})
AFTER.update({f"h_{x}": (f"b_{x}", 8) for x in ("silu", "softplus", "logsig", "sigmoid", "gated", "gated_hi", "gated_lo",
                                                "raw0", "q")})
AFTER.update({f"hq_{x}": (f"a_{x}", 8) for x in ("softplus", "logsig", "sigmoid")})
AFTER.update({f"cv_{x}": (f"cg_{x}", 2) for x in ("softplus", "logsig", "sigmoid")})
AFTER.update({"h_raw1": ("a_raw1", 8), "h_raw2": ("a_vraw", 8), "h_raw3": ("b_zraw", 8), "h_vturn": ("a_vturn", 8),
              "h_v": ("a_v", 8), "h_root": ("b_root0", 8), "h_sq": ("b_sq0", 8), "h_sum": ("b_sum0", 8),
              "h_products": ("b_scores", 16), "h_aT": ("b_exps", 64), "h_x": ("b_probs", 64), "h_diff": ("b_pT", 32),
              "h_exp": ("b_pT_out", 32), "h_o": ("b_o", 16), "h_k": ("b_normed", 8), "h_state": ("b_negmax", 16),
              "h_meansq": ("b_sum0_taken", 8), "h_g": ("b_turned", 8), "h_klog": ("b_turn_taken", 8),
              "h_dec": ("a_qk", 16), "h_update": ("a_silu", 8)})
for _n, _key in enumerate(("a", "kv", "mix", "mlp", "f")):
    AFTER.update({f"{x}_{_key}": (f"norm_{x}", per * _n) for x, per in (("sq", 8), ("sums", 8), ("total", 1), ("meansq", 1),
                                                                    ("root", 1))})
for _n, _key in enumerate(("a", "kv", "b", "mix", "mlp", "f")):
    AFTER.update({f"{x}_{_key}": (f"norm_{x}", 8 * _n) for x in ("h32", "hhi", "lo")})


class Link:

    def __init__(self, eng, sem):
        self.eng, self.sem, self.base, self.here, self.i, self.per = eng, sem, 0, 0, 0, 0

    def __call__(self, *instructions):
        for ins in instructions:
            ins.then_inc(self.sem, 1)
            self.here += 1
        self.eng.wait_ge(self.sem, self.i * self.per + (self.base + self.here))


def repeated(eng, turns, body, link=None, first=0):
    start = link.here if link else 0
    body(first)
    if turns - first > 1:
        if link:
            per = link.here - start
            link.base += link.here - per
            link.here = 0
            link.per = per
            link.base -= per * first
            with eng.Fori(first + 1, turns) as i:
                link.i = i
                body(i)
                assert link.here == per or per == 0, (link.here, per)
            link.base += per * (turns - 1) + per
            link.here = 0
            link.i = link.per = 0
        else:
            with eng.Fori(first + 1, turns) as i:
                body(i)


def build(nc, a, out):
    f32, f32r, bf16, i32 = mybir.dt.float32, mybir.dt.float32r, mybir.dt.bfloat16, mybir.dt.int32
    ALU, ACT, AX = mybir.AluOpType, mybir.ActivationFunctionType, mybir.AxisListType
    ctx = ExitStack()
    with ctx:
        def sb(name, shape, dt=f32):
            return ctx.enter_context(nc.sbuf_tensor(name, shape, dt))

        sems = {}

        def sem(name):
            counter, base = AFTER.get(name, (name, 0))
            if counter not in sems:
                sems[counter] = ctx.enter_context(nc.semaphore(counter))
            return sems[counter]

        def since(name):
            return AFTER.get(name, (name, 0))[1]

        def mark(name, count):
            return sem(name), count + since(name)

        xT = sb("xT", [P, KT, SEQ])
        hi1, lo1 = sb("hi1", [P, KT, SEQ], f32r), sb("lo1", [P, KT, SEQ], f32r)
        hi2, lo2 = sb("hi2", [P, KT, SEQ], f32r), sb("lo2", [P, KT, SEQ], f32r)
        w32 = sb("w32", [P, 2, KT, P])
        wH, wL = sb("wH", [P, SLOTS, KT, P], f32r), sb("wL", [P, SLOTS, KT, P], f32r)
        adaw = sb("adaw", [P, 2, KT, P])
        ident = sb("ident", [P, P])
        identb = sb("identb", [P, P], bf16)
        band = sb("band", [P, 2, P], bf16)
        causal = band[:, 1, :]
        ones = sb("ones", [P, P])
        pair1 = sb("pair1", [P, P])
        turnm = sb("turnm", [P, P])
        epsc = sb("epsc", [P, 1])
        vecs = sb("vecs", [N_VEC, P])
        vecT = sb("vecT", [P, N_VEC])
        gains = sb("gains", [P, 4])
        bfg = sb("bfg", [16, 1])
        sinkb = sb("sinkb", [P, 16])
        cs = sb("cs", [P, 2, SEQ])
        cosb, sinb = cs[:, 0, :], cs[:, 1, :]
        scr = sb("scr", [P, 4096])
        xin = scr[:, :].rearrange("p (q d) -> p q d", q=NQ)
        logits = scr[:, 0:1280]
        probs = scr[:, 1280:2560]
        probsT = scr[:, 2560:3840]
        sq = sb("sq", [P, 2, SEQ])
        rms = sb("rms", [P, 2, SEQ])
        rinv = sb("rinv", [P, 2, SEQ])
        tmp = sb("tmp", [P, 2, SEQ])
        qraw, kraw, vraw = sb("qraw", [P, SEQ]), sb("kraw", [P, SEQ]), sb("vraw", [P, SEQ])
        zraw, th = sb("zraw", [P, SEQ]), sb("th", [P, SEQ])
        qkv = sb("qkv", [P, 3 * SEQ])
        qn, kn = qkv[:, 0:SEQ], qkv[:, SEQ:2 * SEQ]
        vp = qkv[:, 2 * SEQ:3 * SEQ].rearrange("p (q c) -> p q c", q=NQ)
        sg = sb("sg", [P, SEQ])
        og = sb("og", [P, SEQ])
        cbias = sb("cbias", [P, 2, SEQ])
        stat = sb("stat", [P, 2, 8, 4])
        kd = sb("kd", [P, 4, SEQ])
        fz = kd[0:16, :, :]
        vb = sb("vb", [P, 4, NQ, DH])
        kg, vg = kn, vp[:, :, 0:DH]
        c_dram = nc.dram_tensor("c_dram", [16, SEQ], f32).ap()
        row = sb("row", [1, P])
        modT = sb("modT", [P, 48])
        gainm = sb("gainm", [P, 16])
        cact, cth = sb("cact", [P, KT]), sb("cth", [P, KT])
        taps = sb("taps", [62, P])
        tapT = sb("tapT", [P, 62])
        iqT = cs
        ik4 = qraw
        iwp = sb("iwp", [P, NQ, 8])
        best = sb("best", [P, 2, 8])
        flat = adaw[:, :, :, :].rearrange("p a k n -> p (a k n)")
        sel = flat[:, 0:1280]
        restart = flat[:, 1280:1792]
        sqT, skT, svT = cbias, kd[:, 0:2, :], kd[:, 2:4, :]
        svp = vb[:, :, :, :].rearrange("p a b c -> p (a b c)").rearrange("p (q d) -> p q d", q=NQ)
        ca, cb, cth2 = [rms[:, 1, :], rinv[:, 1, :]], tmp, sq
        PAD = 30
        cpad = qkv[:, 0:2 * (PAD + SEQ)].rearrange("p (c s) -> p c s", c=2)
        cacc, term = cb, ca
        gc, gf = cbias[:, 0, :], cbias[:, 1, :]
        dd, xx = kd[:, 0:2, :], kd[:, 2:4, :]
        qe, ke = cs[:, 0, :], cs[:, 1, :]
        keT = scr[:, 0:384].rearrange("p (c k) -> p c k", c=3)
        aT = scr[:, 512:1024].rearrange("p (c k) -> p c k", c=4)
        state = scr[:, 1024:1408].rearrange("p (c k) -> p c k", c=3)
        dec = sb("dec", [P, 4])
        jx = flat[:, 1792:1920]
        jj, ii, it = jx.bitcast(i32), flat[:, 1920:2048].bitcast(i32), flat[:, 1920:2048]
        level = sb("level", [P, 7, P], mybir.dt.uint8)
        invf = sb("invf", [P, 1])
        posi = vb[:, 0:2, :, :].rearrange("p a b c -> p (a b c)").bitcast(i32)
        tmp2 = scr[:, 0:2 * SEQ].rearrange("p (a s) -> p a s", a=2)

        G = [ctx.enter_context(nc.psum_tensor(f"G{n}", [P, SEQ], f32)) for n in range(2)]
        S = [ctx.enter_context(nc.psum_tensor(f"S{n}", [P, SEQ], f32)) for n in range(2)]
        T = [ctx.enter_context(nc.psum_tensor(f"T{n}", [P, SEQ], f32)) for n in range(2)]
        O = ctx.enter_context(nc.psum_tensor("O", [P, SEQ], f32))
        N = ctx.enter_context(nc.psum_tensor("N", [P, SEQ], f32))

        w_here = [sem(f"w_here{n}") for n in range(2)]
        w_hi, w_lo, gemm_done = sem("w_hi"), sem("w_lo"), sem("gemm_done")

        UA, UOA, UKV, UB, UOB, UI, UH, UOM, UM = 1, 33, 41, 45, 61, 69, 82, 98, 106
        NU = UM + 4 * 16

        def cols(w, c):
            return w[0, :, bass.ds(c, P)].rearrange("(k p) n -> p k n", p=P)

        block = ctx.enter_context(nc.Block())

        A_AT = [0, P, 3 * P, 6 * P]
        AT_AT = [0, 512, 896, 1152]
        B_AT = [0, P, 3 * P, 5 * P]
        B_W = [P, 2 * P, 2 * P, 2 * P]

        @block.sync
        def _(sp):
            sp.dma_start(xin, a["x"][0].rearrange("(q p) d -> p q d", p=P)).then_inc(sem("x_here"), 16)
            for name, rows in VEC_ROWS:
                t = a[name]
                flat = t.rearrange("(r p) -> r p", p=P) if len(t.shape) == 1 else t.rearrange("a (r p) -> (a r) p", p=P)
                sp.dma_start(vecs[VEC[name]:VEC[name] + rows, :], flat).then_inc(sem("vec_here"), 16)
            for n, name in enumerate(["qnorm_a_g", "knorm_a_g", "qnorm_b_g", "knorm_b_g"]):
                t = a[name]
                col = t.rearrange("(p o) -> p o", o=1) if len(t.shape) == 1 else t.rearrange("o p -> p o")
                for half in range(2):
                    sp.dma_start(gains[half * DH:(half + 1) * DH, n:n + 1], col).then_inc(sem("vec_here"), 16)
            sp.dma_start(bfg[:, :], a["b_forget"].rearrange("o p -> p o")).then_inc(sem("vec_here"), 16)
            sp.dma_start(taps[:, :], a["cv_w_2"].rearrange("o t (c p) -> (o t c) p", p=P)).then_inc(sem("vec_here"), 16)
            sp.dma_start(sinkb[:, :], a["sinks"][0:1, :].partition_broadcast(P)).then_inc(sem("vec_here"), 16)
            sp.dma_start(posi[:, :], a["positions"].rearrange("(a s) -> a s", a=1).partition_broadcast(P)
                         ).then_inc(sem("pos_here"), 16)

            def load_unit(u, src):
                wait(sp, w_lo, u.n - 1)
                sp.dma_start(w32[:, u.slot % 2], src).then_inc(w_here[u.slot % 2], 16)

            def load_ada(e, slot):
                wait(sp, sem("ada_done"), e - 1)
                sp.dma_start(adaw[:, slot], cols(a["ada_w_2"], e * P)).then_inc(sem(f"ada_here{slot}"), 16)

            def ada_two(e):
                load_ada(e, 0)
                load_ada(e + 1, 1)

            wa, wb = a["w_in_a"], a["w_in_b"]
            load_unit(Unit(0), cols(wa, 3 * WIDTH_A))

            def pair_a(t):
                for j, c in enumerate([0, WIDTH_A, 2 * WIDTH_A, 3 * WIDTH_A + 16]):
                    load_unit(Unit(UA, j, t, 4), cols(wa, t * P + c))
                    if j in (1, 3) and not (isinstance(t, int) and t == 0):
                        ada_two(4 * t - (4 if j == 1 else 2))
            pair_a(0)
            repeated(sp, 8, pair_a, first=1)
            for n in range(8):
                load_unit(Unit(UOA, n), cols(a["w_out_a"], n * P))
                if n in (0, 3):
                    ada_two(28 if n == 0 else 30)
            wkv = a["w_kv"].rearrange("(o k) n -> o k n", o=1)
            for n in range(4):
                load_unit(Unit(UKV, n), cols(wkv, n * P))

            def group_b(g):
                for p in range(2):
                    for j, c in enumerate([0, D]):
                        load_unit(Unit(UB, 2 * p + j, g, 4), cols(wb, g * (2 * P) + (p * P + c)))
                        if j == 0 and not (isinstance(g, int) and g == 0):
                            ada_two(g * 4 + (28 + 2 * p))
            group_b(0)
            repeated(sp, 4, group_b, first=1)
            for n in range(8):
                load_unit(Unit(UOB, n), cols(a["w_out_b"], n * P))
                if n in (0, 2):
                    ada_two(44 + n)
            wi = a["w_in_2"]
            for n, c in enumerate(I_COLUMNS):
                load_unit(Unit(UI, n), cols(wi, c))

            def head(t):
                for j, c in enumerate((1, 0, 2, 3)):
                    load_unit(Unit(UH, j, t, 4), cols(wi, t * P + 512 * c))
            for t in range(4):
                head(t)
            for n in range(8):
                load_unit(Unit(UOM, n), cols(a["w_out_2"], n * P))
            def quarter(c):
                for n in range(8):
                    load_unit(Unit(UM, n, c, 16), cols(a["mlp_w1_2"], c * D + n * P))
                for n in range(8):
                    load_unit(Unit(UM, 8 + n, c, 16), a["mlp_w2_2"][0, bass.ds(c * D, D), n * P:(n + 1) * P]
                              .rearrange("(k p) n -> p k n", p=P))
            repeated(sp, 4, quarter)
            sp.wait_ge(sem("o_stored"), 16 * NQ)

        @block.gpsimd
        def _(pool):
            g = nc.gpsimd
            link = Link(pool, sem("pool_link"))
            g.memset(ones[:, :], 1.0).then_inc(sem("const"), 1)
            g.memset(epsc[:, :], EPS).then_inc(sem("const"), 1)
            link(g.memset(ident[:, :], 0.0), g.memset(band[:, :, :], 0.0),
                 g.memset(pair1[:, :], 0.0), g.memset(turnm[:, :], 0.0), g.memset(row[:, :], 0.0))
            turn3 = turnm[:, :].rearrange("p (h r) -> p h r", h=2)
            link(g.affine_select(out=ident[:, :], in_=ident[:, :], compare_op=ALU.not_equal, fill=1.0, base=0,
                                 pattern=[[-1, P]], channel_multiplier=1),
                 g.affine_select(out=band[:, 1, :], in_=band[:, 1, :], compare_op=ALU.is_ge, fill=NEG, base=0,
                                 pattern=[[-1, P]], channel_multiplier=1),
                 g.affine_select(out=band[:, 0, :], in_=band[:, 0, :], compare_op=ALU.is_gt, fill=NEG, base=0,
                                 pattern=[[1, P]], channel_multiplier=-1),
                 g.affine_select(out=turn3[:, :, 0:8], in_=turn3[:, :, 0:8], compare_op=ALU.not_equal, fill=-1.0,
                                 base=-8, pattern=[[-DH, 2], [-1, 8]], channel_multiplier=1),
                 g.affine_select(out=turn3[:, :, 8:16], in_=turn3[:, :, 8:16], compare_op=ALU.not_equal, fill=1.0,
                                 base=0, pattern=[[-DH, 2], [-1, 8]], channel_multiplier=1))
            link(g.memset(pair1[0:DH, 0:DH], 1.0))
            link(g.memset(pair1[DH:P, DH:P], 1.0))
            freq = row[:, :].rearrange("o (h r) -> o h r", h=2)
            for r in range(16):
                last = g.memset(freq[:, :, r:r + 1], float(ROPE[r % 8]))
            link(last)
            g.tensor_copy(identb[:, :], ident[:, :]).then_inc(sem("const"), 1)

            def split_lo(u):
                pool.wait_ge(w_hi, u.n + 1)
                wait(pool, gemm_done, u.n - (SLOTS - 1))
                g.tensor_tensor(wL[:, u.slot], w32[:, u.slot % 2], wH[:, u.slot].bitcast(f32),
                                ALU.subtract).then_inc(w_lo, 1)

            def split_next(u):
                if u.n + AHEAD < NU:
                    split_lo(Unit(u.n + AHEAD))
            for n in range(AHEAD):
                split_lo(Unit(n))
            split_next(Unit(0))

            def fold_two(e, of_slot):
                for slot in range(2):
                    pool.wait_ge(sem(f"ada_here{slot}"), of_slot * 16 + 16)
                    w = adaw[:, slot]
                    link(g.tensor_tensor(w, w, cact[:, :].unsqueeze(2).broadcast_to((P, KT, P)), ALU.mult))
                    link(g.tensor_tensor(w[:, 0:4, :], w[:, 0:4, :], w[:, 4:8, :], ALU.add))
                    link(g.tensor_tensor(w[:, 0:2, :], w[:, 0:2, :], w[:, 2:4, :], ALU.add))
                    g.tensor_tensor(w[:, 0, :], w[:, 0, :], w[:, 1, :], ALU.add).then_inc(sem("ada_folded"), 1)

            def pair(t):
                for j in range(4):
                    split_lo(Unit(UA + AHEAD, j, t, 4))
                    if j == 1 and isinstance(t, int) and t == 0:
                        pool.wait_ge(sem("c_silu"), 1)
                    if j % 2:
                        fold_two(4 * t + (j - 1), 2 * t + j // 2)
            repeated(pool, 8, pair, link)
            for n in range(8):
                split_next(Unit(UOA, n))
            for n in range(4):
                split_next(Unit(UKV, n))

            def group(t):
                for j in range(4):
                    split_lo(Unit(UB + AHEAD, j, t, 4))
                    if j % 2:
                        fold_two(4 * t + (32 + j - 1), 2 * t + (16 + j // 2))
            repeated(pool, 4, group, link)
            for n in range(8):
                split_next(Unit(UOB, n))
            pool.wait_ge(sem("ada_done"), 48)
            link(g.iota(jj, pattern=[[0, P]], base=0, channel_multiplier=1),
                 g.iota(ii, pattern=[[1, P]], base=0, channel_multiplier=0),
                 g.memset(restart, 1.0))
            g.memset(restart.rearrange("p (c k) -> p c k", k=64)[:, :, 0:1], 0.0).then_inc(sem("iotas"), 1)
            for n in range(3):
                split_next(Unit(UI, n))
            pool.wait_ge(sem("xor"), 1)
            g.affine_select(out=jx, in_=jx, compare_op=ALU.is_gt, fill=0.0, base=0, pattern=[[1, P]],
                            channel_multiplier=-1).then_inc(sem("later"), 1)
            for n in range(3, 7):
                split_next(Unit(UI, n))
            for n in range(2):
                pool.wait_ge(sem("cg_softplus"), n + 1)
                link(g.tensor_scalar(cpad[:, n, PAD:PAD + SEQ], cb[:, n, :], 0.0, None, ALU.min))
                g.tensor_tensor(cth2[:, n, :], cpad[:, n, PAD:PAD + SEQ], cth2[:, n, :], ALU.subtract
                                ).then_inc(sem("cg_logsig"), 1)
            split_next(Unit(UI, 7))
            pool.wait_ge(sem("cg_sigmoid"), 2)
            link(g.memset(cpad[:, :, 0:PAD], 0.0))
            for k in range(2):
                g.tensor_tensor(cpad[:, k, PAD:PAD + SEQ], ca[k], cth2[:, k, :], ALU.mult).then_inc(sem("conv_in"), 1)

            def add_terms(first, last_):
                for n in range(first, last_):
                    pool.wait_ge(sem("conv_term"), n + 3)
                    wait(pool, sem("conv_added"), n - 1)
                    g.tensor_tensor(cacc[:, n % 2, :], cacc[:, n % 2, :], term[n % 2], ALU.add
                                    ).then_inc(sem("conv_added"), 1)
            for n in range(8, 13):
                split_next(Unit(UI, n))
                add_terms(CONV_CUTS[n - 8], CONV_CUTS[n - 7])
            add_terms(CONV_CUTS[5], CONV_CUTS[6])

            def differences(t, steps):
                for step in steps:
                    if step == 0:
                        pool.wait_ge(sem("h_g"), t + 1 + since("h_g"))
                        half = lambda x: x.rearrange("p (c a k) -> p c a k", c=4, a=2)
                        g.tensor_tensor(half(gf)[:, :, 1, :], half(gc)[:, :, 1, :],
                                        half(gc)[:, :, 0, 63:64].broadcast_to((P, 4, 64)), ALU.add)
                        g.tensor_copy(half(gf)[:, :, 0, :], half(gc)[:, :, 0, :]).then_inc(sem("h_diff"), 1)
                        continue
                    wait(pool, sem("h_x"), (t * 9 + (step - 1 if step > 1 else 0)) + since("h_x"))
                    if step == 1:
                        pool.wait_ge(sem("h_diff"), t * 9 + 1 + since("h_diff"))
                        whole = lambda x: x.rearrange("p (c k) -> p c k", c=4)
                        g.tensor_tensor(whole(dd[:, 1, :]), whole(gf)[:, :, P - 1:P].broadcast_to((P, 4, P)), whole(gf),
                                        ALU.subtract).then_inc(sem("h_diff"), 1)
                        continue
                    m = (P // 2) >> (step - 2)
                    half = lambda x: x.rearrange("p (n a m) -> p n a m", a=2, m=m)
                    d, c = half(dd[:, step % 2, :]), half(gc)
                    mid = c[:, :, 0, m - 1:m].broadcast_to((P, SEQ // (2 * m), m))
                    g.tensor_tensor(d[:, :, 0, :], mid, c[:, :, 0, :], ALU.subtract)
                    if m == 64:
                        g.tensor_copy(d[:, :, 1, :], c[:, :, 1, :]).then_inc(sem("h_diff"), 1)
                    else:
                        g.tensor_tensor(d[:, :, 1, :], c[:, :, 1, :], mid, ALU.subtract).then_inc(sem("h_diff"), 1)

            def head(t, work=True):
                for j in range(4):
                    if work and j < 3:
                        differences(t - 1, range(max(3 * j, 2), 3 * j + 3))
                    split_lo(Unit(UH + AHEAD, j, t, 4))
                    if not work:
                        add_terms(CONV_CUTS[j + 6], CONV_CUTS[j + 7])
                if not work:
                    add_terms(CONV_CUTS[10], 60)
                differences(t, (0, 1))
            head(0, False)
            repeated(pool, 4, head, first=1)
            differences(3, range(2, 9))
            for n in range(8):
                split_next(Unit(UOM, n))
            def quarter(c, n_units=16):
                for n in range(n_units):
                    split_lo(Unit(UM + AHEAD, n, c, 16))
            repeated(pool, 3, quarter)
            quarter(3, 13)

        mm = nc.tensor.matmul
        v, s = nc.vector, nc.scalar

        def rsqrt_scalar(link, which, scale, taken, done):
            link(s.activation(rinv[:, which, :], N[:, :], ACT.Ln, bias=epsc[:, 0:1], scale=scale))
            s.activation(rms[:, which, :], N[:, :], ACT.Identity, bias=epsc[:, 0:1], scale=scale).then_inc(taken, 1)
            link(s.activation(rinv[:, which, :], rinv[:, which, :], ACT.Exp, scale=-0.5))
            s.activation(sq[:, which, :], rinv[:, which, :], ACT.Square).then_inc(done, 1)

        def rsqrt_vector(link, which):
            link(v.scalar_tensor_tensor(out=sq[:, which, :], in0=sq[:, which, :], scalar=-0.5, in1=rms[:, which, :],
                                        op0=ALU.mult, op1=ALU.mult))
            link(v.scalar_tensor_tensor(out=rinv[:, which, :], in0=sq[:, which, :], scalar=1.5, in1=rinv[:, which, :],
                                        op0=ALU.add, op1=ALU.mult))

        NORMS = {"a": (vecT, VEC["norm_a_g"], None, hi1, lo1), "kv": (vecT, VEC["kv_norm_g"], None, hi1, lo1),
                 "b": (vecT, VEC["norm_b_g"], None, hi2, lo2), "mix": (gainm, 0, 0, hi2, lo2),
                 "mlp": (gainm, 8, 24, hi2, lo2), "f": (vecT, VEC["final_norm_w_2"], None, None, None)}

        def square(act, key, k, x_ready, before=0):
            act.wait_ge(x_ready, before + k + 1)
            wait(act, sem(f"sums_{key}"), k - 1 + since(f"sums_{key}"))
            s.activation(sq[:, k % 2, :], xT[:, k, :], ACT.Square).then_inc(sem(f"sq_{key}"), 1)

        def norm_scalar(act, link, key):
            act.wait_ge(sem(f"total_{key}"), 1 + since(f"total_{key}"))
            rsqrt_scalar(link, 0, 1.0 / D, sem(f"meansq_{key}"), sem(f"root_{key}"))

        def norm_high(act, key, tiles=range(KT)):
            _, _, shift, H, L = NORMS[key]
            for k in tiles:
                act.wait_ge(sem(f"h32_{key}"), k + 1 + since(f"h32_{key}"))
                bias = 0.0 if shift is None else modT[:, shift + k:shift + k + 1]
                s.activation(H[:, k, :], tmp[:, k % 2, :], ACT.Identity, bias=bias).then_inc(sem(f"hhi_{key}"), 1)

        def add_square(dve, key, k):
            dve.wait_ge(sem(f"sq_{key}"), k + 1 + since(f"sq_{key}"))
            total = rms[:, 1, :]
            if k == 0:
                v.tensor_copy(total, sq[:, 0, :]).then_inc(sem(f"sums_{key}"), 1)
            else:
                dve.wait_ge(sem(f"sums_{key}"), k + since(f"sums_{key}"))
                v.tensor_tensor(total, total, sq[:, k % 2, :], ALU.add).then_inc(sem(f"sums_{key}"), 1)

        def norm_tensor(pe, key):
            pe.wait_ge(sem(f"sums_{key}"), KT + since(f"sums_{key}"))
            mm(N[:, :], ones[:, :], rms[:, 1, :], start=True, stop=True).then_inc(sem(f"total_{key}"), 1)

        def norm_vector(dve, link, key):
            table, gain, shift, H, L = NORMS[key]
            root = key if key != "b" else "kv"
            if key == root:
                dve.wait_ge(sem(f"root_{key}"), 1 + since(f"root_{key}"))
                rsqrt_vector(link, 0)

            def low(k):
                dve.wait_ge(sem(f"hhi_{key}"), k + 1 + since(f"hhi_{key}"))
                if shift is None:
                    v.tensor_tensor(L[:, k, :], tmp[:, k % 2, :], H[:, k, :].bitcast(f32),
                                    ALU.subtract).then_inc(sem(f"lo_{key}"), 1)
                else:
                    v.scalar_tensor_tensor(out=L[:, k, :], in0=tmp[:, k % 2, :], scalar=modT[:, shift + k:shift + k + 1],
                                           in1=H[:, k, :].bitcast(f32), op0=ALU.add, op1=ALU.subtract
                                           ).then_inc(sem(f"lo_{key}"), 1)
            for k in range(KT):
                dst = xT[:, k, :] if H is None else tmp[:, k % 2, :]
                if H is not None:
                    wait(dve, sem(f"lo_{key}"), k - 1 + since(f"lo_{key}"))
                v.scalar_tensor_tensor(out=dst, in0=xT[:, k, :], scalar=table[:, gain + k:gain + k + 1],
                                       in1=rinv[:, 0, :], op0=ALU.mult, op1=ALU.mult).then_inc(sem(f"h32_{key}"), 1)
                if H is not None and k >= 1:
                    low(k - 1)
            if H is not None:
                low(KT - 1)

        def gemm(pe, u, H, L, free, h_ready=None, part=range(KT), first=0, final=KT - 1):
            if part[0] == first:
                pe.wait_ge(w_lo, u.n + 1)
                if free is not None:
                    wait(pe, *free)
            for k in part:
                if h_ready is not None:
                    pe.wait_ge(h_ready[0], h_ready[1] + k + 1)
                whi, wlo = wH[:, u.slot, k, :], wL[:, u.slot, k, :]
                mm(G[u.bank][:, :], whi, H[:, k, :], start=(k == first), stop=False)
                mm(G[u.bank][:, :], whi, L[:, k, :], start=False, stop=False)
                last = mm(G[u.bank][:, :], wlo, H[:, k, :], start=False, stop=(k == final))
            if part[-1] == final:
                last.then_inc(gemm_done, 1)

        FIRST, SECOND = range(KT // 2), range(KT // 2, KT)

        def silu_scalar_1(act, link, ph, n, z, th):
            link(s.activation(th, z, ACT.Abs))
            link(s.activation(th, th, ACT.Exp, scale=-1.0))
            s.activation(th, th, ACT.Ln, bias=1.0).then_inc(sem(f"{ph}_softplus"), 1)

        def silu_vector_1(dve, ph, n, z, th):
            dve.wait_ge(sem(f"{ph}_softplus"), n + 1 + since(f"{ph}_softplus"))
            v.scalar_tensor_tensor(out=th, in0=z, scalar=0.0, in1=th, op0=ALU.min, op1=ALU.subtract
                                   ).then_inc(sem(f"{ph}_logsig"), 1)

        def silu_scalar_2(act, ph, n, th):
            act.wait_ge(sem(f"{ph}_logsig"), n + 1 + since(f"{ph}_logsig"))
            s.activation(th, th, ACT.Exp).then_inc(sem(f"{ph}_sigmoid"), 1)

        def scores(pe, ph, t, h, masked, qn=qn, kn=kn, blocks=range(NQ)):
            lo, hi = h * DH, (h + 1) * DH
            if h == 0 and masked:
                pe.wait_ge(sem(f"{ph}_qk"), 2 * t + 2)
            for q in blocks:
                wait(pe, sem(f"{ph}_logits"), t * 8 + (4 * h + q - 1) + since(f"{ph}_logits"))
                w = (q + 1) * P
                last = mm(S[q % 2][:, 0:w], qn[lo:hi, q * P:(q + 1) * P], kn[lo:hi, 0:w], start=True, stop=not masked)
                if masked:
                    last = mm(S[q % 2][:, q * P:w], identb[:, :], causal, start=False, stop=True)
                last.then_inc(sem(f"{ph}_scores"), 1)

        def take_logits(dve, ph, t, h, bias, blocks=range(NQ)):
            for q in blocks:
                w = (q + 1) * P
                dve.wait_ge(sem(f"{ph}_scores"), t * 8 + (4 * h + q + 1) + since(f"{ph}_scores"))
                if q == 0:
                    wait(dve, sem(f"{ph}_exps"), t * 8 + 4 * h + since(f"{ph}_exps"))
                v.memset(stat[:, h, 0, q:q + 1], 0.0)
                v.tensor_tensor_reduce(out=logits[:, A_AT[q]:A_AT[q] + w], in0=S[q % 2][:, 0:w], in1=bias(h, q),
                                       scale=-1.0, scalar=HUGE, op0=ALU.add, op1=ALU.min,
                                       accum_out=stat[:, h, 1, q:q + 1]).then_inc(sem(f"{ph}_logits"), 1)

        def exps(act, ph, t, h):
            for q in range(NQ):
                act.wait_ge(sem(f"{ph}_logits"), t * 8 + (4 * h + q + 1) + since(f"{ph}_logits"))
                if q == 0:
                    wait(act, sem(f"{ph}_pT"), t * 8 + 4 * h + since(f"{ph}_pT"))
                s.activation(probs[:, A_AT[q]:A_AT[q] + (q + 1) * P], logits[:, A_AT[q]:A_AT[q] + (q + 1) * P],
                             ACT.Exp, bias=stat[:, h, 1, q:q + 1], scale=-1.0,
                             accum_out=stat[:, h, 2, q:q + 1]).then_inc(sem(f"{ph}_exps"), 1)

        def normalise(dve, link, ph, t, h):
            for q in range(NQ):
                w = (q + 1) * P
                dve.wait_ge(sem(f"{ph}_exps"), t * 8 + (4 * h + q + 1) + since(f"{ph}_exps"))
                link(v.reciprocal(stat[:, h, 3, q:q + 1], stat[:, h, 2, q:q + 1]))
                v.tensor_scalar(probs[:, A_AT[q]:A_AT[q] + w], probs[:, A_AT[q]:A_AT[q] + w],
                                stat[:, h, 3, q:q + 1], None, ALU.mult).then_inc(sem(f"{ph}_probs"), 1)

        def turn_probs(pe, ph, t, h, blocks=range(NQ)):
            for kt in blocks:
                wait(pe, sem(f"{ph}_pT_out"), t * 8 + (4 * h + kt - 1) + since(f"{ph}_pT_out"))
                if h == 0 and kt == 0 and ph == "a":
                    pe.wait_ge(sem(f"{ph}_v"), t + 1 + since(f"{ph}_v"))
                for q in range(kt, NQ):
                    pe.wait_ge(sem(f"{ph}_probs"), t * 8 + (4 * h + q + 1) + since(f"{ph}_probs"))
                    last = nc.tensor.transpose(T[kt % 2][:, (q - kt) * P:(q - kt + 1) * P],
                                               probs[:, A_AT[q] + kt * P:A_AT[q] + (kt + 1) * P], ident[:, :])
                last.then_inc(sem(f"{ph}_pT"), 1)

        def take_turned(dve, ph, t, h):
            for kt in range(NQ):
                dve.wait_ge(sem(f"{ph}_pT"), t * 8 + (4 * h + kt + 1) + since(f"{ph}_pT"))
                if kt == 0:
                    wait(dve, sem(f"{ph}_o"), t * 2 + h + since(f"{ph}_o"))
                v.tensor_copy(probsT[:, AT_AT[kt]:AT_AT[kt] + SEQ - kt * P], T[kt % 2][:, 0:SEQ - kt * P]
                              ).then_inc(sem(f"{ph}_pT_out"), 1)

        def mix_values(pe, ph, t, h, v_of, o_taken):
            if h == 0:
                wait(pe, *o_taken)
            for kt in range(NQ):
                pe.wait_ge(sem(f"{ph}_pT_out"), t * 8 + (4 * h + kt + 1) + since(f"{ph}_pT_out"))
                last = mm(O[h * DH:(h + 1) * DH, kt * P:SEQ], v_of(kt, h),
                          probsT[:, AT_AT[kt]:AT_AT[kt] + SEQ - kt * P], start=(kt == 0), stop=(kt == NQ - 1))
            last.then_inc(sem(f"{ph}_o"), 1)

        def raw_scalar(act, ph, n, which, u, dst, used):
            act.wait_ge(gemm_done, u.n + 1)
            if used is not None:
                wait(act, *used)
            s.activation(sq[:, which, :], G[u.bank][:, :], ACT.Square).then_inc(sem(f"{ph}_sq{which}"), 1)
            s.activation(dst[:, :], G[u.bank][:, :], ACT.Copy).then_inc(sem(f"{ph}_raw{which}"), 1)

        def sum_tensor(pe, ph, n, which, n_free):
            pe.wait_ge(sem(f"{ph}_sq{which}"), n + 1)
            if n_free is not None:
                wait(pe, *n_free)
            mm(N[:, :], pair1[:, :], sq[:, which, :], start=True, stop=True).then_inc(sem(f"{ph}_sum{which}"), 1)

        def root_scalar(act, link, ph, n, which):
            act.wait_ge(sem(f"{ph}_sum{which}"), n + 1)
            rsqrt_scalar(link, which, 1.0 / DH, sem(f"{ph}_sum{which}_taken"), sem(f"{ph}_root{which}"))

        def normed_vector(dve, link, ph, n, which, src, dst, gain, used, done):
            dve.wait_ge(sem(f"{ph}_root{which}"), n + 1)
            rsqrt_vector(link, which)
            if used is not None:
                wait(dve, *used)
            v.scalar_tensor_tensor(out=dst, in0=src[:, :], scalar=gains[:, gain:gain + 1], in1=rinv[:, which, :],
                                   op0=ALU.mult, op1=ALU.mult).then_inc(done, 1)

        def gate_vector(dve, ph, t, z, th, o_ready):
            wait(dve, *o_ready)
            dve.wait_ge(sem(f"{ph}_silu"), t + 1 + since(f"{ph}_silu"))
            wait(dve, sem(f"{ph}_gated_lo"), t + since(f"{ph}_gated_lo"))
            v.tensor_tensor(og[:, :], O[:, :], sg[:, :], ALU.mult).then_inc(sem(f"{ph}_gated"), 1)

        def silu_vector_2(dve, ph, n, z, th, used):
            dve.wait_ge(sem(f"{ph}_sigmoid"), n + 1 + since(f"{ph}_sigmoid"))
            wait(dve, *used)
            v.tensor_tensor(sg[:, :], z, th, ALU.mult).then_inc(sem(f"{ph}_silu"), 1)

        def gated_high(act, ph, t, H):
            act.wait_ge(sem(f"{ph}_gated"), t + 1 + since(f"{ph}_gated"))
            s.activation(H[:, bass.ds(t, 1), :], og[:, :].unsqueeze(1), ACT.Copy).then_inc(sem(f"{ph}_gated_hi"), 1)

        def gated_low(dve, ph, t, H, L):
            dve.wait_ge(sem(f"{ph}_gated_hi"), t + 1 + since(f"{ph}_gated_hi"))
            v.tensor_tensor(L[:, bass.ds(t, 1), :], og[:, :].unsqueeze(1), H[:, bass.ds(t, 1), :].bitcast(f32),
                            ALU.subtract).then_inc(sem(f"{ph}_gated_lo"), 1)

        def add_output(dve, ph, unit, gate=None, key=None):
            for n in range(KT):
                u = unit(n)
                dve.wait_ge(gemm_done, u.n + 1)
                if gate is None:
                    v.tensor_tensor(xT[:, n, :], G[u.bank][:, :], xT[:, n, :], ALU.add).then_inc(sem(f"x_{ph}"), 1)
                else:
                    v.scalar_tensor_tensor(out=xT[:, n, :], in0=G[u.bank][:, :], scalar=modT[:, gate + n:gate + n + 1],
                                           in1=xT[:, n, :], op0=ALU.mult, op1=ALU.add).then_inc(sem(f"x_{ph}"), 1)
                if key and n:
                    add_square(dve, key, n - 1)
            if key:
                add_square(dve, key, KT - 1)

        def ada(pe, e, slot):
            pe.wait_ge(sem("ada_folded"), e + 1)
            mm(T[1][:, bass.ds(384 + e, 1)], adaw[:, slot, 0, :], ones[:, 0:1], start=True, stop=True
               ).then_inc(sem("ada_done"), 1)

        def ada_two(pe, e):
            for slot in range(2):
                ada(pe, e + slot, slot)

        def scores_b(pe, t, h):
            lo, hi = h * DH, (h + 1) * DH
            if h == 0:
                pe.wait_ge(sem("b_q"), t + 1)
            wait(pe, sem("b_exps"), t * 8 + 4 * h)
            for q in range(NQ):
                at = [0, P, 0, 2 * P][q]
                w, k0 = B_W[q], max(q - 1, 0) * P
                mm(S[q // 2][:, at:at + w], qn[lo:hi, q * P:(q + 1) * P], kg[lo:hi, k0:k0 + w], start=True, stop=False)
                last = mm(S[q // 2][:, at:at + w], identb[:, :],
                          causal if q == 0 else band[:, :, :].rearrange("p a k -> p (a k)"), start=False, stop=True)
            last.then_inc(sem("b_scores"), 1)

        def maxima_b(dve, link, t, h, head):
            dve.wait_ge(sem("b_scores"), t * 2 + (h + 1))
            wait(dve, sem("b_sink"), t * 2 + (h - 1))
            v.reduce_max(stat[:, h, 0, 0:1], S[0][:, 0:P], AX.X)
            v.reduce_max(stat[:, h, 0, 1:2], S[0][:, P:3 * P], AX.X)
            link(v.reduce_max(stat[:, h, 0, 2:4], S[1][:, :].rearrange("p (q k) -> p q k", q=2), AX.X))
            link(v.tensor_scalar(stat[:, h, 0, :], stat[:, h, 0, :], sinkb[:, bass.ds(head, 1)], None, ALU.max))
            v.tensor_scalar(stat[:, h, 1, :], stat[:, h, 0, :], -1.0, None, ALU.mult).then_inc(sem("b_negmax"), 1)

        def exps_b(act, t, h, head):
            act.wait_ge(sem("b_negmax"), t * 2 + (h + 1))
            wait(act, sem("b_pT"), t * 4 + 2 * h)
            for q in range(NQ):
                at = [0, P, 0, 2 * P][q]
                s.activation(probs[:, B_AT[q]:B_AT[q] + B_W[q]], S[q // 2][:, at:at + B_W[q]], ACT.Exp,
                             bias=stat[:, h, 1, q:q + 1], accum_out=stat[:, h, 2, q:q + 1]).then_inc(sem("b_exps"), 1)
            s.activation(stat[:, h, 4, :], stat[:, h, 1, :], ACT.Exp, bias=sinkb[:, bass.ds(head, 1)]
                         ).then_inc(sem("b_sink"), 1)

        def normalise_b(dve, link, t, h):
            dve.wait_ge(sem("b_sink"), t * 2 + (h + 1))
            link(v.tensor_tensor(stat[:, h, 5, :], stat[:, h, 2, :], stat[:, h, 4, :], ALU.add))
            link(v.reciprocal(stat[:, h, 3, :], stat[:, h, 5, :]))
            for q in range(NQ):
                v.tensor_scalar(probs[:, B_AT[q]:B_AT[q] + B_W[q]], probs[:, B_AT[q]:B_AT[q] + B_W[q]],
                                stat[:, h, 3, q:q + 1], None, ALU.mult).then_inc(sem("b_probs"), 1)

        B_BLOCKS = [(0, 0), (1, 0), (1, 1), (2, 1), (2, 2), (3, 2), (3, 3)]

        def turn_b(pe, t, h):
            for n, (q, kt) in enumerate(B_BLOCKS):
                if n in (0, 4):
                    wait(pe, sem("b_pT_out"), t * 4 + (2 * h - 2 + n // 4 + 1))
                pe.wait_ge(sem("b_probs"), t * 8 + (4 * h + q + 1))
                src = B_AT[q] + (kt - max(q - 1, 0)) * P
                last = nc.tensor.transpose(T[n // 4][:, (n % 4) * P:(n % 4 + 1) * P], probs[:, src:src + P], ident[:, :])
                if n in (3, 6):
                    last.then_inc(sem("b_pT"), 1)

        def take_turned_b(dve, t, h):
            for n, w in ((0, 4), (1, 3)):
                dve.wait_ge(sem("b_pT"), t * 4 + (2 * h + n + 1))
                if n == 0:
                    wait(dve, sem("b_o"), t * 2 + h)
                v.tensor_copy(probsT[:, n * 512:n * 512 + w * P], T[n][:, 0:w * P]).then_inc(sem("b_pT_out"), 1)

        def mix_b(pe, t, h):
            if h == 0:
                wait(pe, sem("b_gated"), t)
            for n, (q, kt) in enumerate(B_BLOCKS):
                if n in (0, 4):
                    pe.wait_ge(sem("b_pT_out"), t * 4 + (2 * h + n // 4 + 1))
                last = mm(O[h * DH:(h + 1) * DH, q * P:(q + 1) * P], vg[:, kt, :], probsT[:, n * P:(n + 1) * P],
                          start=(q != kt or q == 0), stop=(q == kt))
            last.then_inc(sem("b_o"), 1)

        @block.tensor
        def _(pe):
            pe.wait_ge(sem("const"), 3)
            pe.wait_ge(sem("x_here"), 16)
            for k in range(KT):
                wait(pe, sem("x_copied"), k - 1)
                for q in range(NQ):
                    last = nc.tensor.transpose(T[k % 2][:, q * P:(q + 1) * P], xin[:, q, k * P:(k + 1) * P], ident[:, :])
                last.then_inc(sem("x_turned"), 1)
            pe.wait_ge(sem("vec_here"), 16 * (len(VEC_ROWS) + 11))
            nc.tensor.transpose(O[:, 0:N_VEC], vecs[:, :], ident[0:N_VEC, 0:N_VEC])
            nc.tensor.transpose(O[:, 128:129], row[:, :], ident[0:1, 0:1])
            nc.tensor.transpose(O[:, 192:254], taps[:, :], ident[0:62, 0:62]).then_inc(sem("vec_turned"), 1)
            norm_tensor(pe, "a")
            gemm(pe, Unit(0), hi1, lo1, None, mark("lo_a", 0))

            def turn_v(t):
                pe.wait_ge(sem("a_vraw"), t + 1)
                wait(pe, sem("a_pT_out"), t * 8)
                for q in range(NQ):
                    last = nc.tensor.transpose(T[0][:, q * P:(q + 1) * P], vraw[:, q * P:(q + 1) * P], ident[:, :])
                last.then_inc(sem("a_vturn"), 1)

            def v_a(kt, h):
                return vp[:, kt, h * DH:(h + 1) * DH]

            def pair_a(t, attend=True):
                def half(j, part, free):
                    gemm(pe, Unit(UA, j, t, 4), hi1, lo1, free, part=part)

                def attention(step, *args, **blocks):
                    if attend:
                        step(pe, "a", t - 1, *args, **blocks)
                for part, blocks in ((FIRST, (0, 1)), (SECOND, (2, 3))):
                    half(0, part, mark("a_vraw", t))
                    attention(scores, 0, True, blocks=blocks)
                free = mark("a_zraw", t) if attend else mark("f_raw", 1)
                half(1, FIRST, free)
                attention(scores, 1, True, blocks=(0, 1))
                half(1, SECOND, free)
                attention(scores, 1, True, blocks=(2, 3))
                if attend:
                    ada_two(pe, 4 * t - 2)
                attention(turn_probs, 0, blocks=(0, 1))
                half(2, FIRST, mark("a_raw0", t + 1))
                attention(turn_probs, 0, blocks=(2, 3))
                half(2, SECOND, None)
                if attend:
                    mix_values(pe, "a", t - 1, 0, v_a, mark("a_gated", t - 1))
                sum_tensor(pe, "a", t, 0, mark("a_sum1_taken", t))
                half(3, FIRST, mark("a_raw1", t + 1))
                attention(turn_probs, 1, blocks=(0, 1))
                sum_tensor(pe, "a", t, 1, mark("a_sum0_taken", t + 1))
                half(3, SECOND, None)
                attention(turn_probs, 1, blocks=(2, 3))
                if attend:
                    mix_values(pe, "a", t - 1, 1, v_a, mark("a_gated", t - 1))
                ada_two(pe, 4 * t)
                turn_v(t)

            pair_a(0, False)
            repeated(pe, 8, pair_a, first=1)
            scores(pe, "a", 7, 0, True)
            scores(pe, "a", 7, 1, True)
            for h in range(2):
                turn_probs(pe, "a", 7, h)
                mix_values(pe, "a", 7, h, v_a, mark("a_gated", 7))
            for n in range(8):
                gemm(pe, Unit(UOA, n), hi2, lo2, mark("x_a", n - 1) if n > 1 else [mark("a_vraw", 8), mark("a_zraw", 8)][n],
                     mark("a_gated_lo", 0) if n == 0 else None)
                if n == 1:
                    ada_two(pe, 30)

            norm_tensor(pe, "kv")
            for n in range(4):
                gemm(pe, Unit(UKV, n), hi1, lo1, [mark("x_a", 7), mark("x_a", 8), mark("bk_raw0", 1), mark("bk_raw1", 1)][n],
                     mark("lo_kv", 0) if n == 0 else None)
                if n in (1, 2):
                    sum_tensor(pe, "bk", 0, n - 1, mark("bk_sum0_taken", 1) if n == 2 else None)
                if n in (2, 3):
                    pe.wait_ge(sem("bk_normed"), n - 1)
                    pe.wait_ge(sem("bk_sum1_taken" if n == 2 else "bk_turn_taken"), 1)
                    mm(N[:, :], turnm[:, :], tmp[:, n - 2, :], start=True, stop=True).then_inc(sem("bk_turned"), 1)
            for n in range(2):
                pe.wait_ge(sem("bv_raw"), n + 1)
                wait(pe, sem("bv_out"), n)
                src = [vraw, zraw][n]
                for q in range(NQ):
                    last = nc.tensor.transpose(T[0][:, q * P:(q + 1) * P], src[:, q * P:(q + 1) * P], ident[:, :])
                last.then_inc(sem("bv_turn"), 1)

            def pair_b(t, attend, first):
                u0, u1, n = t["u"][0], t["u"][1], t["n"]
                free0 = mark("bv_raw", 1) if first else mark("b_raw0", n)
                free1 = mark("bv_raw", 2) if first else mark("b_zraw", n)
                gemm(pe, u0, hi2, lo2, free0, mark("lo_b", 0) if first else None, part=FIRST)
                if attend:
                    pe.wait_ge(sem("b_kg"), t["gprev"])
                    scores_b(pe, n - 1, 0)
                gemm(pe, u0, hi2, lo2, None, mark("lo_b", 0) if first else None, part=SECOND)
                gemm(pe, u1, hi2, lo2, free1, part=FIRST)
                sum_tensor(pe, "b", n, 0, mark("bk_turn_taken", 2) if first else mark("b_turn_taken", n))
                if attend:
                    scores_b(pe, n - 1, 1)
                    ada_two(pe, 30 + 2 * n)
                    turn_b(pe, n - 1, 0)
                gemm(pe, u1, hi2, lo2, None, part=SECOND)
                if attend:
                    mix_b(pe, n - 1, 0)
                pe.wait_ge(sem("b_normed"), n + 1)
                mm(N[:, :], turnm[:, :], qraw[:, :], start=True, stop=True).then_inc(sem("b_turned"), 1)
                if attend:
                    turn_b(pe, n - 1, 1)
                    mix_b(pe, n - 1, 1)
            def group_b(g):
                static = isinstance(g, int)
                pair_b(dict(n=g * 2, u=(Unit(UB, 0, g, 4), Unit(UB, 1, g, 4)), gprev=g), not (static and g == 0), static and g == 0)
                pair_b(dict(n=g * 2 + 1, u=(Unit(UB, 2, g, 4), Unit(UB, 3, g, 4)), gprev=g + 1), True, False)
            group_b(0)
            repeated(pe, 4, group_b, first=1)
            pe.wait_ge(sem("b_kg"), 4)
            scores_b(pe, 7, 0)
            scores_b(pe, 7, 1)
            turn_b(pe, 7, 0)
            mix_b(pe, 7, 0)
            turn_b(pe, 7, 1)
            mix_b(pe, 7, 1)
            for n in range(8):
                gemm(pe, Unit(UOB, n), hi1, lo1, mark("x_b", n - 1) if n > 1 else [mark("b_raw0", 8), mark("b_zraw", 8)][n],
                     mark("b_gated_lo", 0) if n == 0 else None)
                if n == 2:
                    ada_two(pe, 46)
            norm_tensor(pe, "mix")
            for n in range(3):
                gemm(pe, Unit(UI, n), hi2, lo2, [mark("x_b", 7), mark("x_b", 8), mark("i_raw", 1)][n],
                     mark("lo_mix", 0) if n == 0 else None)
            gemm(pe, Unit(UI, 3), hi2, lo2, mark("i_raw", 2))
            pe.wait_ge(sem("i_raw"), 3)
            for q in range(NQ):
                last = nc.tensor.transpose(T[0][:, q * P:(q + 1) * P], vraw[:, q * P:(q + 1) * P], ident[:, :])
            last.then_inc(sem("iw_turned"), 1)
            pe.wait_ge(sem("ik_here"), 64)
            for q in range(1, NQ):
                for h in range(8):
                    n, lo = 8 * (q - 1) + h, 32 * (h % 4)
                    wait(pe, sem("i_relu"), n - 1)
                    mm(S[n % 2][:, 0:(q + 1) * P], iqT[lo:lo + 32, h // 4, q * P:(q + 1) * P],
                       ik4[lo:lo + 32, 0:(q + 1) * P], start=True, stop=True, tile_position=(lo, 0)).then_inc(sem("i_scores"), 1)
                for n in I_AFTER[q]:
                    gemm(pe, Unit(UI, n), hi2, lo2, mark("i_raw", n - 1))
            def turn_sv(n):
                pe.wait_ge(sem("i_raw"), 12 + n)
                pe.wait_ge(sem("iw_there"), 1)
                pe.wait_ge(sem("mod"), 1)
                for q in range(NQ):
                    last = nc.tensor.transpose(T[n][:, q * P:(q + 1) * P], svT[:, n, q * P:(q + 1) * P], ident[:, :])
                last.then_inc(sem("sv_turned"), 1)

            def v_c(t):
                return lambda kt, h: svp[:, kt, (2 * t + h) * DH:(2 * t + h + 1) * DH]

            def attend_c():
                pe.wait_ge(sem("sv_out"), 2)
                scores(pe, "c", 0, 0, False, sqT[:, 0, :], skT[:, 0, :])
                for n in range(4):
                    t, h = divmod(n + 1, 2)
                    if n < 3:
                        scores(pe, "c", t, h, False, sqT[:, t, :], skT[:, t, :])
                    t, h = divmod(n, 2)
                    turn_probs(pe, "c", t, h)
                    mix_values(pe, "c", t, h, v_c(t), mark("c_gated", t))

            def products(t, first, last_):
                for p in range(first, last_):
                    wait(pe, sem("h_aT"), t * 8 + (p - 1) + since("h_aT"))
                    if p < 7:
                        pe.wait_ge(sem("h_x"), t * 9 + (p + 3) + since("h_x"))
                    for c in range(NQ):
                        cs_ = slice(c * P, (c + 1) * P)
                        x = xx[:, p % 2, cs_]
                        last = mm(S[p % 2][:, cs_], kn[:, cs_] if p == 7 else x, qn[:, cs_] if p == 7 else x,
                                  start=True, stop=True)
                    last.then_inc(sem("h_products"), 1)

            def states(t):
                pe.wait_ge(sem("h_x"), t * 9 + 2 + since("h_x"))
                for c in range(3):
                    last = nc.tensor.transpose(T[1][:, c * P:(c + 1) * P], ke[:, c * P:(c + 1) * P], ident[:, :])
                last.then_inc(sem("h_keT"), 1)

            def updates(t):
                pe.wait_ge(sem("h_keT_out"), t + 1)
                pe.wait_ge(sem("h_v"), t + 1 + since("h_v"))
                for c in range(3):
                    last = mm(T[0][:, c * P:(c + 1) * P], keT[:, c, :], vp[:, c, :], start=True, stop=True)
                last.then_inc(sem("h_update"), 1)

            def outputs(t):
                pe.wait_ge(sem("h_state"), t * 3 + 3 + since("h_state"))
                pe.wait_ge(sem("h_aT"), t * 8 + 8 + since("h_aT"))
                wait(pe, sem("h_normed"), t)
                for c in range(NQ):
                    cs_ = slice(c * P, (c + 1) * P)
                    if c:
                        mm(O[:, cs_], state[:, c - 1, :], qe[:, cs_], start=True, stop=False)
                    last = mm(O[:, cs_], vp[:, c, :], aT[:, c, :], start=(c == 0), stop=True)
                last.then_inc(sem("h_o"), 1)

            def sum_h(t):
                pe.wait_ge(sem("h_sq"), t + 1 + since("h_sq"))
                wait(pe, sem("h_meansq"), t + since("h_meansq"))
                if not (isinstance(t, int) and t == 0):
                    pe.wait_ge(sem("conv_var"), 1)
                mm(N[:, :], ones[:, :], sq[:, 0, :], start=True, stop=True).then_inc(sem("h_sum"), 1)

            def turn_h(t):
                pe.wait_ge(sem("h_raw2"), t + 1 + since("h_raw2"))
                wait(pe, sem("h_state"), t * 3 + since("h_state"))
                for q in range(NQ):
                    last = nc.tensor.transpose(T[0][:, q * P:(q + 1) * P], vraw[:, q * P:(q + 1) * P], ident[:, :])
                last.then_inc(sem("h_vturn"), 1)

            def conv_sum():
                pe.wait_ge(sem("conv_added"), 60)
                pe.wait_ge(sem("h_meansq"), 1 + since("h_meansq"))
                for k in range(2):
                    last = mm(N[:, :], ones[:, :], cacc[:, k, :], start=(k == 0), stop=(k == 1))
                last.then_inc(sem("conv_sum"), 1)

            def conv_sqsum():
                pe.wait_ge(sem("conv_centred"), 2)
                for k in range(2):
                    pe.wait_ge(sem("conv_sq"), k + 1)
                    last = mm(N[:, :], ones[:, :], sq[:, k, :], start=(k == 0), stop=(k == 1))
                last.then_inc(sem("conv_sqsum"), 1)

            def head(t, work=True):
                conv = isinstance(t, int) and t == 2
                def half(j, part, free):
                    gemm(pe, Unit(UH, j, t, 4), hi2, lo2, free, part=part)
                gemm(pe, Unit(UH, 0, t, 4), hi2, lo2, mark("h_raw2", t) if work else mark("i_raw", 12))
                if not work:
                    turn_sv(0)
                    gemm(pe, Unit(UH, 1, t, 4), hi2, lo2, mark("i_raw", 13))
                    turn_sv(1)
                    gemm(pe, Unit(UH, 2, t, 4), hi2, lo2, mark("h_raw0", t + 1))
                    gemm(pe, Unit(UH, 3, t, 4), hi2, lo2, mark("h_raw1", t + 1))
                    return
                if conv:
                    conv_sum()
                    half(1, FIRST, mark("h_raw3", t))
                    half(1, SECOND, None)
                    conv_sqsum()
                states(t - 1)
                if not conv:
                    half(1, FIRST, mark("h_raw3", t))
                updates(t - 1)
                products(t - 1, 0, 2)
                if not conv:
                    half(1, SECOND, None)
                products(t - 1, 2, 4)
                half(2, FIRST, mark("h_raw0", t + 1))
                products(t - 1, 4, 6)
                half(2, SECOND, None)
                products(t - 1, 6, 8)
                gemm(pe, Unit(UH, 3, t, 4), hi2, lo2, mark("h_raw1", t + 1))
                outputs(t - 1)
                turn_h(t)
                sum_h(t - 1)

            head(0, False)
            attend_c()
            turn_h(0)
            head(1)
            repeated(pe, 4, head, first=2)
            states(3)
            updates(3)
            products(3, 0, 8)
            outputs(3)
            sum_h(3)
            for name, count in (("c_gated_lo", 2), ("cv_gated_lo", 2), ("h_gated_lo", 3)):
                wait(pe, sem(name), count + since(name))
            gemm(pe, Unit(UOM), hi1, lo1, mark("h_raw2", 4), part=(4, 5, 6, 7, 0, 1, 2), first=4, final=3)
            pe.wait_ge(sem("h_gated_lo"), 4 + since("h_gated_lo"))
            gemm(pe, Unit(UOM), hi1, lo1, None, part=(3,), first=4, final=3)
            for n in range(1, 8):
                gemm(pe, Unit(UOM, n), hi1, lo1, mark("x_m", n - 1) if n > 1 else mark("h_raw3", 4))
            norm_tensor(pe, "mlp")

            def quarter(c):
                first = isinstance(c, int) and c == 0
                for n in range(8):
                    free = (mark("x_m", 7 + n) if first else mark("x_f", c * 8 + (n - 1))) if n < 2 else mark("f_relu", c * 8 + (n - 1))
                    gemm(pe, Unit(UM, n, c, 16), hi2, lo2, free, mark("lo_mlp", 0) if first and n == 0 else None)
                for n in range(8):
                    free = mark("x_f", c * 8 + (n - 1)) if n > 1 else mark("f_relu", c * 8 + (7 + n))
                    gemm(pe, Unit(UM, 8 + n, c, 16), hi1, lo1, free, mark("f_lo", c * 8) if n == 0 else None)
            repeated(pe, 3, quarter)
            quarter(3)
            norm_tensor(pe, "f")
            for q in range(NQ):
                for half in range(2):
                    wait(pe, sem("y_out"), 2 * q + half - 1)
                    for k in range(4 * half, 4 * half + 4):
                        pe.wait_ge(sem("h32_f"), k + 1 + since("h32_f"))
                        last = nc.tensor.transpose(T[half][:, (k % 4) * P:(k % 4 + 1) * P], xT[:, k, q * P:(q + 1) * P], ident[:, :])
                    last.then_inc(sem("y_turned"), 1)

        @block.scalar
        def _(act):
            link = Link(act, sem("act_link"))
            s.preload_act_table_set("natural_log_exp_and_others")

            def split_hi(u):
                act.wait_ge(w_here[u.slot % 2], u.of_pair * 16 + 16)
                wait(act, gemm_done, u.n - (SLOTS - 1))
                s.activation(wH[:, u.slot], w32[:, u.slot % 2], ACT.Copy).then_inc(w_hi, 1)

            def split_next(u):
                if u.n + AHEAD < NU:
                    split_hi(Unit(u.n + AHEAD))

            for k in range(KT):
                square(act, "a", k, sem("x_copied"))
            split_hi(Unit(0))
            split_hi(Unit(1))
            act.wait_ge(sem("const"), 3)
            norm_scalar(act, link, "a")
            split_hi(Unit(2))
            norm_high(act, "a")
            split_next(Unit(0))
            act.wait_ge(sem("vec_there"), 1)
            cond = vecT[:, VEC["c_2"]:VEC["c_2"] + KT]
            silu_scalar_1(act, link, "c", 0, cond, cth[:, :])
            silu_scalar_2(act, "c", 0, cth[:, :])
            act.wait_ge(gemm_done, 1)
            s.activation(fz[:, 0, :], G[0][0:16, :], ACT.Identity, bias=bfg[:, 0:1]).then_inc(sem("f_raw"), 1)
            act.wait_ge(sem("f_raw"), 1)
            link(s.activation(fz[:, 1, :], fz[:, 0, :], ACT.Abs))
            link(s.activation(fz[:, 2, :], fz[:, 1, :], ACT.Exp, scale=-1.0))
            s.activation(fz[:, 3, :], fz[:, 2, :], ACT.Ln, bias=1.0).then_inc(sem("f_ln"), 1)
            act.wait_ge(sem("c_ready"), 1)
            act.dma_start(c_dram, fz[:, 3, :]).then_inc(sem("c_stored"), 16)

            def load_c(t):
                wait(act, sem("a_logits"), t * 8)
                if isinstance(t, int) and t == 0:
                    act.wait_ge(sem("c_stored"), 16)
                act.dma_start(cbias[:, :, :], c_dram[bass.ds(t * 2, 2), :].partition_broadcast(P)
                              ).then_inc(sem("c_here"), 16)

            def pair_a(t, attend=True):
                split_hi(Unit(UA + AHEAD, 0, t, 4))
                if attend:
                    exps(act, "a", t - 1, 0)
                raw_scalar(act, "a", t, 0, Unit(UA, 0, t, 4), qraw, mark("a_qk", t * 2))
                split_hi(Unit(UA + AHEAD, 1, t, 4))
                raw_scalar(act, "a", t, 1, Unit(UA, 1, t, 4), kraw, mark("a_qk", t * 2))
                split_hi(Unit(UA + AHEAD, 2, t, 4))
                u = Unit(UA, 2, t, 4)
                if attend:
                    exps(act, "a", t - 1, 1)
                load_c(t)
                act.wait_ge(gemm_done, u.n + 1)
                wait(act, sem("a_vturn"), t)
                s.activation(vraw[:, :], G[u.bank][:, :], ACT.Copy).then_inc(sem("a_vraw"), 1)
                root_scalar(act, link, "a", t, 0)
                split_hi(Unit(UA + AHEAD, 3, t, 4))
                root_scalar(act, link, "a", t, 1)
                u = Unit(UA, 3, t, 4)
                act.wait_ge(gemm_done, u.n + 1)
                wait(act, sem("a_silu"), t)
                s.activation(zraw[:, :], G[u.bank][:, :], ACT.Copy).then_inc(sem("a_zraw"), 1)
                act.wait_ge(sem("a_zraw"), t + 1)
                silu_scalar_1(act, link, "a", t, zraw[:, :], th[:, :])
                if attend:
                    gated_high(act, "a", t - 1, hi2)
                silu_scalar_2(act, "a", t, th[:, :])
            pair_a(0, False)
            act.wait_ge(sem("angles"), 1)
            s.activation(sinb[:, :], sinb[:, :], ACT.Sin).then_inc(sem("sines"), 1)
            s.activation(cosb[:, :], cosb[:, :], ACT.Sin).then_inc(sem("sines"), 1)
            s.preload_act_table_set("natural_log_exp_and_others")
            repeated(act, 8, pair_a, link, first=1)
            exps(act, "a", 7, 0)
            exps(act, "a", 7, 1)
            gated_high(act, "a", 7, hi2)
            for n in range(9):
                if n < 8:
                    split_next(Unit(UOA, n))
                if n:
                    square(act, "kv", n - 1, sem("x_a"))
            norm_scalar(act, link, "kv")
            norm_high(act, "kv")
            split_next(Unit(UKV, 0))
            norm_high(act, "b", range(4))
            raw_scalar(act, "bk", 0, 0, Unit(UKV, 0), qraw, None)
            norm_high(act, "b", range(4, 8))
            for n in range(2):
                if n:
                    raw_scalar(act, "bk", 0, n, Unit(UKV, n), kraw, None)
                split_next(Unit(UKV, n + 1))
                root_scalar(act, link, "bk", 0, n)
            for n in range(2):
                u = Unit(UKV, 2 + n)
                act.wait_ge(gemm_done, u.n + 1)
                s.activation([vraw, zraw][n][:, :], G[u.bank][:, :], ACT.Copy).then_inc(sem("bv_raw"), 1)
                if n == 0:
                    split_next(Unit(UKV, 3))
            for n in range(2):
                act.wait_ge(sem("bk_done"), n + 1)
                src = cbias[:, n, :]
                for half in range(2):
                    for dst in range(2):
                        act.dma_start(kd[dst * DH:(dst + 1) * DH, 2 * n + half, :], src[half * DH:(half + 1) * DH, :]
                                      ).then_inc(sem("kd_here"), 16)
            act.wait_ge(sem("bv_turn"), 2)

            def pair_b(n, u0, u1, ahead, attend):
                split_hi(ahead[0])
                if attend:
                    exps_b(act, n - 1, 0, n * 2 - 2)
                raw_scalar(act, "b", n, 0, u0, qraw, mark("b_q", n))
                root_scalar(act, link, "b", n, 0)
                split_hi(ahead[1])
                if attend:
                    exps_b(act, n - 1, 1, n * 2 - 1)
                act.wait_ge(gemm_done, u1.n + 1)
                wait(act, sem("b_silu"), n)
                s.activation(zraw[:, :], G[u1.bank][:, :], ACT.Copy).then_inc(sem("b_zraw"), 1)
                act.wait_ge(sem("b_zraw"), n + 1)
                silu_scalar_1(act, link, "b", n, zraw[:, :], th[:, :])
                if attend:
                    gated_high(act, "b", n - 1, hi1)
                silu_scalar_2(act, "b", n, th[:, :])

            def group_b(g):
                first = isinstance(g, int) and g == 0
                pair_b(g * 2, Unit(UB, 0, g, 4), Unit(UB, 1, g, 4), (Unit(UB + AHEAD, 0, g, 4), Unit(UB + AHEAD, 1, g, 4)), not first)
                pair_b(g * 2 + 1, Unit(UB, 2, g, 4), Unit(UB, 3, g, 4), (Unit(UB + AHEAD, 2, g, 4), Unit(UB + AHEAD, 3, g, 4)), True)
            group_b(0)
            repeated(act, 4, group_b, link, first=1)
            exps_b(act, 7, 0, 14)
            exps_b(act, 7, 1, 15)
            gated_high(act, "b", 7, hi1)
            for n in range(9):
                if n < 8:
                    split_next(Unit(UOB, n))
                if n:
                    square(act, "mix", n - 1, sem("x_b"))
            norm_scalar(act, link, "mix")
            act.wait_ge(sem("mod"), 1)
            norm_high(act, "mix")
            split_next(Unit(UI, 0))

            places = ([(iqT[:, 0, :], 1.0), (iqT[:, 1, :], 1.0), (vraw[:, :], 1.0)] +
                      [(ca[0], 1.0), (ca[1], 1.0), (cb[:, 0, :], 1.0), (cb[:, 1, :], 1.0)] +
                      [(sqT[:, n, :], SA_SCALE) for n in range(2)] + [(skT[:, n, :], 1.0) for n in range(2)] +
                      [(svT[:, n, :], 1.0) for n in range(2)])

            def raw(n):
                u = Unit(UI, n)
                act.wait_ge(gemm_done, u.n + 1)
                if n == 3:
                    act.wait_ge(sem("lo_mix"), KT + since("lo_mix"))
                s.activation(places[n][0], G[u.bank][:, :], ACT.Copy, scale=places[n][1]).then_inc(sem("i_raw"), 1)
                if n < 12:
                    split_next(Unit(UI, n + 1))
            for n in range(3):
                raw(n)
            act.wait_ge(sem("i_raw"), 3)
            for n in range(4):
                act.dma_start(ik4[32 * n:32 * n + 32, :], vraw[0:32, :]).then_inc(sem("ik_here"), 16)
            raw(3)
            def terms(first, last_):
                if first == 0:
                    act.wait_ge(sem("conv_in"), 2)
                    for k in range(2):
                        s.activation(cacc[:, k, :], cpad[:, k, 0:SEQ], ACT.Identity, scale=tapT[:, k:k + 1],
                                     bias=vecT[:, VEC["cv_b_2"] + k:VEC["cv_b_2"] + k + 1]).then_inc(sem("conv_term"), 1)
                for n in range(first, last_):
                    tap, k = 1 + n // 2, n % 2
                    wait(act, sem("conv_added"), n - 1)
                    s.activation(term[n % 2], cpad[:, k, tap:tap + SEQ], ACT.Copy, scale=tapT[:, 2 * tap + k:2 * tap + k + 1]
                                 ).then_inc(sem("conv_term"), 1)

            for q in range(1, NQ):
                if q == 2:
                    for n in range(2):
                        silu_scalar_2(act, "cg", n, cth2[:, n, :])
                for n in range(8 * q - 8, 8 * q):
                    act.wait_ge(sem("i_scores"), n + 1)
                    wait(act, sem("i_acc"), n - 1)
                    s.activation([th, sg][n % 2][:, 0:(q + 1) * P], S[n % 2][:, 0:(q + 1) * P], ACT.Relu,
                                 scale=IDX_SCALE).then_inc(sem("i_relu"), 1)
                    if n == 17:
                        terms(CONV_CUTS[5], CONV_CUTS[6])
                for n in I_AFTER[q]:
                    raw(n)
                    if q == 2:
                        terms(CONV_CUTS[n - 8], CONV_CUTS[n - 7])
                    if n == 6:
                        act.wait_ge(sem("i_raw"), 7)
                        for k in range(2):
                            silu_scalar_1(act, link, "cg", k, cb[:, k, :], cth2[:, k, :])

            def attend_c():
                for n in range(4):
                    exps(act, "c", *divmod(n, 2))
                    terms(CONV_CUTS[n + 10], CONV_CUTS[n + 11])
                    if n >= 2:
                        act.wait_ge(sem("c_gated"), n - 1 + since("c_gated"))
                        s.activation(hi1[:, 2 + n, :], og[:, :], ACT.Copy).then_inc(sem("c_gated_hi"), 1)

            def decay(t, step):
                act.wait_ge(sem("h_diff"), t * 9 + (step + 1) + since("h_diff"))
                wait(act, sem("h_x"), (t * 9 + (step - 1 if step > 1 else 0)) + since("h_x"))
                s.activation(dd[:, step % 2, :], gf if step == 0 else dd[:, step % 2, :], ACT.Exp).then_inc(sem("h_exp"), 1)
                if step == 0:
                    s.activation(dec[:, :], gf.rearrange("p (c k) -> p c k", c=4)[:, :, P - 1], ACT.Exp).then_inc(sem("h_dec"), 1)

            def head(t, work=True):
                raws = [(kraw, "h_k"), (qraw, "h_q"), (vraw, "h_vturn"), (zraw, "h_silu")]
                steps = [(2,), (3, 4, 5), (6, 7, 8), ()]
                for j in range(4):
                    if work:
                        for step in steps[j]:
                            decay(t - 1, step)
                    split_hi(Unit(UH + AHEAD, j, t, 4))
                    raw_h(t, j, *raws[j])
                    if not work:
                        terms(CONV_CUTS[j + 6], CONV_CUTS[j + 7])
                    if j == 1:
                        act.wait_ge(sem("h_raw0"), t + 1 + since("h_raw0"))
                        if work:
                            act.wait_ge(sem("h_silu"), t + since("h_silu"))
                        else:
                            act.wait_ge(sem("i_acc"), 24)
                        link(s.activation(th[:, :], kraw[:, :], ACT.Abs))
                        link(s.activation(th[:, :], th[:, :], ACT.Exp, scale=-1.0))
                        s.activation(th[:, :], th[:, :], ACT.Ln, bias=1.0).then_inc(sem("hf_softplus"), 1)
                if not work:
                    attend_c()
                act.wait_ge(sem("h_klog"), t + 1 + since("h_klog"))
                s.activation(kn[:, :], th[:, :], ACT.Exp, scale=-1.0).then_inc(sem("h_k"), 1)
                act.wait_ge(sem("h_k"), t + 1 + since("h_k"))
                silu_scalar_1(act, link, "hq", t, qraw[:, :], th[:, :])
                decay(t, 0)
                decay(t, 1)
                silu_scalar_2(act, "hq", t, th[:, :])
                if work:
                    norm_head(t - 1)
                act.wait_ge(sem("h_q"), t + 1 + since("h_q"))
                silu_scalar_1(act, link, "h", t, zraw[:, :], th[:, :])
                if work:
                    gated_h(t - 1)
                silu_scalar_2(act, "h", t, th[:, :])

            def raw_h(t, j, dst, used):
                u = Unit(UH, j, t, 4)
                act.wait_ge(gemm_done, u.n + 1)
                wait(act, sem(used), t + since(used))
                s.activation(dst[:, :], G[u.bank][:, :], ACT.Copy).then_inc(sem(f"h_raw{j}"), 1)

            def norm_head(t):
                act.wait_ge(sem("h_o"), t + 1 + since("h_o"))
                wait(act, sem("h_normed"), t)
                s.activation(sq[:, 0, :], O[:, :], ACT.Square).then_inc(sem("h_sq"), 1)
                act.wait_ge(sem("h_sum"), t + 1 + since("h_sum"))
                rsqrt_scalar(link, 0, 1.0 / P, sem("h_meansq"), sem("h_root"))

            def gated_h(t):
                act.wait_ge(sem("h_gated"), t + 1 + since("h_gated"))
                s.activation(hi1[:, bass.ds(t, 1), :], og[:, :].unsqueeze(1), ACT.Copy).then_inc(sem("h_gated_hi"), 1)

            def conv_norm():
                act.wait_ge(sem("h_normed"), 1)
                for k in range(2):
                    act.wait_ge(sem("conv_centred"), k + 1)
                    s.activation(sq[:, k, :], cacc[:, k, :], ACT.Square).then_inc(sem("conv_sq"), 1)
                act.wait_ge(sem("conv_sqsum"), 1)
                rsqrt_scalar(link, 0, 1.0 / 256, sem("conv_var"), sem("conv_root"))
                for k in range(2):
                    act.wait_ge(sem("conv_z"), k + 1)
                    silu_scalar_1(act, link, "cv", k, cacc[:, k, :], cth2[:, k, :])
                for k in range(2):
                    silu_scalar_2(act, "cv", k, cth2[:, k, :])
                for k in range(2):
                    act.wait_ge(sem("cv_gated"), k + 1)
                    s.activation(hi1[:, 6 + k, :], cth2[:, k, :], ACT.Copy).then_inc(sem("cv_gated_hi"), 1)
                act.wait_ge(sem("cv_gated_lo"), 2)
            head(0, False)
            head(1)
            conv_norm()
            repeated(act, 4, head, link, first=2)
            for step in range(2, 9):
                decay(3, step)
            norm_head(3)
            gated_h(3)
            for n in range(9):
                if n < 8:
                    split_next(Unit(UOM, n))
                if n:
                    square(act, "mlp", n - 1, sem("x_m"))
            norm_scalar(act, link, "mlp")
            norm_high(act, "mlp")

            def quarter(c, ahead=True):
                for n in range(16):
                    if n < 8:
                        u = Unit(UM, n, c, 16)
                        act.wait_ge(gemm_done, u.n + 1)
                        wait(act, sem("f_sq"), c * 8 + (n - 1))
                        s.activation(tmp[:, n % 2, :], G[u.bank][:, :], ACT.Relu).then_inc(sem("f_relu"), 1)
                    if ahead or n < 13:
                        split_hi(Unit(UM + AHEAD, n, c, 16))
                    if not ahead and n >= 9:
                        square(act, "f", n - 9, sem("x_f"), 24)
                    if 1 <= n < 9:
                        wait(act, sem("f_sq"), c * 8 + n)
                        s.activation(hi1[:, n - 1, :], rms[:, (n - 1) % 2, :], ACT.Copy).then_inc(sem("f_hi"), 1)
            repeated(act, 3, quarter)
            quarter(3, False)
            square(act, "f", 7, sem("x_f"), 24)
            norm_scalar(act, link, "f")
            for q in range(NQ):
                for half in range(2):
                    act.wait_ge(sem("y_turned"), 2 * q + half + 1)
                    s.activation(xin[:, q, half * 512:half * 512 + 512], T[half][:, :], ACT.Copy
                                 ).then_inc(sem("y_out"), 1)
                act.wait_ge(sem("y_out"), 2 * q + 2)
                act.dma_start(out[0, q * P:(q + 1) * P, :], xin[:, q, :]).then_inc(sem("o_stored"), 16)

        @block.vector
        def _(dve):
            link = Link(dve, sem("dve_link"))
            cond = vecT[:, VEC["c_2"]:VEC["c_2"] + KT]
            for k in range(KT):
                dve.wait_ge(sem("x_turned"), k + 1)
                v.tensor_copy(xT[:, k, :], T[k % 2][:, :]).then_inc(sem("x_copied"), 1)
                if k:
                    add_square(dve, "a", k - 1)
            add_square(dve, "a", KT - 1)
            dve.wait_ge(sem("vec_turned"), 1)
            link(v.tensor_copy(vecT[:, :], O[:, 0:N_VEC]), v.tensor_copy(invf[:, :], O[:, 128:129]),
                 v.tensor_copy(tapT[:, :], O[:, 192:254]))
            v.memset(stat[:, 0, 0, 0:1], 0.0).then_inc(sem("vec_there"), 1)
            link(v.tensor_scalar(gains[:, 0:1], gains[:, 0:1], DH ** -0.5, None, ALU.mult),
                 v.tensor_scalar(gains[:, 2:3], gains[:, 2:3], DH ** -0.5, None, ALU.mult))
            norm_vector(dve, link, "a")
            silu_vector_1(dve, "c", 0, cond, cth[:, :])

            dve.wait_ge(sem("pos_here"), 16)
            if True:
                ang, num, t0 = probs[:, 0:SEQ], probsT[:, 0:SEQ], logits[:, 0:SEQ]
                link(v.tensor_copy(t0, posi[:, :]))
                link(v.tensor_scalar(ang, t0, invf[:, 0:1], None, ALU.mult))
                for dst, quarter in ((sinb, 0.0), (cosb, 0.25)):
                    link(v.tensor_scalar(num.bitcast(i32), ang, 1.0 / TWO_PI, quarter, ALU.mult, ALU.add))
                    link(v.tensor_copy(t0, num.bitcast(i32)))
                    for n, part in enumerate(TURN_PARTS):
                        link(v.scalar_tensor_tensor(out=(dst[:, :]), in0=t0, scalar=-part, in1=ang if n == 0 else dst[:, :],
                                                    op0=ALU.mult, op1=ALU.add))
                    link(v.tensor_scalar(dst[:, :], dst[:, :], quarter * TWO_PI, PI_DOWN, ALU.add, ALU.min))
                    link(v.tensor_scalar(dst[:, :], dst[:, :], -PI_DOWN, None, ALU.max))
            v.memset(stat[:, 0, 0, 0:1], 0.0).then_inc(sem("angles"), 1)
            dve.wait_ge(sem("c_sigmoid"), 1)
            v.tensor_tensor(cact[:, :], cond, cth[:, :], ALU.mult).then_inc(sem("c_silu"), 1)
            dve.wait_ge(sem("f_ln"), 1)
            link(v.tensor_scalar(fz[:, 1, :], fz[:, 0, :], 0.0, None, ALU.min))
            link(v.tensor_tensor(fz[:, 2, :], fz[:, 3, :], fz[:, 1, :], ALU.subtract), v.memset(fz[:, 0, :], 1.0))
            v.tensor_tensor_scan(fz[:, 3, :], fz[:, 0, :], fz[:, 2, :], 0.0, ALU.mult, ALU.add
                                 ).then_inc(sem("c_ready"), 1)

            def c_bias(h, q):
                return cbias[:, h, 0:(q + 1) * P]

            def attend_a(t):
                dve.wait_ge(sem("c_here"), t * 16 + 16)
                take_logits(dve, "a", t, 0, c_bias)
                take_logits(dve, "a", t, 1, c_bias, (0, 1))
                normalise(dve, link, "a", t, 0)
                take_logits(dve, "a", t, 1, c_bias, (2, 3))
                take_turned(dve, "a", t, 0)
                normalise(dve, link, "a", t, 1)
                take_turned(dve, "a", t, 1)

            def pair_a(t, attend=True):
                if attend:
                    attend_a(t - 1)
                normed_vector(dve, link, "a", t, 0, qraw, qn[:, :], 0, mark("a_scores", t * 8), sem("a_qk"))
                normed_vector(dve, link, "a", t, 1, kraw, kn[:, :], 1, mark("a_scores", t * 8), sem("a_qk"))
                if attend:
                    gate_vector(dve, "a", t - 1, None, None, mark("a_o", 2 * t))
                dve.wait_ge(sem("a_vturn"), t + 1)
                v.tensor_copy(vp[:, :, :], T[0][:, :].rearrange("p (q d) -> p q d", q=NQ)).then_inc(sem("a_v"), 1)
                silu_vector_1(dve, "a", t, zraw[:, :], th[:, :])
                if attend:
                    gated_low(dve, "a", t - 1, hi2, lo2)
                silu_vector_2(dve, "a", t, zraw[:, :], th[:, :], mark("a_gated", t))
            pair_a(0, False)
            repeated(dve, 8, pair_a, link, first=1)
            attend_a(7)
            gate_vector(dve, "a", 7, None, None, mark("a_o", 16))
            gated_low(dve, "a", 7, hi2, lo2)
            add_output(dve, "a", lambda n: Unit(UOA, n), key="kv")

            norm_vector(dve, link, "kv")
            dve.wait_ge(sem("lo_kv"), KT + since("lo_kv"))
            norm_vector(dve, link, "b")
            dve.wait_ge(sem("sines"), 2)
            def rotate(n, which, src, dst, ph, rot_ready, done):
                wait(dve, *rot_ready)
                v.tensor_tensor(tmp2[:, 0, :], N[:, :], sinb[:, :], ALU.mult).then_inc(sem(f"{ph}_turn_taken"), 1)
                dve.wait_ge(sem(f"{ph}_turn_taken"), n + 1)
                v.tensor_tensor(dst, tmp2[:, 0, :], tmp2[:, 1, :], ALU.add).then_inc(done, 1)

            for n in range(2):
                normed_vector(dve, link, "bk", 0, n, [qraw, kraw][n], tmp[:, n, :], 3, mark("lo_b", KT), sem("bk_normed"))
                dve.wait_ge(sem("bk_normed"), n + 1)
                link(v.tensor_tensor(tmp2[:, 1, :], tmp[:, n, :], cosb[:, :], ALU.mult))
                rotate(n, 0, tmp[:, n, :], cbias[:, n, :], "bk", mark("bk_turned", n + 1), sem("bk_done"))
            for n in range(2):
                dve.wait_ge(sem("bv_turn"), n + 1)
                v.tensor_copy(vb[:, 2 * n:2 * n + 2, :, :].rearrange("p g q d -> p q g d"),
                              T[0][:, :].rearrange("p (q g d) -> p q g d", q=NQ, g=2)).then_inc(sem("bv_out"), 1)

            def load_group(g, scores_used, o_used):
                wait(dve, sem("b_scores"), scores_used)
                if isinstance(g, int) and g == 0:
                    dve.wait_ge(sem("kd_here"), 16 * 8)
                    dve.wait_ge(sem("bv_out"), 2)
                v.tensor_copy(kg[:, :].unsqueeze(1), kd[:, bass.ds(g, 1), :])
                wait(dve, sem("b_o"), o_used)
                v.tensor_copy(vg.unsqueeze(1), vb[:, bass.ds(g, 1), :, :]).then_inc(sem("b_kg"), 1)

            def pair_b(n, attend, g=None):
                if attend:
                    maxima_b(dve, link, n - 1, 0, n * 2 - 2)
                    normalise_b(dve, link, n - 1, 0)
                    maxima_b(dve, link, n - 1, 1, n * 2 - 1)
                    take_turned_b(dve, n - 1, 0)
                dve.wait_ge(sem("b_root0"), n + 1)
                rsqrt_vector(link, 0)
                v.scalar_tensor_tensor(out=qraw[:, :], in0=qraw[:, :], scalar=gains[:, 2:3], in1=rinv[:, 0, :],
                                       op0=ALU.mult, op1=ALU.mult).then_inc(sem("b_normed"), 1)
                dve.wait_ge(sem("b_normed"), n + 1)
                link(v.tensor_tensor(tmp2[:, 1, :], qraw[:, :], cosb[:, :], ALU.mult))
                if attend:
                    normalise_b(dve, link, n - 1, 1)
                wait(dve, sem("b_scores"), n * 2)
                rotate(n, 0, qraw[:, :], qn[:, :], "b", mark("b_turned", n + 1), sem("b_q"))
                if attend:
                    take_turned_b(dve, n - 1, 1)
                silu_vector_1(dve, "b", n, zraw[:, :], th[:, :])
                if attend:
                    gate_vector(dve, "b", n - 1, None, None, mark("b_o", 2 * n))
                    gated_low(dve, "b", n - 1, hi1, lo1)
                silu_vector_2(dve, "b", n, zraw[:, :], th[:, :], mark("b_gated", n))
                if g is not None:
                    load_group(g, n * 2, n * 2)

            def group_b(g):
                first = isinstance(g, int) and g == 0
                pair_b(g * 2, not first, g)
                pair_b(g * 2 + 1, True)
            group_b(0)
            repeated(dve, 4, group_b, link, first=1)
            maxima_b(dve, link, 7, 0, 14)
            normalise_b(dve, link, 7, 0)
            maxima_b(dve, link, 7, 1, 15)
            take_turned_b(dve, 7, 0)
            normalise_b(dve, link, 7, 1)
            take_turned_b(dve, 7, 1)
            gate_vector(dve, "b", 7, None, None, mark("b_o", 16))
            gated_low(dve, "b", 7, hi1, lo1)
            add_output(dve, "b", lambda n: Unit(UOB, n), key="mix")
            dve.wait_ge(sem("ada_done"), 48)
            link(v.tensor_tensor(modT[:, :], T[1][:, 384:432], vecT[:, 0:48], ALU.add))
            link(v.scalar_tensor_tensor(out=gainm[:, 0:8], in0=modT[:, 8:16], scalar=1.0,
                                        in1=vecT[:, VEC["norm_mix_w_2"]:VEC["norm_mix_w_2"] + 8], op0=ALU.add, op1=ALU.mult))
            link(v.scalar_tensor_tensor(out=gainm[:, 8:16], in0=modT[:, 32:40], scalar=1.0,
                                        in1=vecT[:, VEC["norm_mlp_w_2"]:VEC["norm_mlp_w_2"] + 8], op0=ALU.add, op1=ALU.mult))
            v.memset(stat[:, 0, 0, 0:1], 0.0).then_inc(sem("mod"), 1)
            norm_vector(dve, link, "mix")
            dve.wait_ge(sem("iotas"), 1)
            link(v.tensor_tensor(ii, jj, ii, ALU.bitwise_xor))
            v.tensor_copy(jx, ii).then_inc(sem("xor"), 1)
            dve.wait_ge(sem("later"), 1)
            for n in range(7):
                link(v.tensor_scalar(it, jx, float(64 >> n), None, ALU.is_ge))
                link(v.scalar_tensor_tensor(out=level[:, n, :], in0=jx, scalar=float(128 >> n), in1=it, op0=ALU.is_lt,
                                            op1=ALU.mult))
            dve.wait_ge(sem("iw_turned"), 1)
            v.tensor_scalar(iwp[:, :, :], T[0][:, :].rearrange("p (q c) -> p q c", q=NQ)[:, :, 32:40], 8 ** -0.5, None,
                            ALU.mult).then_inc(sem("iw_there"), 1)
            dve.wait_ge(sem("iw_there"), 1)
            v.tensor_copy(sel[:, 0:P], causal)
            def index_score(q, h):
                n, w = 8 * q - 8 + h, (q + 1) * P
                part = sel[:, A_AT[q]:A_AT[q] + w]
                dve.wait_ge(sem("i_relu"), n + 1)
                relu = [th, sg][n % 2][:, 0:w]
                if h == 0:
                    v.tensor_scalar(part, relu, iwp[:, q, h:h + 1], None, ALU.mult).then_inc(sem("i_acc"), 1)
                else:
                    wait(dve, sem("i_acc"), n)
                    v.scalar_tensor_tensor(out=part, in0=relu, scalar=iwp[:, q, h:h + 1], in1=part, op0=ALU.mult,
                                           op1=ALU.add).then_inc(sem("i_acc"), 1)
            for q in range(1, NQ):
                for h in range(8):
                    index_score(q, h)
                part = sel[:, A_AT[q]:A_AT[q] + (q + 1) * P]
                own = sel[:, A_AT[q] + q * P:A_AT[q] + (q + 1) * P]
                wait(dve, sem("i_acc"), 8 * q)
                link(v.tensor_tensor(own, own, causal, ALU.add))
                for n in range(TOPK // 8):
                    link(v.max(best[:, n % 2, :], part))
                    link(v.match_replace(part, best[:, n % 2, :], part, -HUGE))
                link(v.tensor_scalar(part, part, -HUGE, -NEG, ALU.is_equal, ALU.mult))
                link(v.tensor_scalar(part, part, NEG, None, ALU.add))
            for n in range(2):
                dve.wait_ge(sem("sv_turned"), n + 1)
                v.tensor_copy(svp[:, :, n * P:(n + 1) * P], T[n][:, :].rearrange("p (q d) -> p q d", q=NQ)
                              ).then_inc(sem("sv_out"), 1)

            def sel_bias(h, q):
                return sel[:, A_AT[q]:A_AT[q] + (q + 1) * P]
            take_logits(dve, "c", 0, 0, sel_bias)
            normalise(dve, link, "c", 0, 0)
            for n in range(4):
                t, h = divmod(n + 1, 2)
                if n < 3:
                    take_logits(dve, "c", t, h, sel_bias)
                take_turned(dve, "c", *divmod(n, 2))
                if n < 3:
                    normalise(dve, link, "c", t, h)
                if n % 2:
                    t = n // 2
                    dve.wait_ge(sem("c_o"), 2 * t + 2 + since("c_o"))
                    if t:
                        dve.wait_ge(sem("c_gated_lo"), t + since("c_gated_lo"))
                    v.tensor_copy(og[:, :], O[:, :]).then_inc(sem("c_gated"), 1)
                    dve.wait_ge(sem("c_gated_hi"), t + 1 + since("c_gated_hi"))
                    v.tensor_tensor(lo1[:, 4 + t, :], og[:, :], hi1[:, 4 + t, :].bitcast(f32), ALU.subtract).then_inc(sem("c_gated_lo"), 1)

            def conv_norm():
                dve.wait_ge(sem("conv_sum"), 1)
                for k in range(2):
                    v.scalar_tensor_tensor(out=cacc[:, k, :], in0=N[:, :], scalar=-1.0 / 256, in1=cacc[:, k, :],
                                           op0=ALU.mult, op1=ALU.add).then_inc(sem("conv_centred"), 1)
                dve.wait_ge(sem("conv_root"), 1)
                rsqrt_vector(link, 0)
                w0, b1 = VEC["cv_ln_w_2"], VEC["cv_ln_b_2"]
                for k in range(2):
                    link(v.scalar_tensor_tensor(out=cacc[:, k, :], in0=cacc[:, k, :], scalar=vecT[:, w0 + k:w0 + k + 1],
                                                in1=rinv[:, 0, :], op0=ALU.mult, op1=ALU.mult))
                    v.tensor_scalar(cacc[:, k, :], cacc[:, k, :], vecT[:, b1 + k:b1 + k + 1], None, ALU.add
                                    ).then_inc(sem("conv_z"), 1)
                for k in range(2):
                    dve.wait_ge(sem("conv_z"), k + 1)
                    silu_vector_1(dve, "cv", k, cacc[:, k, :], cth2[:, k, :])
                for k in range(2):
                    dve.wait_ge(sem("cv_sigmoid"), k + 1 + since("cv_sigmoid"))
                    v.tensor_tensor(cth2[:, k, :], cacc[:, k, :], cth2[:, k, :], ALU.mult).then_inc(sem("cv_gated"), 1)
                for k in range(2):
                    dve.wait_ge(sem("cv_gated_hi"), k + 1)
                    v.tensor_tensor(lo1[:, 6 + k, :], cth2[:, k, :], hi1[:, 6 + k, :].bitcast(f32), ALU.subtract
                                    ).then_inc(sem("cv_gated_lo"), 1)

            q4 = lambda x: x.rearrange("p (c k) -> p c k", c=4)

            def work_1(t):
                dve.wait_ge(sem("h_keT"), t + 1)
                v.tensor_copy(keT[:, :, :], T[1][:, 0:384].rearrange("p (c k) -> p c k", c=3)).then_inc(sem("h_keT_out"), 1)
                operands(t, 0)
                operands(t, 1)
                states_of(t)

            def decayed(t):
                dve.wait_ge(sem("h_k"), t + 1 + since("h_k"))
                dve.wait_ge(sem("h_q"), t + 1 + since("h_q"))
                for step in range(2):
                    dve.wait_ge(sem("h_exp"), t * 9 + (step + 1) + since("h_exp"))
                    wait(dve, sem("h_o"), t + since("h_o"))
                    v.tensor_tensor([qe, ke][step], dd[:, step, :], [qn, kn][step][:, :], ALU.mult).then_inc(sem("h_x"), 1)

            def states_of(t):
                dve.wait_ge(sem("h_update"), t + 1 + since("h_update"))
                dve.wait_ge(sem("h_dec"), t + 1 + since("h_dec"))
                v.tensor_copy(state[:, 0, :], T[0][:, 0:P]).then_inc(sem("h_state"), 1)
                for c in range(1, 3):
                    wait(dve, sem("h_state"), t * 3 + c + since("h_state"))
                    v.scalar_tensor_tensor(out=state[:, c, :], in0=state[:, c - 1, :], scalar=dec[:, c:c + 1],
                                           in1=T[0][:, c * P:(c + 1) * P], op0=ALU.mult, op1=ALU.add).then_inc(sem("h_state"), 1)

            def operands(t, lv):
                m = (P // 2) >> lv
                split = lambda x: x.rearrange("p (n a m) -> p n a m", a=2, m=m)
                e, x = split(dd[:, lv % 2, :]), split(xx[:, lv % 2, :])
                dve.wait_ge(sem("h_exp"), t * 9 + (lv + 3) + since("h_exp"))
                wait(dve, sem("h_products"), (t * 8 + (lv - 1 if lv > 1 else 0)) + since("h_products"))
                v.tensor_tensor(x[:, :, 0, :], e[:, :, 0, :], split(kn[:, :])[:, :, 0, :], ALU.mult)
                v.tensor_tensor(x[:, :, 1, :], e[:, :, 1, :], split(qn[:, :])[:, :, 1, :], ALU.mult).then_inc(sem("h_x"), 1)

            def joined(t, p):
                dve.wait_ge(sem("h_products"), t * 8 + (p + 1) + since("h_products"))
                mask = ident[:, :].bitcast(i32) if p == 7 else level[:, p, :]
                wait(dve, sem("h_aT"), t * 8 + p + since("h_aT"))
                v.memset(stat[:, 0, 0, 0:1], 0.0)
                v.copy_predicated(aT[:, :, :], mask.unsqueeze(1).broadcast_to((P, NQ, P)), q4(S[p % 2][:, :])
                                  ).then_inc(sem("h_aT"), 1)

            def work_2(t):
                for lv in range(2, 7):
                    joined(t, lv - 2)
                    operands(t, lv)
                for p in range(5, 8):
                    joined(t, p)

            def work_3(t):
                dve.wait_ge(sem("h_root"), t + 1 + since("h_root"))
                rsqrt_vector(link, 0)
                v.scalar_tensor_tensor(out=og[:, :], in0=O[:, :], scalar=vecT[:, bass.ds(VEC["hg_onorm_w_2"] + t, 1)],
                                       in1=rinv[:, 0, :], op0=ALU.mult, op1=ALU.mult).then_inc(sem("h_normed"), 1)
                dve.wait_ge(sem("h_normed"), t + 1)
                dve.wait_ge(sem("h_silu"), t + 1 + since("h_silu"))
                v.tensor_tensor(og[:, :], og[:, :], sg[:, :], ALU.mult).then_inc(sem("h_gated"), 1)
                dve.wait_ge(sem("h_gated_hi"), t + 1 + since("h_gated_hi"))
                v.tensor_tensor(lo1[:, bass.ds(t, 1), :], og[:, :].unsqueeze(1), hi1[:, bass.ds(t, 1), :].bitcast(f32),
                                ALU.subtract).then_inc(sem("h_gated_lo"), 1)

            def gates(t):
                if isinstance(t, int) and t == 0:
                    dve.wait_ge(sem("conv_term"), 62)
                dve.wait_ge(sem("hf_softplus"), t + 1)
                link(v.scalar_tensor_tensor(out=gf, in0=kraw[:, :], scalar=0.0, in1=th[:, :], op0=ALU.min,
                                            op1=ALU.subtract))
                v.scalar_tensor_tensor(out=th[:, :], in0=kraw[:, :], scalar=0.0, in1=th[:, :], op0=ALU.max,
                                       op1=ALU.add).then_inc(sem("h_klog"), 1)
                link(v.tensor_scalar(gf, gf, LN_TINY, None, ALU.max))
                v.tensor_tensor_scan(gc, restart, gf, 0.0, ALU.mult, ALU.add).then_inc(sem("h_g"), 1)

            def queries(t):
                silu_vector_1(dve, "hq", t, qraw[:, :], th[:, :])
                dve.wait_ge(sem("hq_sigmoid"), t + 1 + since("hq_sigmoid"))
                v.scalar_tensor_tensor(out=qn[:, :], in0=qraw[:, :], scalar=P ** -0.5, in1=th[:, :], op0=ALU.mult,
                                       op1=ALU.mult).then_inc(sem("h_q"), 1)

            def head(t, work=True):
                if work:
                    work_1(t - 1)
                    work_2(t - 1)
                gates(t)
                queries(t)
                decayed(t)
                dve.wait_ge(sem("h_vturn"), t + 1 + since("h_vturn"))
                v.tensor_copy(vp[:, :, :], q4(T[0][:, :])).then_inc(sem("h_v"), 1)
                if work:
                    work_3(t - 1)
                silu_vector_1(dve, "h", t, zraw[:, :], th[:, :])
                silu_vector_2(dve, "h", t, zraw[:, :], th[:, :], mark("h_gated", t))
            head(0, False)
            link(v.memset(scr[:, 512:1024], 0.0))
            head(1)
            conv_norm()
            repeated(dve, 4, head, link, first=2)
            work_1(3)
            work_2(3)
            work_3(3)
            add_output(dve, "m", lambda n: Unit(UOM, n), 16, "mlp")
            norm_vector(dve, link, "mlp")

            def quarter(c, key=None):
                for n in range(9):
                    if n < 8:
                        dve.wait_ge(sem("f_relu"), c * 8 + (n + 1))
                        wait(dve, sem("f_lo"), c * 8 + (n - 1))
                        v.tensor_tensor(rms[:, n % 2, :], tmp[:, n % 2, :], tmp[:, n % 2, :], ALU.mult
                                        ).then_inc(sem("f_sq"), 1)
                    if n:
                        wait(dve, sem("f_hi"), c * 8 + n)
                        v.tensor_tensor(lo1[:, n - 1, :], rms[:, (n - 1) % 2, :], hi1[:, n - 1, :].bitcast(f32),
                                        ALU.subtract).then_inc(sem("f_lo"), 1)
                add_output(dve, "f", lambda n: Unit(UM, 8 + n, c, 16), 40, key)
            repeated(dve, 3, quarter)
            quarter(3, "f")
            norm_vector(dve, link, "f")


def kernel(**inputs):
    import numpy as np
    import concourse.bacc as bacc
    from concourse.bass_utils import run_bass_kernel_spmd as run

    nc = bacc.Bacc("TRN2", target_bir_lowering=False, num_devices=1)
    arrays, aps = {}, {}
    for name, value in inputs.items():
        value = np.ascontiguousarray(value)
        arrays[name + "_dram"] = value
        aps[name] = nc.dram_tensor(name + "_dram", value.shape, mybir.dt.from_np(value.dtype), kind="ExternalInput").ap()
    out = nc.dram_tensor("out_dram", (1, SEQ, D), mybir.dt.float32, kind="ExternalOutput").ap()
    build(nc, aps, out)
    r = run(nc, [arrays], core_ids=[0])
    return r.results[0]["out_dram"]
```
